# Optimizing a Trainium2 kernel written in Bass

```python
import math
import jax, jax.numpy as jnp
from jax import lax
import numpy as np

D_MODEL = 1024
BATCH = 1
SEQ = 256
DEPTH = 2

HEAD_DIM = 64
GLA_WIDTH = D_MODEL // 4
GLA_HEADS = GLA_WIDTH // HEAD_DIM
GLA_GATE_RANK = 16
GLA_GATE_TAU = 16.0
GLA_CHUNK = 16
SSD_WIDTH = D_MODEL // 2
SSD_HEADS = SSD_WIDTH // HEAD_DIM
SSD_GROUPS = 2
SSD_HEADS_PER_GROUP = SSD_HEADS // SSD_GROUPS
SSD_STATE = 64
SSD_CONV = 4
SSD_CHUNK = 64
SSD_XBC = SSD_WIDTH + 2 * SSD_GROUPS * SSD_STATE
RWKV_WIDTH = D_MODEL // 4
RWKV_HEADS = RWKV_WIDTH // HEAD_DIM
RWKV_DECAY_RANK = 64
RWKV_A_RANK = 64
RWKV_GATE_RANK = 128
RWKV_GN_EPS = 64e-5
MIX_WIDTH = GLA_WIDTH + SSD_WIDTH + RWKV_WIDTH
GLA_SPLITS = (GLA_WIDTH, GLA_WIDTH, GLA_WIDTH, GLA_WIDTH, GLA_GATE_RANK)
SSD_SPLITS = (SSD_WIDTH, SSD_XBC, SSD_HEADS)
RWKV_SPLITS = (RWKV_WIDTH, RWKV_WIDTH, RWKV_WIDTH, RWKV_DECAY_RANK, RWKV_A_RANK, RWKV_GATE_RANK)
GLA_COLS = sum(GLA_SPLITS)
SSD_COLS = sum(SSD_SPLITS)
RWKV_COLS = sum(RWKV_SPLITS)
N_IN = GLA_COLS + SSD_COLS + RWKV_COLS
N_EXPERTS = 16
N_EXPERT_GROUPS = 4
EXPERTS_PER_GROUP = N_EXPERTS // N_EXPERT_GROUPS
TOP_K = 2
EXPERT_FF = D_MODEL // 2
DEEPNORM_ALPHA = (2 * DEPTH) ** 0.25
DEEPNORM_BETA = (8 * DEPTH) ** -0.25
LN_EPS = 1e-5

kernel_name = "hymba_style_gla_ssd_rwkv7_grouped_moe_deepnorm"

def _offsets(sizes):
    out, acc = [], 0
    for s in sizes[:-1]:
        acc += s
        out.append(acc)
    return out

def layer_norm(x, g, b, eps=LN_EPS):
    xf = x.astype(jnp.float32)
    mu = jnp.mean(xf, axis=-1, keepdims=True)
    var = jnp.mean(jnp.square(xf - mu), axis=-1, keepdims=True)
    return ((xf - mu) * lax.rsqrt(var + eps) * g + b).astype(x.dtype)

def rms_norm(x, g, eps=LN_EPS):
    xf = x.astype(jnp.float32)
    return xf * lax.rsqrt(jnp.mean(jnp.square(xf), axis=-1, keepdims=True) + eps) * g

def token_shift(x):
    return jnp.pad(x, ((0, 0), (1, 0), (0, 0)))[:, :-1]

def causal_depthwise_conv(x, w, b):
    k_w, ch = w.shape
    y = lax.conv_general_dilated(x, w.astype(x.dtype)[:, None, :], window_strides=(1,),
                                 padding=[(k_w - 1, 0)], dimension_numbers=('NWC', 'WIO', 'NWC'),
                                 feature_group_count=ch)
    return y + b

def scan_chunk_states(d_state, decay):
    def step(s, inp):
        d, dec = inp
        return dec * s + d, s
    s0 = jnp.zeros_like(d_state[:, 0])
    _, s_in = lax.scan(step, s0, (jnp.moveaxis(d_state, 1, 0), jnp.moveaxis(decay, 1, 0)))
    return jnp.moveaxis(s_in, 0, 1)

def gla_mixer(q, k, v, g, a_lr, w_alpha, b_alpha, norm_g):
    f32 = jnp.float32
    bsz, seq, _ = q.shape
    n_chunks = seq // GLA_CHUNK
    shape = (bsz, n_chunks, GLA_CHUNK, GLA_HEADS, HEAD_DIM)
    log_a = jax.nn.log_sigmoid((a_lr @ w_alpha + b_alpha).astype(f32)) / GLA_GATE_TAU
    qc = q.astype(f32).reshape(shape) * HEAD_DIM ** -0.5
    kc = k.astype(f32).reshape(shape)
    vc = v.astype(f32).reshape(shape)
    cum = jnp.cumsum(log_a.reshape(shape), axis=2)
    causal = jnp.tril(jnp.ones((GLA_CHUNK, GLA_CHUNK), dtype=bool))[:, :, None, None]
    decay = jnp.exp(jnp.where(causal, cum[:, :, :, None] - cum[:, :, None, :], -jnp.inf))
    scores = jnp.einsum('bcthk,bcshk,bctshk->bchts', qc, kc, decay)
    o = jnp.einsum('bchts,bcshv->bcthv', scores, vc)
    cum_last = cum[:, :, -1]
    d_state = jnp.einsum('bcshk,bcshv->bchkv', kc * jnp.exp(cum_last[:, :, None] - cum), vc)
    s_in = scan_chunk_states(d_state, jnp.exp(cum_last)[..., None])
    o = o + jnp.einsum('bcthk,bchkv->bcthv', qc * jnp.exp(cum), s_in)
    o = rms_norm(o.reshape(bsz, seq, GLA_HEADS, HEAD_DIM), norm_g) * \
        jax.nn.silu(g.astype(f32).reshape(bsz, seq, GLA_HEADS, HEAD_DIM))
    return o.reshape(bsz, seq, GLA_WIDTH)

def ssd_mixer(z, xbc, dt_raw, conv_w, conv_b, dt_bias, a_log, d_skip, norm_g):
    f32 = jnp.float32
    bsz, seq, _ = z.shape
    n_chunks = seq // SSD_CHUNK
    G, E, P, M = SSD_GROUPS, SSD_HEADS_PER_GROUP, HEAD_DIM, SSD_STATE
    xbc = jax.nn.silu(causal_depthwise_conv(xbc, conv_w, conv_b).astype(f32))
    xs, bm, cm = jnp.split(xbc, [SSD_WIDTH, SSD_WIDTH + G * M], axis=-1)
    xs = xs.reshape(bsz, n_chunks, SSD_CHUNK, G, E, P)
    bm = bm.reshape(bsz, n_chunks, SSD_CHUNK, G, M)
    cm = cm.reshape(bsz, n_chunks, SSD_CHUNK, G, M)
    dt = jax.nn.softplus(dt_raw.astype(f32) + dt_bias).reshape(bsz, n_chunks, SSD_CHUNK, G, E)
    da = dt * (-jnp.exp(a_log.astype(f32))).reshape(G, E)
    cs = jnp.cumsum(da, axis=2)
    xdt = xs * dt[..., None]
    causal = jnp.tril(jnp.ones((SSD_CHUNK, SSD_CHUNK), dtype=bool))[:, :, None, None]
    seg = jnp.exp(jnp.where(causal, cs[:, :, :, None] - cs[:, :, None, :], -jnp.inf))
    cb = jnp.einsum('bctgm,bcsgm->bctsg', cm, bm)
    y = jnp.einsum('bctsg,bctsge,bcsgep->bctgep', cb, seg, xdt)
    cs_last = cs[:, :, -1]
    d_state = jnp.einsum('bcsgm,bcsge,bcsgep->bcgepm', bm, jnp.exp(cs_last[:, :, None] - cs), xdt)
    s_in = scan_chunk_states(d_state, jnp.exp(cs_last)[..., None, None])
    y = y + jnp.einsum('bctgm,bctge,bcgepm->bctgep', cm, jnp.exp(cs), s_in)
    y = y + d_skip.astype(f32).reshape(G, E, 1) * xs
    y = y.reshape(bsz, seq, SSD_WIDTH) * jax.nn.silu(z.astype(f32))
    y = rms_norm(y.reshape(bsz, seq, G, SSD_WIDTH // G), norm_g.reshape(G, SSD_WIDTH // G))
    return y.reshape(bsz, seq, SSD_WIDTH)

def rwkv7_mixer(cols, mu, w0, w2, a0, a2, g2, k_k, k_a, r_k, ln_g, ln_b):
    f32 = jnp.float32
    bsz, seq, _ = cols.shape
    H, N = RWKV_HEADS, HEAD_DIM
    cols = cols.astype(f32)
    cols = cols + (token_shift(cols) - cols) * mu
    r, k, v, w_lr, a_lr, g_lr = jnp.split(cols, _offsets(RWKV_SPLITS), axis=-1)
    w = -jax.nn.softplus(-(w0 + jnp.tanh(w_lr) @ w2)) - 0.5
    decay = jnp.exp(-jnp.exp(w.astype(f32)))
    a = jax.nn.sigmoid(a0 + a_lr @ a2)
    g = jax.nn.sigmoid(g_lr) @ g2
    heads = lambda t: t.astype(f32).reshape(bsz, seq, H, N)
    kk = heads(k * k_k)
    kk = kk / jnp.maximum(jnp.linalg.norm(kk, axis=-1, keepdims=True), 1e-12)
    k = heads(k * (1.0 + (a - 1.0) * k_a))
    r, v, decay, a = heads(r), heads(v), heads(decay), heads(a)

    def step(s, inp):
        r_t, w_t, k_t, v_t, kk_t, a_t = inp
        sa = jnp.einsum('bhvk,bhk->bhv', s, -kk_t)
        s = s * w_t[:, :, None, :] + sa[..., None] * (kk_t * a_t)[:, :, None, :] + v_t[..., None] * k_t[:, :, None, :]
        return s, jnp.einsum('bhvk,bhk->bhv', s, r_t)

    tm = lambda t: jnp.moveaxis(t, 1, 0)
    s0 = jnp.zeros((bsz, H, N, N), f32)
    _, y = lax.scan(step, s0, (tm(r), tm(decay), tm(k), tm(v), tm(kk), tm(a)))
    y = jnp.moveaxis(y, 0, 1)
    y = layer_norm(y, ln_g.reshape(H, N), ln_b.reshape(H, N), eps=RWKV_GN_EPS)
    y = y + jnp.sum(r * k * r_k, axis=-1, keepdims=True) * v
    return y.reshape(bsz, seq, RWKV_WIDTH) * g

def grouped_moe(x, router_w, router_b, w_gate, w_up, w_down):
    f32 = jnp.float32
    bsz, seq, dm = x.shape
    h = x.reshape(-1, dm)
    scores = jax.nn.sigmoid((h @ router_w).astype(f32))
    sel = (scores + router_b).reshape(-1, N_EXPERT_GROUPS, EXPERTS_PER_GROUP)
    group_score = jnp.sum(lax.top_k(sel, 2)[0], axis=-1)
    best_group = jnp.argmax(group_score, axis=-1)
    in_group = jax.nn.one_hot(best_group, N_EXPERT_GROUPS, dtype=f32)[..., None] > 0
    masked = jnp.where(in_group, sel, -jnp.inf).reshape(-1, N_EXPERTS)
    _, top_idx = lax.top_k(masked, TOP_K)
    top_w = jnp.take_along_axis(scores, top_idx, axis=-1)
    top_w = top_w / jnp.sum(top_w, axis=-1, keepdims=True)
    gate = jnp.sum(jax.nn.one_hot(top_idx, N_EXPERTS, dtype=f32) * top_w[..., None], axis=1)
    gate = gate.astype(h.dtype)
    out = jnp.zeros_like(h)
    for e in range(N_EXPERTS):
        he = jax.nn.silu(h @ w_gate[e]) * (h @ w_up[e])
        out = out + gate[:, e:e + 1] * (he @ w_down[e])
    return out.reshape(bsz, seq, dm)

def setup_inputs(seed: int = 0) -> dict:
    key = jax.random.key(seed)
    ks = iter(jax.random.split(key, 48))
    f32 = jnp.float32
    L = DEPTH
    nrm = lambda shape, scale: jax.random.normal(next(ks), shape, f32) * scale
    uni = lambda shape, lo, hi: jax.random.uniform(next(ks), shape, f32, lo, hi)
    ones_n = lambda shape: 1.0 + nrm(shape, 0.02)
    dt0 = jnp.exp(uni((L, SSD_HEADS), math.log(1e-3), math.log(1e-1)))
    ramp = (jnp.arange(RWKV_WIDTH, dtype=f32) / (RWKV_WIDTH - 1)) ** 0.85
    return {
        "x": nrm((BATCH, SEQ, D_MODEL), 1.0),
        "w_in": nrm((L, D_MODEL, N_IN), D_MODEL ** -0.5),
        "gla_w_alpha": nrm((L, GLA_GATE_RANK, GLA_WIDTH), GLA_GATE_RANK ** -0.5),
        "gla_b_alpha": nrm((L, GLA_WIDTH), 0.1),
        "gla_norm_g": ones_n((L, HEAD_DIM)),
        "ssd_conv_w": nrm((L, SSD_CONV, SSD_XBC), SSD_CONV ** -0.5),
        "ssd_conv_b": nrm((L, SSD_XBC), 0.02),
        "ssd_dt_bias": dt0 + jnp.log(-jnp.expm1(-dt0)),
        "ssd_A_log": jnp.log(uni((L, SSD_HEADS), 1.0, 16.0)),
        "ssd_D": ones_n((L, SSD_HEADS)),
        "ssd_norm_g": ones_n((L, SSD_WIDTH)),
        "rwkv_mu": uni((L, RWKV_COLS), 0.0, 1.0),
        "rwkv_w0": -6.0 + 5.0 * ramp + nrm((L, RWKV_WIDTH), 0.1),
        "rwkv_w2": nrm((L, RWKV_DECAY_RANK, RWKV_WIDTH), 0.1),
        "rwkv_a0": nrm((L, RWKV_WIDTH), 0.1),
        "rwkv_a2": nrm((L, RWKV_A_RANK, RWKV_WIDTH), 0.1),
        "rwkv_g2": nrm((L, RWKV_GATE_RANK, RWKV_WIDTH), RWKV_GATE_RANK ** -0.5),
        "rwkv_k_k": 0.85 + nrm((L, RWKV_WIDTH), 0.02),
        "rwkv_k_a": ones_n((L, RWKV_WIDTH)),
        "rwkv_r_k": nrm((L, RWKV_HEADS, HEAD_DIM), 0.1),
        "rwkv_ln_g": ones_n((L, RWKV_WIDTH)),
        "rwkv_ln_b": nrm((L, RWKV_WIDTH), 0.02),
        "w_out": nrm((L, MIX_WIDTH, D_MODEL), MIX_WIDTH ** -0.5 * DEEPNORM_BETA),
        "ln1_g": ones_n((L, D_MODEL)),
        "ln1_b": nrm((L, D_MODEL), 0.02),
        "router_w": nrm((D_MODEL, N_EXPERTS), D_MODEL ** -0.5),
        "router_b": nrm((N_EXPERTS,), 0.01),
        "exp_w_gate": nrm((L, N_EXPERTS, D_MODEL, EXPERT_FF), D_MODEL ** -0.5),
        "exp_w_up": nrm((L, N_EXPERTS, D_MODEL, EXPERT_FF), D_MODEL ** -0.5),
        "exp_w_down": nrm((L, N_EXPERTS, EXPERT_FF, D_MODEL), EXPERT_FF ** -0.5 * DEEPNORM_BETA),
        "ln2_g": ones_n((L, D_MODEL)),
        "ln2_b": nrm((L, D_MODEL), 0.02),
    }

def reference(x, w_in, gla_w_alpha, gla_b_alpha, gla_norm_g, ssd_conv_w, ssd_conv_b, ssd_dt_bias,
              ssd_A_log, ssd_D, ssd_norm_g, rwkv_mu, rwkv_w0, rwkv_w2, rwkv_a0, rwkv_a2, rwkv_g2,
              rwkv_k_k, rwkv_k_a, rwkv_r_k, rwkv_ln_g, rwkv_ln_b, w_out, ln1_g, ln1_b, router_w,
              router_b, exp_w_gate, exp_w_up, exp_w_down, ln2_g, ln2_b):
    for l in range(DEPTH):
        proj = x @ w_in[l]
        gla_cols, ssd_cols, rwkv_cols = jnp.split(proj, [GLA_COLS, GLA_COLS + SSD_COLS], axis=-1)
        gq, gk, gv, gg, ga = jnp.split(gla_cols, _offsets(GLA_SPLITS), axis=-1)
        sz, sxbc, sdt = jnp.split(ssd_cols, _offsets(SSD_SPLITS), axis=-1)
        o_gla = gla_mixer(gq, gk, gv, gg, ga, gla_w_alpha[l], gla_b_alpha[l], gla_norm_g[l])
        o_ssd = ssd_mixer(sz, sxbc, sdt, ssd_conv_w[l], ssd_conv_b[l], ssd_dt_bias[l], ssd_A_log[l],
                          ssd_D[l], ssd_norm_g[l])
        o_rwkv = rwkv7_mixer(rwkv_cols, rwkv_mu[l], rwkv_w0[l], rwkv_w2[l], rwkv_a0[l], rwkv_a2[l],
                             rwkv_g2[l], rwkv_k_k[l], rwkv_k_a[l], rwkv_r_k[l], rwkv_ln_g[l], rwkv_ln_b[l])
        heads_out = jnp.concatenate([o_gla.astype(x.dtype), o_ssd.astype(x.dtype), o_rwkv.astype(x.dtype)], axis=-1)
        x = layer_norm(DEEPNORM_ALPHA * x + heads_out @ w_out[l], ln1_g[l], ln1_b[l])
        ffn = grouped_moe(x, router_w, router_b, exp_w_gate[l], exp_w_up[l], exp_w_down[l])
        x = layer_norm(DEEPNORM_ALPHA * x + ffn, ln2_g[l], ln2_b[l])
    return x


_drawn_inputs = setup_inputs


def setup_inputs(seed=0):
    import zlib

    import numpy as np

    out = dict(_drawn_inputs(seed))
    spreads = {}
    factors = {'ssd_norm_g': 2.948,
     'rwkv_a0': 8.0,
     'rwkv_k_k': 2.935,
     'rwkv_ln_g': 3.982,
     'rwkv_ln_b': 2.967}
    for name, (base, spread) in spreads.items():
        noise = np.random.default_rng([zlib.crc32(name.encode()), seed]).standard_normal(out[name].shape)
        drawn = base * np.exp(spread * noise) if base else spread * noise
        out[name] = __import__('jax').numpy.asarray(drawn.astype(out[name].dtype))
    for name, factor in factors.items():
        out[name] = (out[name] * factor).astype(out[name].dtype)
    return out
```

```python
from contextlib import ExitStack

import concourse.bass as bass
import numpy as np
from concourse import mybir

ALU = mybir.AluOpType
ACT = mybir.ActivationFunctionType
AX = mybir.AxisListType
F32 = mybir.dt.float32

P = 128
HALF = 64


def hybrid_trunk(nc: bass.Bass, t: dict, out: bass.AP):
    L, D, N_IN = t["w_in"].shape
    S = t["x"].shape[1]
    TT = S // P
    KD = D // P
    NE = t["exp_w_gate"].shape[1]
    FF = t["exp_w_gate"].shape[3]
    FB = FF // P
    GW = t["gla_w_alpha"].shape[2]
    RANK = t["gla_w_alpha"].shape[1]
    SW = t["ssd_norm_g"].shape[1]
    SH = t["ssd_D"].shape[1]
    RW = t["rwkv_w0"].shape[1]
    HD = t["gla_norm_g"].shape[1]
    NH = GW // HD
    XBC = t["ssd_conv_w"].shape[2]
    TAPS = t["ssd_conv_w"].shape[1]
    XB = XBC // P
    NG = 4
    EPG = NE // NG
    CH = 64
    NC = S // CH
    ALPHA = float((2 * L) ** 0.25)
    EPS = 1e-5
    GN_EPS = 64e-5
    BCOL = 512
    o_gla, o_z = 0, 4 * GW + RANK
    o_xbc = o_z + SW
    o_dt = o_xbc + XBC
    o_rw = o_dt + SH
    assert o_rw + 4 * RW == N_IN and D == 1024 and S == 256 and HD == CH == HALF

    NSLOT = 4

    def w_in_cols(l, c, n):
        return t["w_in"][l, :, c:c + n].rearrange("(p k) n -> p k n", k=KD)

    def blocks(l):
        b = [("rw0", [(w_in_cols(l, o_rw, BCOL), 0)]),
             ("rw1", [(w_in_cols(l, o_rw + BCOL, BCOL), 0)]),
             ("xbc0", [(w_in_cols(l, o_xbc, BCOL), 0)]),
             ("xbc1", [(w_in_cols(l, o_xbc + BCOL, XBC - BCOL + SH), 0),
                       (w_in_cols(l, 4 * GW, RANK), XBC - BCOL + SH)]),
             ("qk", [(w_in_cols(l, 0, BCOL), 0)]),
             ("vg", [(w_in_cols(l, BCOL, BCOL), 0)]),
             ("z", [(w_in_cols(l, o_z, BCOL), 0)])]
        for h in range(2):
            b.append((f"out{h}", [(t["w_out"][l, :, h * BCOL:(h + 1) * BCOL].rearrange("(b p) n -> p b n", p=P), 0)]))
        for e in range(NE):
            b.append((f"gate{e}", [(t["exp_w_gate"][l, e].rearrange("(p k) f -> p k f", k=KD), 0)]))
            b.append((f"up{e}", [(t["exp_w_up"][l, e].rearrange("(p k) f -> p k f", k=KD), 0)]))
            b.append((f"down{e}", [(t["exp_w_down"][l, e].rearrange("(p b) n -> p b n", b=FB), 0)]))
        return b

    order = [(l, name, parts) for l in range(L) for name, parts in blocks(l)]
    index = {(l, name): n for n, (l, name, _) in enumerate(order)}
    landed, seen = [], [0] * NSLOT
    for n, (_, _, parts) in enumerate(order):
        seen[n % NSLOT] += 16 * len(parts)
        landed.append(seen[n % NSLOT])

    rows, n_rows = {}, 0
    for name, per in (("ssd_conv_w", TAPS * XB), ("ssd_conv_b", XB), ("rwkv_mu", 8), ("rwkv_w0", 2), ("rwkv_a0", 2),
                      ("rwkv_k_k", 2), ("rwkv_k_a", 2), ("rwkv_r_k", 2), ("gla_b_alpha", 2), ("ssd_norm_g", 4),
                      ("gla_norm_g", 1)):
        rows[name] = (n_rows, per)
        n_rows += L * per

    with ExitStack() as ctx:
        def sb(name, shape, dt=F32):
            return ctx.enter_context(nc.sbuf_tensor(name, shape, dt))

        class Signal:

            def __init__(self, name, per=1):
                self.sem, self.per, self.given = ctx.enter_context(nc.semaphore(name)), per, 0

            def __call__(self, l, n=None):
                return self.sem, l * self.per + (self.per if n is None else n)

        class Chain:

            def __init__(self, name):
                self.sem, self.n = ctx.enter_context(nc.semaphore(name)), 0

            def add(self, ins):
                ins.then_inc(self.sem, 1)
                self.n += 1

            def join(self, eng):
                eng.wait_ge(self.sem, self.n)

        bank = [ctx.enter_context(nc.psum_tensor(f"bank{i}", [P, 512], F32)) for i in range(8)]

        ring = sb("ring", [P, NSLOT, KD, BCOL])
        x_tm = sb("x_rows", [P, TT, D])
        x_cm = sb("x_cm", [P, KD, S])
        heads = sb("heads", [P, TT, D])
        ident = sb("ident", [P, P])
        ident2 = sb("ident2", [P, HD])
        head_ones = sb("head_ones", [P, P])
        tri_incl = sb("tri_incl", [P, P])
        tri_after = sb("tri_after", [P, P])
        chunk_mask = sb("chunk_mask", [P, 2, P])
        level_mask = sb("level_mask", [P, 6, P])
        level0_tm = sb("level0_tm", [P, P])
        scan_reset = sb("scan_reset", [P, S])
        vec_rows = sb("vec_rows", [P, P])
        vec = sb("vec", [P, n_rows])
        om_mu = sb("om_mu", [P, L * 8])
        om_ka = sb("om_ka", [P, L * 2])
        neg_w0 = sb("neg_w0", [P, L * 2])
        neg_a0 = sb("neg_a0", [P, L * 2])
        lr_w = sb("lr_w", [P, L, RW])
        g2_w = sb("g2_w", [P, L, RW])
        alpha_w = sb("alpha_w", [RANK, L, GW])
        rout_w = sb("rout_w", [P, KD, NE])
        rout_b = sb("rout_b", [P, NE])
        ln_vec = sb("ln_vec", [P, 2, D])
        gn_vec = sb("gn_vec", [P, 2, RW])
        ssd_small = sb("ssd_small", [P, 3, L, SH])

        gla_q = sb("gla_q", [P, 2, S])
        gla_k = sb("gla_k", [P, 2, S])
        gla_kt = sb("gla_kt", [P, TT, GW])
        gla_vg = sb("gla_vg", [P, TT, 2 * GW])
        z_tm = sb("z_rows", [P, TT, SW])
        xbc = sb("xbc", [P, XB, S])
        alr = sb("alr", [RANK, S])
        dt = sb("dt", [P, TT, SH])
        da = sb("da", [P, TT, SH])
        dte = sb("dte", [P, 4, SH])
        big = sb("big", [P, 16 * S])
        rwc = big[:, 0:8 * S].rearrange("p (b s) -> p b s", b=8)
        fac = [big[:, (8 + 2 * i) * S:(10 + 2 * i) * S].rearrange("p (b s) -> p b s", b=2) for i in range(4)]
        gmat = big[:].rearrange("p (t h x y s) -> p t h x y s", t=TT, h=NH, x=2, y=2)
        sc = [sb(f"sc{i}", [P, 2, S]) for i in range(4)]
        tmq = sb("tmq", [P, TT, 3, RW])
        a_w1 = sb("a_w1", [P, TT, NH, 2, HD])
        b_cm = sb("b_cm", [P, 2, S])
        k_cm = sb("k_cm", [P, 2, S])
        ar_cm = sb("ar_cm", [P, 2, 2, S])
        anchor = sb("anchor", [P, 2, 3, NC])
        anchor_g = sb("anchor_g", [P, 2, 3, NC])
        inv = sb("inv", [P, TT, NH, P])
        inv_t = sb("inv_t", [P, TT, NH, P])
        lvl = sb("lvl", [P, TT, NH, P])
        tm_t = sb("tm_t", [P, 2, 2, HD])
        g_tm = sb("g_rows", [P, TT, RW])
        st_rw = sb("st_rw", [P, 2, NC, HD])
        st_gla = sb("st_gla", [P, 2, NC, HD])
        st_ssd = sb("st_ssd", [P, 4 * HD])
        bonus = sb("bonus", [P, TT, NH])
        g_silu = sb("g_silu", [P, TT, GW])
        b_tm = sb("b_tm", [P, P])
        unit_gain = sb("unit_gain", [P, 1])
        ln_shift = sb("ln_shift", [P, 1])
        eps_ln = sb("eps_ln", [P, 1])
        eps_gn = sb("eps_gn", [P, 1])
        gn = sb("gn", [P, 2, TT, NH])
        rms = sb("rms", [P, TT, NH])
        rms_s = sb("rms_s", [P, TT, 2])
        bn6 = sb("bn6", [P, TT, 2, 6])
        bn2 = sb("bn2", [P, TT, 2])
        rt = sb("rt", [P, 6, TT, NE])
        rg = sb("rg", [P, 4, TT, NG])
        gate = sb("gate", [P, TT, NE])
        he = big[:, 0:FB * S].rearrange("p (b s) -> p b s", b=FB)
        sil = [big[:, (4 + i) * S:(5 + i) * S] for i in range(4)]

        slot_full = [ctx.enter_context(nc.semaphore(f"slot_full{i}")) for i in range(NSLOT)]
        x_loaded = ctx.enter_context(nc.semaphore("x_loaded"))
        rows_loaded = ctx.enter_context(nc.semaphore("rows_loaded"))
        small_loaded = ctx.enter_context(nc.semaphore("small_loaded"))
        ln_loaded = Signal("ln_loaded", 2 * 32)
        gn_loaded = Signal("gn_loaded", 32)
        stored = ctx.enter_context(nc.semaphore("stored"))
        masks_done = ctx.enter_context(nc.semaphore("masks_done"))
        s_small = ctx.enter_context(nc.semaphore("s_small"))
        rows_zero = ctx.enter_context(nc.semaphore("rows_zero"))
        pool_step = ctx.enter_context(nc.semaphore("pool_step"))
        vec_turned = ctx.enter_context(nc.semaphore("vec_turned"))
        vec_ready = ctx.enter_context(nc.semaphore("vec_ready"))
        SIG = {}
        for name, per in dict(
                t_x=4, t_x1=4, t_proj=14, t_lowrank=4, t_turned=5, t_pair=8, t_ltm=2, t_mv=2, t_lp=10, t_inv=10, t_xa=2,
                t_q=1, t_carry=1, t_srw=3, t_yrw=1, t_glaz=1, t_ssd_tm=3, t_edge=1, t_cb=1, t_seg=4, t_yssd=3,
                t_sssd=1, t_gkt=1, t_gsc=2, t_sgla=1, t_ygla=1, t_cat=4, t_mix=4, t_route=1, t_gu=FB * NE, t_down=NE,
                v_proj=8, v_gates=2, v_ssmax=1, v_decay=1, v_ratio=1, v_bonus=1, v_kcm=1, v_bcm=1, v_rcm=1,
                v_pair=8, v_inv0=2, v_lvl=10, v_inv=10, v_q=1, v_carry=1, v_srw=3, v_gz=1, v_gcum=1, v_gqk=1,
                v_xbc=3, v_dt=1, v_da=1, v_lhs=4, v_w=4, v_xdt=2, v_xw=1, v_sssd=1, v_yssd=2,
                v_gsc=2, v_sgla=3, v_gnvar=1, v_glasum=1, v_heads=3, v_var=4, v_x1=1, v_logit=1,
 v_he=FB * NE, v_acc=NE, v_x2=1, v_cat=4,
                s_x=4, s_x1=4, s_route=1, s_mu=4, s_conv=3, s_low=2, s_sq=1, s_ez=1, s_ea=1, s_g=1, s_norm=1, s_e=3, s_turned=5,
                s_mv=2, s_lp=10, s_xa=2, s_qk=2, s_vg=2, s_z=2, s_gln=1, s_ge=1, s_silx=3, s_dtl=1, s_seg=4,
                s_edge=1, s_xs=3, s_rssd=2, s_gnr=1, s_rgla=1, s_cat=4, s_rstd=4, s_eg=FB * NE, s_expl=1,
                s_silg=1, s_silz=2).items():
            SIG[name] = Signal(name, per)

        def done(name, l, n=None):
            assert n is None or 1 <= n <= SIG[name].per
            return SIG[name](l, n)

        def inc(ins, name):
            SIG[name].given += 1
            return ins.then_inc(SIG[name].sem, 1)

        def last_use(l, name):
            kind = name.rstrip("0123456789")
            e = int(name[len(kind):] or 0)
            n = {"rw": 2 * e + 2, "xbc": 2 * e + 6, "qk": 10, "vg": 12, "z": 14, "out": 2 * e + 2,
                 "gate": (e + 1) * FB, "up": (e + 1) * FB, "down": e + 1}[kind]
            return {"out": "t_mix", "gate": "t_gu", "up": "t_gu", "down": "t_down"}.get(kind, "t_proj"), l, n

        def vcol(name, l, b):
            at, per = rows[name]
            return vec[:, at + l * per + b:at + l * per + b + 1]

        def halves(h):
            return slice(HALF * (h % 2), HALF * (h % 2) + HALF), h // 2

        def tile_(j):
            return slice(P * j, P * j + P)

        def each(ap, n):
            return ap.unsqueeze(1).to_broadcast([P, n, ap.shape[-1]])

        def wide(ap, n):
            return ap.unsqueeze(2).to_broadcast([P, ap.shape[1], n])

        V, A, T, G = nc.vector, nc.scalar, nc.tensor, nc.gpsimd
        block = ctx.enter_context(nc.Block())


        def seg_in(q, i):
            return sc[q][:].rearrange("p b s -> p (b s)")[:, tile_(i)]

        def seg_w4(q):
            return (lvl, inv)[q // 2][:, q % 2]

        def seg_w(q, i):
            return seg_w4(q)[:, i, :]

        def xdt(j):
            return inv_t[:, j].rearrange("p h s -> p (h s)")

        xw = b_cm[:].rearrange("p b s -> p (b s)")

        def gsc4(j):
            return sc[j][:].rearrange("p b s -> p (b s)").rearrange("p (h s) -> p h s", h=NH)

        def gsc(j, h):
            return gsc4(j)[:, h, :]

        def cat_gain(l, b):
            return vcol("gla_norm_g", l, 0) if b < 2 else vcol("ssd_norm_g", l, b - 2) if b < 6 else unit_gain[:]
        @block.sync
        def _(sp):
            for j in range(TT):
                sp.dma_start(x_tm[:, j, :], t["x"][0, tile_(j), :]).then_inc(x_loaded, 16)
            sp.wait_ge(rows_zero, 1)
            for name, (at, per) in rows.items():
                src = t[name]
                if name == "gla_norm_g":
                    for h in range(2):
                        sp.dma_start(vec_rows[at:at + L, h * HD:(h + 1) * HD], src).then_inc(rows_loaded, 16)
                    continue
                if name == "ssd_conv_w":
                    flat = src.rearrange("l k (b p) -> (l k b) p", p=P)
                elif name == "rwkv_r_k":
                    flat = src.rearrange("l (b h) n -> (l b) (h n)", h=2)
                else:
                    flat = src.rearrange("l (b p) -> (l b) p", p=P)
                sp.dma_start(vec_rows[at:at + L * per, :], flat).then_inc(rows_loaded, 16)
            for n, (l, name, parts) in enumerate(order):
                if n >= NSLOT:
                    sp.wait_ge(*done(*last_use(*order[n - NSLOT][:2])))
                for src, c in parts:
                    rows_n, cols = src.shape[1], src.shape[2]
                    dst = ring[:, n % NSLOT].rearrange("p k n -> p (k n)").rearrange("p (k n) -> p k n", k=rows_n)
                    sp.dma_start(dst[:, :, c:c + cols], src).then_inc(slot_full[n % NSLOT], 16)
            sp.wait_ge(*done("v_x2", L - 1))
            for j in range(TT):
                sp.dma_start(out[0, tile_(j), :], x_tm[:, j, :]).then_inc(stored, 16)
            sp.wait_ge(stored, 16 * TT)

        @block.gpsimd
        def _(pool):
            n = 0

            def step(ins):
                nonlocal n
                ins.then_inc(pool_step, 1)
                n += 1
                pool.wait_ge(pool_step, n)

            def keep(ap, base, pattern, mult, op=ALU.is_ge):
                step(G.affine_select(out=ap, in_=ap, compare_op=op, fill=0.0, base=base, pattern=pattern,
                                     channel_multiplier=mult))

            G.memset(vec_rows[:], 0.0).then_inc(rows_zero, 1)
            small = [(lr_w[0:HALF], t["rwkv_w2"].rearrange("l r c -> r l c")),
                     (lr_w[HALF:P], t["rwkv_a2"].rearrange("l r c -> r l c")),
                     (g2_w[:], t["rwkv_g2"].rearrange("l r c -> r l c")),
                     (alpha_w[:], t["gla_w_alpha"].rearrange("l r c -> r l c")),
                     (rout_w[:], t["router_w"].rearrange("(p k) e -> p k e", k=KD)),
                     (rout_b[:], t["router_b"].partition_broadcast(P))]
            for i, name in enumerate(("ssd_dt_bias", "ssd_A_log", "ssd_D")):
                for l in range(L):
                    small.append((ssd_small[:, i, l, :], t[name][l].partition_broadcast(P)))
            for dst, src in small:
                pool.dma_start(dst, src).then_inc(small_loaded, 16)
            n_small = len(small)

            for m in (ident, ident2, head_ones, tri_incl, tri_after, chunk_mask, level_mask, level0_tm, scan_reset):
                one = 0.0 if m is level_mask else 1.0
                step(G.memset(m[:], one))
            keep(ident[:], 0, [[-1, P]], 1)
            keep(ident[:], 0, [[1, P]], -1)
            for h in range(2):
                keep(ident2[HALF * h:HALF * h + HALF, :], 0, [[-1, HD]], 1)
                keep(ident2[HALF * h:HALF * h + HALF, :], 0, [[1, HD]], -1)
            halves2 = head_ones[:].rearrange("p (b c) -> p b c", b=2)
            keep(halves2, 0, [[-HALF, 2], [0, HALF]], 1)
            keep(halves2, HALF - 1, [[HALF, 2], [0, HALF]], -1)
            keep(tri_incl[:], 0, [[1, P]], -1)
            keep(tri_after[:], -1, [[-1, P]], 1)
            for i in range(2):
                m = chunk_mask[:, i, :].rearrange("p (b c) -> p b c", b=2)
                keep(m, 0, [[-CH, 2], [0, CH]], 1)
                keep(m, i - 1, [[CH, 2], [1, CH]], -1)
            for j in range(6):
                m, nb = 2 ** j, P // 2 ** (j + 1)
                v = level_mask[:, j, :].rearrange("p (b h i) -> p b h i", h=2, i=m)[:, :, 1, :]
                step(G.memset(v, 1.0))
                keep(v, 0, [[-2 * m, nb], [0, m]], 1)
                keep(v, m - 1, [[2 * m, nb], [0, m]], -1)
            v = level0_tm[:].rearrange("p (b h) -> p b h", h=2)
            step(G.memset(v[:, :, 1], 0.0))
            keep(v[:, :, 0], -1, [[-2, P // 2]], 1)
            keep(v[:, :, 0], 1, [[2, P // 2]], -1)
            step(G.memset(scan_reset[:].rearrange("p (c i) -> p c i", i=CH)[:, :, 0], 0.0))
            for ap, value in ((ln_shift, 15 * float(np.log(2.0))), (eps_ln, EPS), (eps_gn, GN_EPS)):
                step(G.memset(ap[:], value))
            G.memset(unit_gain[:], 1.0).then_inc(masks_done, 1)
            for l in range(L):
                if l:
                    pool.wait_ge(*done("v_x2", l - 1))
                for which in range(2):
                    if which:
                        pool.wait_ge(*done("v_x1", l))
                    for i, name in enumerate(("ln1_g", "ln1_b") if which == 0 else ("ln2_g", "ln2_b")):
                        pool.dma_start(ln_vec[:, i, :], t[name][l].partition_broadcast(P)).then_inc(ln_loaded.sem, 16)
                    if which == 0:
                        for i, name in enumerate(("rwkv_ln_g", "rwkv_ln_b")):
                            pool.dma_start(gn_vec[:, i, :], t[name][l].partition_broadcast(P)) \
                                .then_inc(gn_loaded.sem, 16)

        @block.tensor
        def _(pe):
            def weights(l, name):
                n = index[l, name]
                pe.wait_ge(slot_full[n % NSLOT], landed[n])
                return ring[:, n % NSLOT]

            rows_chain = Chain("t_rows")

            def rows_done(m):
                rows_chain.add(m)
                rows_chain.join(pe)

            def turn_x(l):
                for i in range(4):
                    for k in (2 * i, 2 * i + 1):
                        for j in range(TT):
                            m = T.transpose(bank[i][:, (k % 2) * S + P * j:(k % 2) * S + P * j + P],
                                            x_tm[:, j, k::KD], ident[:])
                    inc(m, "t_x")

            def project(l, i):
                if i < 2:
                    pass
                elif i - 2 < 8:
                    pe.wait_ge(*done("v_proj", l, i - 1))
                else:
                    pe.wait_ge(*done(("s_qk", "s_qk", "s_vg", "s_vg")[i - 10], l, (i - 10) % 2 + 1))
                dst = bank[i % 2]
                name = ("rw0", "rw0", "rw1", "rw1", "xbc0", "xbc0", "xbc1", "xbc1", "qk", "qk", "vg", "vg", "z", "z")[i]
                w = weights(l, name)

                def cm(out_, c, n):
                    for k in range(KD):
                        m = T.matmul(out_, w[:, k, c:c + n], x_cm[:, k, :], start=(k == 0), stop=(k == KD - 1))
                    return m

                def tm(out_, j, c, n):
                    for k in range(KD):
                        m = T.matmul(out_, x_cm[:, k, tile_(j)], w[:, k, c:c + n], start=(k == 0), stop=(k == KD - 1))
                    return m

                if i == 7:
                    c = XBC - BCOL
                    cm(dst[0:RANK, 0:S], c + SH, RANK)
                    for j in range(TT):
                        m = tm(dst[:, S + SH * j:S + SH * j + SH], j, c, SH)
                elif i < 10:
                    for b in range(2):
                        m = cm(dst[:, b * S:b * S + S], (2 * (i % 2) + b) * P if i != 6 else b * P, P)
                else:
                    m = tm(dst[:], i % 2, 0, BCOL)
                inc(m, "t_proj")

            for l in range(L):
                def proj(i):
                    project(l, i)

                if l == 0:
                    pe.wait_ge(x_loaded, 16 * TT)
                    pe.wait_ge(masks_done, 1)
                    turn_x(0)
                    pe.wait_ge(rows_loaded, 16 * (len(rows) + 1))
                    T.transpose(bank[4][:, 0:P], vec_rows[:], ident[:]).then_inc(vec_turned, 1)
                    pe.wait_ge(small_loaded, 16 * (6 + 3 * L))
                pe.wait_ge(*done("s_x", l))
                for i in range(4):
                    proj(i)
                proj(4)
                pe.wait_ge(*done("v_gates", l, 1))
                for b in range(2):
                    m = T.matmul(bank[2][:, b * S:b * S + S], lr_w[0:HALF, l, b * P:b * P + P],
                                 fac[3][0:HALF, 0, :], start=True, stop=True)
                inc(m, "t_lowrank")
                for b in range(2):
                    m = T.matmul(bank[3][:, b * S:b * S + S], lr_w[HALF:P, l, b * P:b * P + P],
                                 rwc[HALF:P, 6, :], start=True, stop=True)
                inc(m, "t_lowrank")
                pe.wait_ge(*done("v_gates", l, 2))
                for j in range(TT):
                    m = T.matmul(bank[4][:, j * RW:j * RW + RW], fac[3][:, 1, tile_(j)], g2_w[:, l, :],
                                 start=True, stop=True)
                inc(m, "t_lowrank")
                pe.wait_ge(*done("s_sq", l))
                inc(T.matmul(bank[5][:], head_ones[:], fac[2], start=True, stop=True), "t_lowrank")
                for i in (5, 6, 7):
                    proj(i)
                pe.wait_ge(*done("v_ssmax", l))
                pe.wait_ge(*done("v_proj", l, 8))
                for b in range(2):
                    m = T.matmul(bank[5][:, b * S:b * S + S], alpha_w[:, l, b * P:b * P + P], alr[:],
                                 start=True, stop=True)
                inc(m, "t_glaz")
                proj(8)
                for j in range(TT):
                    for b in range(2):
                        m = T.transpose(bank[6][:, j * RW + b * P:j * RW + b * P + P], rwc[:, 4 + b, tile_(j)], ident[:])
                inc(m, "t_turned")
                pe.wait_ge(*done("v_bonus", l))
                pe.wait_ge(*done("s_g", l))
                for j in range(TT):
                    for b in range(2):
                        m = T.matmul(bank[4][:, j * NH + 2 * b:j * NH + 2 * b + 2], fac[0][:, b, tile_(j)],
                                     head_ones[:, 0:P:HALF], start=True, stop=True)
                inc(m, "t_turned")
                for src, dst, ready in ((ar_cm[:, :, 0, :], bank[7], "v_ratio"), (k_cm, bank[3], "v_kcm"),
                                        (b_cm, bank[2], "v_bcm")):
                    pe.wait_ge(*done(ready, l))
                    for j in range(TT):
                        for b in range(2):
                            m = T.transpose(dst[:, j * RW + b * P:j * RW + b * P + P], src[:, b, tile_(j)], ident[:])
                    inc(m, "t_turned")
                proj(9)
                pe.wait_ge(*done("v_rcm", l))
                for u in range(TT * NH):
                    j, h = divmod(u, NH)
                    ps, b = halves(h)
                    if u < 2:
                        pe.wait_ge(*done("s_turned", l, 3))
                    else:
                        pe.wait_ge(*done("v_pair", l, u - 1))
                    for i, src in enumerate((b_cm, k_cm)):
                        m = T.matmul(bank[6 + u % 2][:, 2 * P * i:2 * P * i + 2 * P], src[ps, b, tile_(j)],
                                     ar_cm[ps, b, :, tile_(j)], start=True, stop=True)
                    inc(m, "t_pair")
                pe.wait_ge(*done("s_turned", l, 5))
                for par in range(2):
                    for j in range(TT):
                        for h in (par, par + 2):
                            ps, b = halves(h)
                            m = T.matmul(bank[2 + j][:, tile_(h)], ar_cm[ps, b, 0, tile_(j)], b_cm[ps, b, tile_(j)],
                                         start=True, stop=True)
                        if par:
                            inc(m, "t_ltm")
                    if not par:
                        rows_done(m)
                for j in range(TT):
                    pe.wait_ge(*done("v_pair", l, NH * (j + 1)))
                    for h in range(NH):
                        m = T.matmul(bank[4][:, j * RW + h * HD:j * RW + h * HD + HD], gmat[:, j, h, 1, 0, :],
                                     tmq[:, j, 2, h * HD:h * HD + HD], start=True, stop=True)
                    inc(m, "t_mv")
                for lev in range(5):
                    for j in range(TT):
                        n = lev * TT + j
                        pe.wait_ge(*done("v_lvl", l, n + 1))
                        if lev == 0:
                            pe.wait_ge(*done("v_inv0", l, j + 1))
                        else:
                            pe.wait_ge(*done("v_inv", l, n - 1))
                        for h in range(NH):
                            m = T.matmul(bank[2 + j][:, tile_(h)], lvl[:, j, h, :], inv[:, j, h, :], start=True, stop=True)
                        inc(m, "t_lp")
                    if lev < 4:
                        proj(10 + lev)
                    for j in range(TT):
                        n = lev * TT + j
                        pe.wait_ge(*done("s_lp", l, n + 1))
                        if lev == 0:
                            pe.wait_ge(*done("s_mv", l, j + 1))
                            pe.wait_ge(*done("v_gz", l))
                        for h in range(NH):
                            m = T.matmul(bank[4 + j][:, tile_(h)], lvl[:, j, h, :], inv_t[:, j, h, :], start=True, stop=True)
                        if lev < 4:
                            for h in range(NH):
                                m = T.matmul(bank[6 + j][:, tile_(h)], inv_t[:, j, h, :], lvl[:, j, h, :],
                                             start=True, stop=True)
                        inc(m, "t_inv")
                for j in range(TT):
                    pe.wait_ge(*done("v_inv", l, 9 + j))
                    for h in range(NH):
                        m = T.matmul(bank[2 + j][:, tile_(h)], inv_t[:, j, h, :],
                                     a_w1[:, j, h].rearrange("p a b -> p (a b)"), start=True, stop=True)
                    inc(m, "t_xa")
                pe.wait_ge(*done("s_xa", l))
                for h in range(NH):
                    ps, b = halves(h)
                    for j in range(TT):
                        m = T.matmul(bank[4][ps, (j * 2 + b) * P:(j * 2 + b) * P + P], a_w1[:, j, h, 0, :],
                                     gmat[:, j, h, 0, 1, :], start=True, stop=True)
                inc(m, "t_q")
                for c in (1, 2):
                    pc, j = halves(c)
                    for h in range(NH):
                        ps, b = halves(h)
                        m = T.matmul(bank[6][ps, (b * 2 + c - 1) * HD:(b * 2 + c) * HD], a_w1[pc, j, h, 0, :],
                                     tmq[pc, j, 0, h * HD:h * HD + HD], start=True, stop=True)
                    if c == 1:
                        rows_done(m)
                inc(m, "t_carry")
                for j in range(TT):
                    for h in range(NH):
                        o = bank[5][:, j * RW + h * HD:j * RW + h * HD + HD]
                        T.matmul(o, gmat[:, j, h, 0, 1, :], a_w1[:, j, h, 1, :], start=(j == 0 and h == 0), stop=False,
                                 skip_group_check=True)
                        T.matmul(o, gmat[:, j, h, 1, 1, :], tmq[:, j, 2, h * HD:h * HD + HD], start=False, stop=False,
                                 skip_group_check=True)
                def carried(c, h):
                    ps, b = halves(h)
                    return bank[7][ps, (c * 2 + b) * HD:(c * 2 + b) * HD + HD]

                for c in (0, 2, 1):
                    pc, j = halves(c)
                    for h in range(NH):
                        hs = slice(h * HD, h * HD + HD)
                        T.matmul(carried(c, h), tmq[pc, j, 0, hs], a_w1[pc, j, h, 1, :], start=(c == 0 and h < 2), stop=False,
                                 skip_group_check=True)
                        m = T.matmul(carried(c, h), tmq[pc, j, 1, hs], tmq[pc, j, 2, hs], start=False, stop=(c == 0),
                                     skip_group_check=True)
                    if c == 1:
                        inc(m, "t_srw")
                    else:
                        rows_done(m)
                pe.wait_ge(*done("v_carry", l))
                for c in (1, 2):
                    pe.wait_ge(*done("v_srw", l, c))
                    for par in range(2):
                        for h in (par, par + 2):
                            ps, b = halves(h)
                            m = T.matmul(carried(c, h), tm_t[ps, b, c - 1, :], st_rw[ps, b, c, :], start=False, stop=True,
                                         skip_group_check=True)
                        if not par:
                            rows_done(m)
                    inc(m, "t_srw")
                pe.wait_ge(*done("v_q", l))
                pe.wait_ge(*done("v_srw", l))

                def from_state(q, st, name):
                    for par in range(2):
                        for c in range(1, NC):
                            pc, j = halves(c)
                            for h in (par, par + 2):
                                ps, b = halves(h)
                                m = T.matmul(bank[5][pc, j * RW + h * HD:j * RW + h * HD + HD],
                                             q[ps, b, c * CH:c * CH + CH], st[ps, b, c, :], start=False,
                                             stop=(c == NC - 1), skip_group_check=True)
                        if not par:
                            rows_done(m)
                    inc(m, name)

                from_state(ar_cm[:, :, 1, :], st_rw, "t_yrw")

                pe.wait_ge(*done("s_z", l))
                pe.wait_ge(*done("v_xbc", l))
                for j in range(TT):
                    for b in range(4):
                        m = T.transpose(bank[j][:, tile_(b)], xbc[:, b, tile_(j)], ident[:])
                    inc(m, "t_ssd_tm")
                inc(T.transpose(bank[2][:, 0:P], xbc[:, 4, tile_(0)], ident[:]), "t_ssd_tm")
                pe.wait_ge(*done("v_da", l))
                T.matmul(bank[2][:, 2 * P:2 * P + SH], tri_after[:], da[:, 0, :], start=True, stop=True)
                inc(T.matmul(bank[2][:, 2 * P + SH:2 * P + 2 * SH], tri_incl[:], da[:, 1, :], start=True, stop=True), "t_edge")
                for g in range(2):
                    ps = slice(HALF * g, HALF * g + HALF)
                    for j in range(TT):
                        m = T.matmul(bank[3][:, (j * 2 + g) * P:(j * 2 + g) * P + P], xbc[ps, 4, tile_(j)],
                                     xbc[ps, 5, tile_(j)], start=True, stop=True)
                    if g == 0:
                        rows_done(m)
                inc(m, "t_cb")
                for q in range(4):
                    pe.wait_ge(*done("v_lhs", l, q + 1))
                    if q == 3:
                        pe.wait_ge(*done("s_seg", l, 1))
                    dst = bank[(4, 6, 7, 4)[q]]
                    for i in range(4):
                        m = T.matmul(dst[:, tile_(i)], seg_in(q, i), tri_incl[:], start=True, stop=True)
                    inc(m, "t_seg")
                for j in range(TT):
                    pe.wait_ge(*done("v_w", l, 2 * j + 2))
                    pe.wait_ge(*done("s_xs", l, j + 1))
                    pe.wait_ge(*done("v_xdt", l, j + 1))
                    for h in range(SH):
                        m = T.matmul(bank[j][:, h * HD:h * HD + HD], seg_w(2 * j + h // 4, h % 4),
                                     xdt(j)[:, h * HD:h * HD + HD], start=True, stop=True)
                    inc(m, "t_yssd")
                pe.wait_ge(*done("v_xw", l))
                pe.wait_ge(*done("s_xs", l, 3))
                pe.wait_ge(*done("s_edge", l))
                for g in range(2):
                    ps = slice(HALF * g, HALF * g + HALF)
                    m = T.matmul(bank[2][ps, 0:4 * HD], b_tm[:, ps], xw[:, 4 * HD * g:4 * HD * g + 4 * HD],
                                 start=True, stop=True)
                inc(m, "t_sssd")
                pe.wait_ge(*done("v_sssd", l))
                pe.wait_ge(*done("s_seg", l, 2))
                for g in range(2):
                    ps = slice(HALF * g, HALF * g + HALF)
                    m = T.matmul(bank[6][:, 4 * HD * g:4 * HD * g + 4 * HD], xbc[ps, 5, tile_(1)], st_ssd[ps, :],
                                 start=True, stop=True)
                    if g == 0:
                        rows_done(m)
                inc(m, "t_yssd")

                pe.wait_ge(*done("v_gqk", l))
                pe.wait_ge(*done("v_w", l))
                for j in range(TT):
                    for b in range(2):
                        m = T.transpose(bank[3][:, j * GW + b * P:j * GW + b * P + P], gla_k[:, b, tile_(j)], ident[:])
                inc(m, "t_gkt")
                pe.wait_ge(*done("s_seg", l))
                for par in range(2):
                    for j in range(TT):
                        for h in (par, par + 2):
                            ps, b = halves(h)
                            m = T.matmul(bank[(4, 7)[j]][:, tile_(h)], gla_k[ps, b, tile_(j)], gla_q[ps, b, tile_(j)],
                                         start=True, stop=True)
                        if par:
                            inc(m, "t_gsc")
                    if not par:
                        rows_done(m)
                pe.wait_ge(*done("s_gln", l))
                for c in range(NC - 1):
                    pc, j = halves(c)
                    for h in range(NH):
                        ps, b = halves(h)
                        hs = slice(h * HD, h * HD + HD)
                        m = T.matmul(bank[2][ps, (c * 2 + b) * HD:(c * 2 + b) * HD + HD], gla_kt[pc, j, hs],
                                     gla_vg[pc, j, hs], start=True, stop=True)
                    if c < NC - 2:
                        rows_done(m)
                inc(m, "t_sgla")
                pe.wait_ge(*done("v_heads", l, 1))
                for j in range(TT):
                    pe.wait_ge(*done("v_gsc", l, j + 1))
                    for h in range(NH):
                        hs = slice(h * HD, h * HD + HD)
                        T.matmul(bank[5][:, j * GW + h * HD:j * GW + h * HD + HD], gsc(j, h), gla_vg[:, j, hs],
                                 start=(j == 0 and h == 0), stop=False, skip_group_check=True)
                pe.wait_ge(*done("v_sgla", l))
                from_state(gla_q, st_gla, "t_ygla")

                pe.wait_ge(*done("v_heads", l))
                for i in range(4):
                    for b in (2 * i, 2 * i + 1):
                        for j in range(TT):
                            m = T.transpose(bank[i][:, (b % 2) * S + P * j:(b % 2) * S + P * j + P],
                                            heads[:, j, b * P:b * P + P], ident[:])
                    inc(m, "t_cat")
                pe.wait_ge(*done("v_cat", l))
                pe.wait_ge(*done("s_cat", l))
                for hf in range(2):
                    w = weights(l, f"out{hf}")
                    for j in range(TT):
                        for b in range(KD):
                            m = T.matmul(bank[4 + 2 * hf + j][:], x_cm[:, b, tile_(j)], w[:, b, :], start=(b == 0),
                                         stop=(b == KD - 1))
                        inc(m, "t_mix")
                pe.wait_ge(*done("v_x1", l))
                for i in range(4):
                    for k in (2 * i, 2 * i + 1):
                        for j in range(TT):
                            m = T.transpose(bank[i][:, (k % 2) * S + P * j:(k % 2) * S + P * j + P],
                                            x_tm[:, j, k::KD], ident[:])
                    inc(m, "t_x1")
                pe.wait_ge(*done("s_x1", l))
                for j in range(TT):
                    for k in range(KD):
                        m = T.matmul(bank[4][:, j * NE:j * NE + NE], x_cm[:, k, tile_(j)], rout_w[:, k, :],
                                     start=(k == 0), stop=(k == KD - 1))
                inc(m, "t_route")
                for e in range(NE):
                    wg, wu = weights(l, f"gate{e}"), weights(l, f"up{e}")
                    for fb in range(FB):
                        n = e * FB + fb
                        if n >= 4:
                            pe.wait_ge(*done("v_he", l, n - 3))
                        for i, w in enumerate((wg, wu)):
                            for k in range(KD):
                                m = T.matmul(bank[n % 4][:, i * S:i * S + S], w[:, k, fb::FB], x_cm[:, k, :],
                                             start=(k == 0), stop=(k == KD - 1))
                        inc(m, "t_gu")
                    w = weights(l, f"down{e}").rearrange("p a b -> p (a b)").rearrange("p (b n) -> p b n", b=FB)
                    if e:
                        pe.wait_ge(*done("v_acc", l, e))
                    else:
                        pe.wait_ge(*done("v_logit", l))
                    pe.wait_ge(*done("v_he", l, (e + 1) * FB))
                    for j in range(TT):
                        for hf in range(2):
                            for fb in range(FB):
                                m = T.matmul(bank[4 + 2 * j + hf][:], he[:, fb, tile_(j)],
                                             w[:, fb, hf * 512:hf * 512 + 512], start=(fb == 0), stop=(fb == FB - 1))
                    inc(m, "t_down")
                if l < L - 1:
                    pe.wait_ge(*done("v_x2", l))
                    turn_x(l + 1)

        E_HALF = float(np.exp(-0.5))

        def conv_taps(l, i):
            for b in range(2):
                blk = 2 * (i - 4) + b
                for tap in range(TAPS - 1):
                    s = TAPS - 1 - tap
                    yield (xbc[:, blk, s:], bank[i % 2][:, b * S:b * S + S - s], vcol("ssd_conv_w", l, tap * XB + blk))

        @block.vector
        def _(dve):
            c = Chain("v_chain")

            def do(ins):
                c.add(ins)
                c.join(dve)

            def recip1(ap, plus=True):
                do(V.tensor_scalar(ap, ap, 1.0, None, ALU.add))
                return V.reciprocal(ap, ap)

            dve.wait_ge(vec_turned, 1)
            c.add(V.tensor_copy(vec[:], bank[4][:, 0:n_rows]))
            dve.wait_ge(small_loaded, 16 * (6 + 3 * L))
            c.join(dve)
            for dst, name, sc_, off in ((om_mu, "rwkv_mu", -1.0, 1.0), (om_ka, "rwkv_k_a", -1.0, 1.0),
                                        (neg_w0, "rwkv_w0", -1.0, 0.0), (neg_a0, "rwkv_a0", -1.0, 0.0)):
                at, per = rows[name]
                c.add(V.tensor_scalar(dst[:], vec[:, at:at + L * per], sc_, off, ALU.mult, ALU.add))
            c.join(dve)
            dve.wait_ge(s_small, 1)
            V.tensor_scalar(ssd_small[:, 1], ssd_small[:, 1], -1.0, None, ALU.mult).then_inc(vec_ready, 1)
            dve.wait_ge(vec_ready, 1)

            def cat(p):
                return p.rearrange("p b s -> p (b s)")

            def by_chunk(p):
                return p.rearrange("p b (c i) -> p (b c) i", i=CH)

            def anchors(cum, an):
                v = cum.rearrange("p b (c i) -> p b c i", i=CH)
                do(V.tensor_copy(an[:, :, 0, :], v[:, :, :, CH // 2 - 1]))
                do(V.tensor_tensor(an[:, :, 1, :], v[:, :, :, CH - 1], an[:, :, 0, :], ALU.subtract))
                c.add(V.tensor_tensor(an[:, :, 2, 0:NC - 1], an[:, :, 1, 0:NC - 1], an[:, :, 0, 1:NC], ALU.add))
                do(V.tensor_copy(an[:, :, 2, NC - 1:NC], an[:, :, 1, NC - 1:NC]))

            def minus_anchor(out_, cum, an):
                for b in range(2):
                    i = V.tensor_tensor(out_[:, b].rearrange("p (c i) -> p c i", i=CH),
                                        cum[:, b].rearrange("p (c i) -> p c i", i=CH),
                                        wide(an[:, b, 0, :], CH), ALU.subtract)
                    if b == 0:
                        c.add(i)
                return i

            def layer_norm(l, which):
                for j in range(TT):
                    if which == 0:
                        for hf in range(2):
                            dve.wait_ge(*done("t_mix", l, 2 * hf + j + 1))
                            cs = slice(hf * 512, hf * 512 + 512)
                            c.add(V.scalar_tensor_tensor(out=x_tm[:, j, cs], in0=x_tm[:, j, cs], scalar=ALPHA,
                                                         in1=bank[4 + 2 * hf + j][:], op0=ALU.mult, op1=ALU.add))
                        c.join(dve)
                    for hf in range(2):
                        c.add(V.bn_stats(bn6[:, j, hf, :], x_tm[:, j, hf * 512:hf * 512 + 512]))
                    c.join(dve)
                    inc(V.bn_aggr(bn2[:, j, :], bn6[:, j].rearrange("p a b -> p (a b)")), "v_var")
                dve.wait_ge(ln_loaded.sem, 64 * l + 32 * (which + 1))
                for j in range(TT):
                    dve.wait_ge(*done("s_rstd", l, 2 * which + j + 1))
                    do(V.tensor_scalar(x_tm[:, j], x_tm[:, j], bn2[:, j, 0:1], bn2[:, j, 1:2], ALU.subtract, ALU.mult))
                    do(V.tensor_tensor(x_tm[:, j], x_tm[:, j], ln_vec[:, 0], ALU.mult))
                    ins = V.tensor_tensor(x_tm[:, j], x_tm[:, j], ln_vec[:, 1], ALU.add)
                inc(ins, "v_x1" if which == 0 else "v_x2")

            for l in range(L):
                for i in range(4):
                    dve.wait_ge(*done("s_mu", l, i + 1))
                    for b in range(2):
                        k = 2 * i + b
                        ins = V.scalar_tensor_tensor(out=rwc[:, k, 1:], in0=bank[i % 2][:, b * S:b * S + S - 1],
                                                     scalar=vcol("rwkv_mu", l, k), in1=rwc[:, k, 1:],
                                                     op0=ALU.mult, op1=ALU.add)
                        if b == 0:
                            c.add(ins)
                    c.join(dve)
                    inc(ins, "v_proj")
                dve.wait_ge(*done("v_proj", l, 4))
                dve.wait_ge(*done("s_low", l, 1))
                th = fac[3][0:HALF, 0, :]
                do(recip1(th))
                inc(V.tensor_scalar(th, th, 2.0, -1.0, ALU.mult, ALU.add), "v_gates")
                dve.wait_ge(*done("s_low", l, 2))
                inc(recip1(fac[3][:, 1, :]), "v_gates")

                def conv(i):
                    dve.wait_ge(*done("s_conv", l, i - 3))
                    for n, (o, p, w) in enumerate(conv_taps(l, i)):
                        if n % 3:
                            c.join(dve)
                        ins = V.scalar_tensor_tensor(out=o, in0=p, scalar=w, in1=o, op0=ALU.mult, op1=ALU.add)
                        if n < 5:
                            c.add(ins)
                    c.join(dve)
                    inc(ins, "v_proj")

                conv(4)
                dve.wait_ge(*done("t_lowrank", l, 4))
                inc(V.tensor_scalar(cat(fac[2]), bank[5][:], 1e-24, None, ALU.max), "v_ssmax")
                dve.wait_ge(*done("s_ez", l))
                do(recip1(cat(fac[0])))
                do(V.tensor_scalar(cat(fac[0]), cat(fac[0]), -E_HALF, None, ALU.mult))
                dve.wait_ge(*done("t_lowrank", l, 3))
                for b in range(2):
                    c.add(V.tensor_tensor_scan(fac[3][:, b], scan_reset[:], fac[0][:, b], 0.0, ALU.mult, ALU.add))
                c.join(dve)
                anchors(fac[3], anchor)
                do(minus_anchor(fac[3], fac[3], anchor))
                inc(V.tensor_tensor(cat(fac[0]), cat(fac[3]), cat(fac[0]), ALU.subtract), "v_decay")
                conv(5)
                dve.wait_ge(*done("s_ea", l))
                do(recip1(cat(fac[1])))
                dve.wait_ge(*done("s_norm", l))
                for b in range(2):
                    c.add(V.scalar_tensor_tensor(out=fac[2][:, b], in0=rwc[:, 2 + b], scalar=vcol("rwkv_k_k", l, b),
                                                 in1=fac[2][:, b], op0=ALU.mult, op1=ALU.mult))
                c.join(dve)
                dve.wait_ge(*done("s_e", l, 1))
                inc(V.scalar_tensor_tensor(out=ar_cm[:, :, 0, :], in0=fac[2], scalar=-1.0, in1=fac[0],
                                           op0=ALU.mult, op1=ALU.mult), "v_ratio")
                dve.wait_ge(*done("v_ratio", l))
                for b in range(2):
                    c.add(V.tensor_scalar(fac[0][:, b], fac[1][:, b], vcol("rwkv_k_a", l, b),
                                          om_ka[:, l * 2 + b:l * 2 + b + 1], ALU.mult, ALU.add))
                c.join(dve)
                do(V.tensor_tensor(rwc[:, 2:4], rwc[:, 2:4], fac[0], ALU.mult))
                for b in range(2):
                    ins = V.scalar_tensor_tensor(out=fac[0][:, b], in0=rwc[:, b], scalar=vcol("rwkv_r_k", l, b),
                                                 in1=rwc[:, 2 + b], op0=ALU.mult, op1=ALU.mult)
                    if b == 0:
                        c.add(ins)
                c.join(dve)
                inc(ins, "v_bonus")
                do(V.tensor_tensor(fac[1], fac[2], fac[1], ALU.mult))
                dve.wait_ge(*done("s_e", l, 2))
                inc(V.tensor_tensor(k_cm[:], rwc[:, 2:4], b_cm[:], ALU.mult), "v_kcm")
                dve.wait_ge(*done("v_kcm", l))
                inc(V.tensor_tensor(b_cm[:], fac[1], b_cm[:], ALU.mult), "v_bcm")
                dve.wait_ge(*done("s_e", l, 3))
                inc(V.tensor_tensor(ar_cm[:, :, 1, :], rwc[:, 0:2], fac[3], ALU.mult), "v_rcm")
                conv(6)
                dve.wait_ge(*done("t_proj", l, 8))
                c.add(V.tensor_copy(alr[:], bank[1][0:RANK, 0:S]))
                ins = V.tensor_tensor(dt[:], bank[1][:, S:S + TT * SH].rearrange("p (j h) -> p j h", j=TT),
                                      each(ssd_small[:, 0, l, :], TT), ALU.add)
                c.join(dve)
                inc(ins, "v_proj")

                dve.wait_ge(*done("t_glaz", l))
                for b in range(2):
                    ins = V.tensor_scalar(sc[1][:, b], bank[5][:, b * S:b * S + S], vcol("gla_b_alpha", l, b), None, ALU.add)
                inc(ins, "v_gz")

                for u in range(TT * NH):
                    j, h = divmod(u, NH)
                    dve.wait_ge(*done("t_pair", l, u + 1))
                    inc(V.tensor_tensor(gmat[:, j, h].rearrange("p x y s -> p x (y s)"),
                                        bank[6 + u % 2][:].rearrange("p (x z) -> p x z", x=2),
                                        each(chunk_mask[:].rearrange("p y s -> p (y s)"), 2), ALU.mult), "v_pair")
                for j in range(TT):
                    dve.wait_ge(*done("v_pair", l, NH * (j + 1)))
                    c.add(V.tensor_tensor(inv_t[:, j], gmat[:, j, :, 0, 0, :], each(level_mask[:, 0, :], NH), ALU.mult))
                    inc(V.tensor_tensor(lvl[:, j], gmat[:, j, :, 0, 0, :], each(level_mask[:, 1, :], NH), ALU.mult), "v_lvl")
                    dve.wait_ge(*done("t_ltm", l, j + 1))
                    do(V.tensor_tensor(inv[:, j], bank[2 + j][:].rearrange("p (h s) -> p h s", h=NH),
                                       each(level0_tm[:], NH), ALU.mult))
                    do(V.tensor_tensor(inv_t[:, j], inv_t[:, j], each(ident[:], NH), ALU.add))
                    inc(V.tensor_tensor(inv[:, j], inv[:, j], each(ident[:], NH), ALU.add), "v_inv0")

                def xbc_silu(i):
                    dve.wait_ge(*done("s_silx", l, i + 1))
                    do(recip1(cat(sc[0][:])))
                    inc(V.tensor_tensor(xbc[:, 2 * i:2 * i + 2], xbc[:, 2 * i:2 * i + 2], sc[0][:], ALU.mult), "v_xbc")

                def gla_cum():
                    dve.wait_ge(*done("s_ge", l))
                    do(V.scalar_tensor_tensor(out=cat(sc[1][:]), in0=cat(sc[1][:]), scalar=0.0, in1=cat(sc[2][:]),
                                              op0=ALU.min, op1=ALU.subtract))
                    for b in range(2):
                        c.add(V.tensor_tensor_scan(sc[3][:, b], scan_reset[:], sc[1][:, b], 0.0, ALU.mult, ALU.add))
                    c.join(dve)
                    anchors(sc[3][:], anchor_g)
                    inc(minus_anchor(sc[3], sc[3], anchor_g), "v_gcum")

                def gla_qk():
                    dve.wait_ge(*done("s_expl", l))
                    dve.wait_ge(*done("s_qk", l))
                    c.add(V.scalar_tensor_tensor(out=cat(gla_q[:]), in0=cat(gla_q[:]), scalar=HD ** -0.5,
                                                 in1=cat(sc[2][:]), op0=ALU.mult, op1=ALU.mult))
                    ins = V.tensor_tensor(cat(gla_k[:]), cat(gla_k[:]), cat(sc[3][:]), ALU.mult)
                    c.join(dve)
                    inc(ins, "v_gqk")

                def ssd_dt():
                    dve.wait_ge(*done("s_dtl", l))
                    inc(V.scalar_tensor_tensor(out=dt[:], in0=dt[:], scalar=0.0, in1=dte[:, 0:2], op0=ALU.max,
                                               op1=ALU.add), "v_dt")
                    dve.wait_ge(*done("v_dt", l))
                    inc(V.tensor_tensor(da[:], dt[:], each(ssd_small[:, 1, l, :], TT), ALU.mult), "v_da")

                def gate_silu():
                    dve.wait_ge(*done("s_silg", l))
                    for j in range(TT):
                        g = g_silu[:, j]
                        do(recip1(g))
                        c.add(V.tensor_tensor(gla_vg[:, j, GW:], gla_vg[:, j, GW:], g, ALU.mult))
                    c.join(dve)

                fill = [lambda: xbc_silu(0), gla_cum, lambda: xbc_silu(1), ssd_dt, gla_qk, lambda: xbc_silu(2)]
                for lev in range(5):
                    for j in range(TT):
                        n = lev * TT + j
                        dve.wait_ge(*done("t_inv", l, n + 1))
                        if lev < 4:
                            c.add(V.tensor_tensor(inv[:, j], inv[:, j],
                                                  bank[6 + j][:].rearrange("p (h s) -> p h s", h=NH), ALU.add))
                        ins = V.tensor_tensor(inv_t[:, j], inv_t[:, j],
                                              bank[4 + j][:].rearrange("p (h s) -> p h s", h=NH), ALU.add)
                        c.join(dve)
                        inc(ins, "v_inv")
                        if lev < 4:
                            inc(V.tensor_tensor(lvl[:, j], gmat[:, j, :, 0, 0, :],
                                                each(level_mask[:, lev + 2, :], NH), ALU.mult), "v_lvl")
                    if fill:
                        fill.pop(0)()
                for f in fill:
                    f()
                for q in range(4):
                    if q == 0:
                        for name in ("v_gqk", "v_da", "v_xbc"):
                            dve.wait_ge(*done(name, l))
                    for i in range(4):
                        j, h = q // 2, 4 * (q % 2) + i
                        ins = V.tensor_scalar(seg_in(q, i), tri_after[:], da[:, j, h:h + 1], None, ALU.mult)
                        if i < 3:
                            c.add(ins)
                    c.join(dve)
                    inc(ins, "v_lhs")
                dve.wait_ge(*done("t_q", l))
                for j in range(TT):
                    ins = V.tensor_tensor(ar_cm[:, :, 1, tile_(j)], ar_cm[:, :, 1, tile_(j)],
                                          bank[4][:, j * S:j * S + S].rearrange("p (b s) -> p b s", b=2), ALU.add)
                    if j == 0:
                        c.add(ins)
                c.join(dve)
                inc(ins, "v_q")
                dve.wait_ge(*done("t_carry", l))
                inc(V.tensor_tensor(tm_t[:].rearrange("p b c n -> p (b c) n"),
                                    bank[6][:, 0:S].rearrange("p (b n) -> p b n", n=HD), each(ident2[:], 4), ALU.add), "v_carry")
                dve.wait_ge(*done("s_e", l, 3))
                for i in range(NC - 1):
                    dve.wait_ge(*done("t_srw", l, i + 1))
                    inc(V.tensor_tensor(st_rw[:, :, i + 1, :],
                                        bank[7][:, i * P:i * P + P].rearrange("p (b n) -> p b n", b=2),
                                        wide(anchor[:, :, 2, i], HD), ALU.mult), "v_srw")
                dve.wait_ge(*done("t_cb", l))
                do(V.tensor_tensor(k_cm[:].rearrange("p a b -> p (a b)").rearrange("p (q s) -> p q s", q=4),
                                   bank[3][:].rearrange("p (q s) -> p q s", q=4), each(tri_incl[:], 4), ALU.mult))
                for j in range(TT):
                    dve.wait_ge(*done("s_xs", l, j + 1))
                    inc(V.tensor_tensor(xdt(j).rearrange("p (h n) -> p h n", n=HD),
                                        heads[:, j, GW:GW + SW].rearrange("p (h n) -> p h n", n=HD),
                                        wide(dt[:, j, :], HD), ALU.mult), "v_xdt")
                for q in range(4):
                    dve.wait_ge(*done("s_seg", l, q + 1))
                    cb = k_cm[:].rearrange("p a b -> p (a b)")[:, q * P:q * P + P]
                    inc(V.tensor_tensor(seg_w4(q), seg_w4(q), each(cb, 4), ALU.mult), "v_w")
                dve.wait_ge(*done("s_edge", l))
                dve.wait_ge(*done("v_xdt", l, 1))
                inc(V.tensor_tensor(xw.rearrange("p (h n) -> p h n", n=HD), xdt(0).rearrange("p (h n) -> p h n", n=HD),
                                    wide(dte[:, 2, :], HD), ALU.mult), "v_xw")
                dve.wait_ge(*done("t_sssd", l))
                inc(V.tensor_copy(st_ssd[:], bank[2][:, 0:4 * HD]), "v_sssd")
                gate_silu()
                dve.wait_ge(*done("t_seg", l))
                for j in range(TT):
                    dve.wait_ge(*done("t_gsc", l, j + 1))
                    inc(V.tensor_tensor(gsc4(j), bank[(4, 7)[j]][:].rearrange("p (h s) -> p h s", h=NH),
                                        each(chunk_mask[:, 1, :], NH), ALU.mult), "v_gsc")
                dve.wait_ge(*done("t_sgla", l))
                for i in range(NC - 1):
                    src = bank[2][:, i * P:i * P + P].rearrange("p (b n) -> p b n", b=2)
                    dst = st_gla[:, :, i + 1, :]
                    if i:
                        do(V.tensor_tensor(dst, src, st_gla[:, :, i, :], ALU.add))
                        src = dst
                    inc(V.tensor_tensor(dst, src, wide(anchor_g[:, :, 2, i], HD), ALU.mult), "v_sgla")
                    dve.wait_ge(*done("v_sgla", l, i + 1))
                dve.wait_ge(*done("t_yrw", l))
                y = bank[5][:].rearrange("p (h n) -> p h n", n=HD)
                mean = gn[:, 0].rearrange("p j h -> p (j h)")
                rstd = gn[:, 1].rearrange("p j h -> p (j h)")
                yc, sq = cat(sc[2][:]).rearrange("p (h n) -> p h n", n=HD), cat(sc[3][:]).rearrange("p (h n) -> p h n", n=HD)
                do(V.tensor_reduce(mean, y, AX.X, ALU.add))
                do(V.tensor_scalar(mean, mean, 1.0 / HD, None, ALU.mult))
                do(V.tensor_tensor(yc, y, wide(mean, HD), ALU.subtract))
                do(V.tensor_tensor(sq, yc, yc, ALU.mult))
                inc(V.tensor_reduce(rstd, sq, AX.X, ALU.add), "v_gnvar")
                dve.wait_ge(*done("s_gnr", l))
                dve.wait_ge(gn_loaded.sem, 32 * (l + 1))
                do(V.tensor_tensor(yc, yc, wide(rstd, HD), ALU.mult))
                for j in range(TT):
                    o = heads[:, j, GW + SW:]
                    yj = sc[2][:, j]
                    bv = sc[3][:, j]
                    c.add(V.tensor_tensor(yj, yj, gn_vec[:, 0], ALU.mult))
                    do(V.tensor_tensor(bv.rearrange("p (h n) -> p h n", n=HD),
                                       tmq[:, j, 2, :].rearrange("p (h n) -> p h n", n=HD), wide(bonus[:, j, :], HD), ALU.mult))
                    do(V.tensor_tensor(yj, yj, gn_vec[:, 1], ALU.add))
                    do(V.tensor_tensor(yj, yj, bv, ALU.add))
                    ins = V.tensor_tensor(o, yj, g_tm[:, j], ALU.mult)
                    if j == 0:
                        c.add(ins)
                c.join(dve)
                inc(ins, "v_heads")
                for j in range(TT):
                    dve.wait_ge(*done("s_silz", l, j + 1))
                    zj, o = z_tm[:, j], heads[:, j, GW:GW + SW]
                    oh = o.rearrange("p (h n) -> p h n", n=HD)
                    do(recip1(cat(sc[2][:])) if j == 0 else recip1(cat(sc[3][:])))
                    do(V.tensor_tensor(zj, zj, cat(sc[2 + j][:]), ALU.mult))
                    do(V.tensor_tensor(oh, oh, wide(ssd_small[:, 2, l, :], HD), ALU.mult))
                    dve.wait_ge(*done("t_yssd", l, j + 1))
                    do(V.tensor_tensor(o, o, bank[j][:], ALU.add))
                    if j:
                        dve.wait_ge(*done("t_yssd", l, 3))
                        tmp = cat(sc[2][:])
                        do(V.tensor_tensor(tmp.rearrange("p (h n) -> p h n", n=HD),
                                           bank[6][:].rearrange("p (h n) -> p h n", n=HD), wide(dte[:, 3, :], HD), ALU.mult))
                        do(V.tensor_tensor(o, o, tmp, ALU.add))
                    inc(V.tensor_tensor(o, o, zj, ALU.mult), "v_yssd")
                for j in range(TT):
                    dve.wait_ge(*done("s_rssd", l, j + 1))
                    for g in range(2):
                        o = heads[:, j, GW + g * 256:GW + g * 256 + 256]
                        ins = V.tensor_scalar(o, o, rms_s[:, j, g:g + 1], None, ALU.mult)
                        if (j, g) != (1, 1):
                            c.add(ins)
                c.join(dve)
                inc(ins, "v_heads")
                dve.wait_ge(*done("t_ygla", l))
                do(V.tensor_copy(cat(sc[2][:]), bank[5][:]))
                do(V.tensor_tensor(cat(sc[3][:]), cat(sc[2][:]), cat(sc[2][:]), ALU.mult))
                rr = rms[:].rearrange("p j h -> p (j h)")
                inc(V.tensor_reduce(rr, cat(sc[3][:]).rearrange("p (h n) -> p h n", n=HD), AX.X, ALU.add), "v_glasum")
                dve.wait_ge(*done("s_rgla", l))
                do(V.tensor_tensor(yc, yc, wide(rr, HD), ALU.mult))
                for j in range(TT):
                    ins = V.tensor_tensor(heads[:, j, 0:GW], sc[2][:, j], gla_vg[:, j, GW:], ALU.mult)
                    if j == 0:
                        c.add(ins)
                c.join(dve)
                inc(ins, "v_heads")
                for i in (1, 3):
                    dve.wait_ge(*done("t_cat", l, i + 1))
                    for b in range(2):
                        inc(V.tensor_scalar(x_cm[:, 2 * i + b, :], bank[i][:, b * S:b * S + S], cat_gain(l, 2 * i + b),
                                            None, ALU.mult), "v_cat")
                layer_norm(l, 0)

                dve.wait_ge(*done("t_x1", l))
                for j in range(TT):
                    c.add(V.tensor_scalar(x_tm[:, j], x_tm[:, j], ALPHA, None, ALU.mult))
                dve.wait_ge(*done("t_route", l))
                inc(V.tensor_copy(rt[:, 0].rearrange("p j e -> p (j e)"), bank[4][:, 0:TT * NE]), "v_logit")
                dve.wait_ge(*done("s_route", l))
                score, sel = rt[:, 1], rt[:, 2]
                do(recip1(score))
                do(V.tensor_tensor(sel, score, each(rout_b[:], TT), ALU.add))
                s4 = sel.rearrange("p j (g k) -> p (j g) k", k=EPG)
                pr = rt[:, 3:5].rearrange("p a j e -> p (a j e)")[:, 0:6 * TT * NG].rearrange("p (k m) -> p k m", k=6)
                n = 0
                for a in range(EPG):
                    for b in range(a + 1, EPG):
                        c.add(V.tensor_tensor(pr[:, n, :], s4[:, :, a], s4[:, :, b], ALU.add))
                        n += 1
                c.join(dve)
                gs = rg[:, 0].rearrange("p j g -> p (j g)")
                do(V.tensor_reduce(gs, pr.rearrange("p k m -> p m k"), AX.X, ALU.max))
                beat = rg[:, 1]
                do(V.memset(beat, 0.0))
                g3 = rg[:, 0]
                for a in range(NG):
                    if a:
                        do(V.tensor_tensor(rg[:, 2, :, 0:a], g3[:, :, a:a + 1].to_broadcast([P, TT, a]), g3[:, :, 0:a], ALU.is_gt))
                        do(V.tensor_tensor(beat[:, :, 0:a], beat[:, :, 0:a], rg[:, 2, :, 0:a], ALU.add))
                    if a < NG - 1:
                        do(V.tensor_tensor(rg[:, 2, :, a + 1:], g3[:, :, a:a + 1].to_broadcast([P, TT, NG - 1 - a]),
                                           g3[:, :, a + 1:], ALU.is_ge))
                        do(V.tensor_tensor(beat[:, :, a + 1:], beat[:, :, a + 1:], rg[:, 2, :, a + 1:], ALU.add))
                do(V.tensor_scalar(beat, beat, 0.5, None, ALU.is_lt))
                rank = rt[:, 3]
                do(V.memset(rank, 0.0))
                r4 = rank.rearrange("p j (g k) -> p (j g) k", k=EPG)
                t4 = rt[:, 4].rearrange("p j (g k) -> p (j g) k", k=EPG)
                for a in range(EPG):
                    if a:
                        do(V.tensor_tensor(t4[:, :, 0:a], s4[:, :, a:a + 1].to_broadcast([P, TT * NG, a]), s4[:, :, 0:a], ALU.is_gt))
                        do(V.tensor_tensor(r4[:, :, 0:a], r4[:, :, 0:a], t4[:, :, 0:a], ALU.add))
                    if a < EPG - 1:
                        do(V.tensor_tensor(t4[:, :, a + 1:], s4[:, :, a:a + 1].to_broadcast([P, TT * NG, EPG - 1 - a]),
                                           s4[:, :, a + 1:], ALU.is_ge))
                        do(V.tensor_tensor(r4[:, :, a + 1:], r4[:, :, a + 1:], t4[:, :, a + 1:], ALU.add))
                do(V.tensor_scalar(rank, rank, 1.5, None, ALU.is_lt))
                do(V.tensor_tensor(r4, r4, wide(beat.rearrange("p j g -> p (j g)"), EPG), ALU.mult))
                do(V.tensor_tensor(gate[:], rank, score, ALU.mult))
                do(V.tensor_reduce(rms_s[:, :, 0], gate[:], AX.X, ALU.add))
                do(V.reciprocal(rms_s[:, :, 0], rms_s[:, :, 0]))
                do(V.tensor_tensor(gate[:], gate[:], wide(rms_s[:, :, 0], NE), ALU.mult))

                for e in range(NE):
                    for fb in range(FB):
                        n = e * FB + fb
                        dve.wait_ge(*done("s_eg", l, n + 1))
                        s_ = sil[n % 4]
                        do(recip1(s_))
                        do(V.tensor_tensor(s_, s_, bank[n % 4][:, 0:S], ALU.mult))
                        if e:
                            dve.wait_ge(*done("t_down", l, e))
                        inc(V.tensor_tensor(he[:, fb, :], s_, bank[n % 4][:, S:2 * S], ALU.mult), "v_he")
                    dve.wait_ge(*done("t_down", l, e + 1))
                    for j in range(TT):
                        for hf in range(2):
                            o = x_tm[:, j, hf * 512:hf * 512 + 512]
                            ins = V.scalar_tensor_tensor(out=o, in0=bank[4 + 2 * j + hf][:], scalar=gate[:, j, e:e + 1],
                                                         in1=o, op0=ALU.mult, op1=ALU.add)
                            if (j, hf) != (1, 1):
                                c.add(ins)
                    c.join(dve)
                    inc(ins, "v_acc")
                dve.wait_ge(*done("v_acc", l))
                layer_norm(l, 1)

        LN2 = float(np.log(2.0))

        @block.scalar
        def _(act):
            c = Chain("s_chain")

            def do(ins):
                c.add(ins)
                c.join(act)

            def flat(p):
                return p.rearrange("p b s -> p (b s)")

            def silu_arg(out_, in_, name):
                return inc(A.activation(out_, in_, ACT.Exp, scale=-1.0), name)

            A.preload_act_table_set("natural_log_exp_and_others")
            act.wait_ge(small_loaded, 16 * (6 + 3 * L))
            A.activation(ssd_small[:, 1], ssd_small[:, 1], ACT.Exp).then_inc(s_small, 1)
            for l in range(L):
                for i in range(4):
                    act.wait_ge(*done("t_x", l, i + 1))
                    inc(A.activation(x_cm[:, 2 * i:2 * i + 2, :], bank[i][:].rearrange("p (k s) -> p k s", k=2),
                                     ACT.Copy), "s_x")
                if l == 0:
                    act.wait_ge(vec_ready, 1)
                for i in range(4):
                    act.wait_ge(*done("t_proj", l, i + 1))
                    for b in range(2):
                        k = 2 * i + b
                        ins = A.activation(rwc[:, k, :], bank[i % 2][:, b * S:b * S + S], ACT.Copy,
                                           scale=om_mu[:, l * 8 + k:l * 8 + k + 1])
                    inc(ins, "s_mu")

                def conv(i):
                    act.wait_ge(*done("t_proj", l, i + 1))
                    for b in range(2):
                        blk = 2 * (i - 4) + b
                        ins = A.activation(xbc[:, blk, :], bank[i % 2][:, b * S:b * S + S], ACT.Identity,
                                           scale=vcol("ssd_conv_w", l, (TAPS - 1) * XB + blk), bias=vcol("ssd_conv_b", l, blk))
                    inc(ins, "s_conv")

                act.wait_ge(*done("v_proj", l, 4))
                inc(A.activation(fac[3][0:HALF, 0, :], rwc[0:HALF, 6, :], ACT.Exp, scale=-2.0), "s_low")
                inc(A.activation(fac[3][:, 1, :], rwc[:, 7, :], ACT.Exp, scale=-1.0), "s_low")
                for b in range(2):
                    ins = A.activation(fac[2][:, b], rwc[:, 2 + b], ACT.Square, scale=vcol("rwkv_k_k", l, b))
                inc(ins, "s_sq")
                conv(4)
                act.wait_ge(*done("t_lowrank", l, 1))
                for b in range(2):
                    ins = A.activation(fac[0][:, b], bank[2][:, b * S:b * S + S], ACT.Exp, scale=-1.0,
                                       bias=neg_w0[:, l * 2 + b:l * 2 + b + 1])
                inc(ins, "s_ez")
                act.wait_ge(*done("t_lowrank", l, 2))
                for b in range(2):
                    ins = A.activation(fac[1][:, b], bank[3][:, b * S:b * S + S], ACT.Exp, scale=-1.0,
                                       bias=neg_a0[:, l * 2 + b:l * 2 + b + 1])
                inc(ins, "s_ea")
                act.wait_ge(*done("t_lowrank", l, 3))
                inc(A.activation(g_tm[:], bank[4][:].rearrange("p (j c) -> p j c", j=TT), ACT.Copy), "s_g")
                act.wait_ge(*done("v_ssmax", l))
                do(A.activation(flat(fac[2]), flat(fac[2]), ACT.Ln, scale=2.0 ** 30))
                inc(A.activation(flat(fac[2]), flat(fac[2]), ACT.Exp, scale=-0.5, bias=ln_shift[:]), "s_norm")
                conv(5)
                act.wait_ge(*done("v_decay", l))
                inc(A.activation(flat(fac[0]), flat(fac[0]), ACT.Exp), "s_e")
                inc(A.activation(b_cm[:], fac[3], ACT.Exp, scale=-1.0), "s_e")
                A.activation(anchor[:, :, 2, :], anchor[:, :, 2, :], ACT.Exp)
                inc(A.activation(flat(fac[3]), flat(fac[3]), ACT.Exp), "s_e")
                conv(6)
                act.wait_ge(*done("v_proj", l, 8))
                do(A.activation(dte[:, 0:2], dt[:], ACT.Abs))
                do(A.activation(dte[:, 0:2], dte[:, 0:2], ACT.Exp, scale=-1.0))
                inc(A.activation(dte[:, 0:2], dte[:, 0:2], ACT.Ln, bias=1.0), "s_dtl")
                act.wait_ge(*done("v_gz", l))
                do(A.activation(flat(sc[2][:]), flat(sc[1][:]), ACT.Abs))
                do(A.activation(flat(sc[2][:]), flat(sc[2][:]), ACT.Exp, scale=-1.0))
                inc(A.activation(flat(sc[2][:]), flat(sc[2][:]), ACT.Ln, bias=1.0), "s_ge")
                for n, (src, dst) in enumerate(((6, tmq[:, :, 2, :]), (4, None), (7, None), (3, tmq[:, :, 1, :]),
                                                (2, tmq[:, :, 0, :]))):
                    act.wait_ge(*done("t_turned", l, n + 1))
                    if n == 1:
                        ins = A.activation(bonus[:].rearrange("p j h -> p (j h)"), bank[4][:, 0:TT * NH], ACT.Copy)
                    elif n == 2:
                        for j in range(TT):
                            ins = A.activation(a_w1[:, j, :, 0, :], bank[7][:, j * RW:j * RW + RW]
                                               .rearrange("p (h n) -> p h n", n=HD), ACT.Copy)
                    else:
                        ins = A.activation(dst, bank[src][:].rearrange("p (j c) -> p j c", j=TT), ACT.Copy)
                    inc(ins, "s_turned")
                for i, (name, dst) in enumerate((("s_qk", gla_q), ("s_qk", gla_k))):
                    act.wait_ge(*done("t_proj", l, 9 + i))
                    inc(A.activation(dst[:], bank[i][:].rearrange("p (b s) -> p b s", b=2), ACT.Copy), name)
                act.wait_ge(*done("t_mv", l))
                for j in range(TT):
                    inc(A.activation(a_w1[:, j, :, 1, :], bank[4][:, j * RW:j * RW + RW].rearrange("p (h n) -> p h n", n=HD),
                                     ACT.Copy), "s_mv")

                def silx(i):
                    act.wait_ge(*done("v_proj", l, 5 + i))
                    if i:
                        act.wait_ge(*done("v_xbc", l, i))
                    inc(A.activation(sc[0][:], xbc[:, 2 * i:2 * i + 2], ACT.Exp, scale=-1.0), "s_silx")

                def gla_exp():
                    act.wait_ge(*done("v_gcum", l))
                    A.activation(anchor_g[:, :, 2, :], anchor_g[:, :, 2, :], ACT.Exp, scale=1.0 / 16)
                    do(A.activation(sc[2][:], sc[3][:], ACT.Exp, scale=1.0 / 16))
                    inc(A.activation(sc[3][:], sc[3][:], ACT.Exp, scale=-1.0 / 16), "s_expl")

                def vg(i):
                    act.wait_ge(*done("t_proj", l, 11 + i))
                    inc(A.activation(gla_vg[:, i], bank[i % 2][:], ACT.Copy), "s_vg")

                def zz(i):
                    act.wait_ge(*done("t_proj", l, 13 + i))
                    inc(A.activation(z_tm[:, i], bank[i % 2][:], ACT.Copy), "s_z")

                fill = [lambda: (silx(0), vg(0)), lambda: (vg(1), gla_exp()), lambda: (silx(1), zz(0)), lambda: zz(1),
                        lambda: silx(2)]
                for lev in range(5):
                    for j in range(TT):
                        n = lev * TT + j
                        act.wait_ge(*done("t_lp", l, n + 1))
                        inc(A.activation(lvl[:, j], bank[2 + j][:].rearrange("p (h s) -> p h s", h=NH), ACT.Copy), "s_lp")
                    fill.pop(0)()
                act.wait_ge(*done("v_xbc", l))
                inc(A.activation(g_silu[:], gla_vg[:, :, GW:], ACT.Exp, scale=-1.0), "s_silg")
                for j in range(TT):
                    act.wait_ge(*done("t_xa", l, j + 1))
                    inc(A.activation(a_w1[:, j].rearrange("p h a n -> p (h a n)"), bank[2 + j][:], ACT.Copy), "s_xa")
                for j in range(TT):
                    act.wait_ge(*done("t_ssd_tm", l, j + 1))
                    inc(A.activation(heads[:, j, GW:GW + SW], bank[j][:], ACT.Copy), "s_xs")
                act.wait_ge(*done("t_edge", l))
                inc(A.activation(b_tm[:], bank[2][:, 0:P], ACT.Copy), "s_xs")
                act.wait_ge(*done("t_edge", l))
                inc(A.activation(dte[:, 2:4].rearrange("p a b -> p (a b)"), bank[2][:, 2 * P:2 * P + 2 * SH], ACT.Exp), "s_edge")
                act.wait_ge(*done("t_q", l))
                for q in range(4):
                    act.wait_ge(*done("t_seg", l, q + 1))
                    inc(A.activation(seg_w4(q), bank[(4, 6, 7, 4)[q]][:].rearrange("p (h s) -> p h s", h=4), ACT.Exp), "s_seg")
                act.wait_ge(*done("t_gkt", l))
                inc(A.activation(gla_kt[:], bank[3][:].rearrange("p (j c) -> p j c", j=TT), ACT.Copy), "s_gln")

                def rstd(out_, in_, n, eps, name):
                    do(A.activation(out_, in_, ACT.Ln, scale=1.0 / n, bias=eps[:]))
                    inc(A.activation(out_, out_, ACT.Exp, scale=-0.5), name)

                act.wait_ge(*done("v_gnvar", l))
                rstd(gn[:, 1], gn[:, 1], HD, eps_gn, "s_gnr")
                act.wait_ge(*done("v_heads", l, 1))
                for j in range(TT):
                    inc(A.activation(flat(sc[2 + j][:]), z_tm[:, j], ACT.Exp, scale=-1.0), "s_silz")
                for j in range(TT):
                    act.wait_ge(*done("v_yssd", l, j + 1))
                    for g in range(2):
                        ins = A.activation(k_cm[:, 0, :], heads[:, j, GW + g * 256:GW + g * 256 + 256], ACT.Square,
                                           accum_out=rms_s[:, j, g:g + 1])
                        do(ins)
                    rstd(rms_s[:, j], rms_s[:, j], SW // 2, eps_ln, "s_rssd")
                act.wait_ge(*done("v_glasum", l))
                rstd(rms[:], rms[:], HD, eps_ln, "s_rgla")
                for i in (0, 2):
                    act.wait_ge(*done("t_cat", l, i + 1))
                    for b in range(2):
                        inc(A.activation(x_cm[:, 2 * i + b, :], bank[i][:, b * S:b * S + S], ACT.Copy,
                                         scale=cat_gain(l, 2 * i + b)), "s_cat")

                def ln_rstd(which):
                    for j in range(TT):
                        act.wait_ge(*done("v_var", l, 2 * which + j + 1))
                        rstd(bn2[:, j, 1:2], bn2[:, j, 1:2], 1, eps_ln, "s_rstd")

                ln_rstd(0)
                for i in range(4):
                    act.wait_ge(*done("t_x1", l, i + 1))
                    inc(A.activation(x_cm[:, 2 * i:2 * i + 2, :], bank[i][:].rearrange("p (k s) -> p k s", k=2),
                                     ACT.Copy), "s_x1")
                act.wait_ge(*done("v_logit", l))
                inc(A.activation(rt[:, 1], rt[:, 0], ACT.Exp, scale=-1.0), "s_route")
                for n in range(NE * FB):
                    act.wait_ge(*done("t_gu", l, n + 1))
                    if n >= 4:
                        act.wait_ge(*done("v_he", l, n - 3))
                    inc(A.activation(sil[n % 4], bank[n % 4][:, 0:S], ACT.Exp, scale=-1.0), "s_eg")
                ln_rstd(1)

        for name, signal in SIG.items():
            assert signal.given == L * signal.per, (name, signal.given, signal.per)


_INS = ["x", "w_in", "gla_w_alpha", "gla_b_alpha", "gla_norm_g", "ssd_conv_w", "ssd_conv_b", "ssd_dt_bias", "ssd_A_log",
        "ssd_D", "ssd_norm_g", "rwkv_mu", "rwkv_w0", "rwkv_w2", "rwkv_a0", "rwkv_a2", "rwkv_g2", "rwkv_k_k", "rwkv_k_a",
        "rwkv_r_k", "rwkv_ln_g", "rwkv_ln_b", "w_out", "ln1_g", "ln1_b", "router_w", "router_b", "exp_w_gate",
        "exp_w_up", "exp_w_down", "ln2_g", "ln2_b"]


def kernel(**inputs):
    import numpy as _np
    import concourse.bacc as _bacc
    from concourse import mybir as _mybir
    from concourse.bass_utils import run_bass_kernel_spmd as _run

    nc = _bacc.Bacc("TRN2", target_bir_lowering=False, num_devices=1)
    arrays, aps = {}, {}
    for name in _INS:
        a = _np.ascontiguousarray(inputs[name])
        arrays[f"in_{name}"] = a
        aps[name] = nc.dram_tensor(f"in_{name}", a.shape, _mybir.dt.from_np(a.dtype), kind="ExternalInput").ap()
    shape = inputs["x"].shape
    out = nc.dram_tensor("out_x", shape, _mybir.dt.float32, kind="ExternalOutput").ap()
    hybrid_trunk(nc, aps, out)
    r = _run(nc, [arrays], core_ids=[0])
    return r.results[0]["out_x"]
```

```python
from contextlib import ExitStack

import concourse.bass as bass
import numpy as np
from concourse import mybir

ALU = mybir.AluOpType
ACT = mybir.ActivationFunctionType
AX = mybir.AxisListType
F32 = mybir.dt.float32

P = 128
HALF = 64


def hybrid_trunk(nc: bass.Bass, t: dict, out: bass.AP):
    L, D, N_IN = t["w_in"].shape
    S = t["x"].shape[1]
    TT = S // P
    KD = D // P
    NE = t["exp_w_gate"].shape[1]
    FF = t["exp_w_gate"].shape[3]
    FB = FF // P
    GW = t["gla_w_alpha"].shape[2]
    RANK = t["gla_w_alpha"].shape[1]
    SW = t["ssd_norm_g"].shape[1]
    SH = t["ssd_D"].shape[1]
    RW = t["rwkv_w0"].shape[1]
    HD = t["gla_norm_g"].shape[1]
    NH = GW // HD
    XBC = t["ssd_conv_w"].shape[2]
    TAPS = t["ssd_conv_w"].shape[1]
    XB = XBC // P
    NG = 4
    EPG = NE // NG
    CH = 64
    NC = S // CH
    ALPHA = float((2 * L) ** 0.25)
    EPS = 1e-5
    GN_EPS = 64e-5
    BCOL = 512
    o_gla, o_z = 0, 4 * GW + RANK
    o_xbc = o_z + SW
    o_dt = o_xbc + XBC
    o_rw = o_dt + SH
    assert o_rw + 4 * RW == N_IN and D == 1024 and S == 256 and HD == CH == HALF

    NSLOT = 4

    def w_in_cols(l, c, n):
        return t["w_in"][l, :, c:c + n].rearrange("(p k) n -> p k n", k=KD)

    def blocks(l):
        b = [("rw0", [(w_in_cols(l, o_rw, BCOL), 0)]),
             ("rw1", [(w_in_cols(l, o_rw + BCOL, BCOL), 0)]),
             ("xbc0", [(w_in_cols(l, o_xbc, BCOL), 0)]),
             ("xbc1", [(w_in_cols(l, o_xbc + BCOL, XBC - BCOL + SH), 0),
                       (w_in_cols(l, 4 * GW, RANK), XBC - BCOL + SH)]),
             ("qk", [(w_in_cols(l, 0, BCOL), 0)]),
             ("vg", [(w_in_cols(l, BCOL, BCOL), 0)]),
             ("z", [(w_in_cols(l, o_z, BCOL), 0)])]
        for h in range(2):
            b.append((f"out{h}", [(t["w_out"][l, :, h * BCOL:(h + 1) * BCOL].rearrange("(b p) n -> p b n", p=P), 0)]))
        for e in range(NE):
            b.append((f"gate{e}", [(t["exp_w_gate"][l, e].rearrange("(p k) f -> p k f", k=KD), 0)]))
            b.append((f"up{e}", [(t["exp_w_up"][l, e].rearrange("(p k) f -> p k f", k=KD), 0)]))
            b.append((f"down{e}", [(t["exp_w_down"][l, e].rearrange("(p b) n -> p b n", b=FB), 0)]))
        return b

    order = [(l, name, parts) for l in range(L) for name, parts in blocks(l)]
    index = {(l, name): n for n, (l, name, _) in enumerate(order)}
    landed, seen = [], [0] * NSLOT
    for n, (_, _, parts) in enumerate(order):
        seen[n % NSLOT] += 16 * len(parts)
        landed.append(seen[n % NSLOT])

    rows, n_rows = {}, 0
    for name, per in (("ssd_conv_w", TAPS * XB), ("ssd_conv_b", XB), ("rwkv_mu", 8), ("rwkv_w0", 2), ("rwkv_a0", 2),
                      ("rwkv_k_k", 2), ("rwkv_k_a", 2), ("rwkv_r_k", 2), ("gla_b_alpha", 2), ("ssd_norm_g", 4),
                      ("gla_norm_g", 1)):
        rows[name] = (n_rows, per)
        n_rows += L * per

    with ExitStack() as ctx:
        def sb(name, shape, dt=F32):
            return ctx.enter_context(nc.sbuf_tensor(name, shape, dt))

        class Signal:

            def __init__(self, name, per=1):
                self.sem, self.per, self.given = ctx.enter_context(nc.semaphore(name)), per, 0

            def __call__(self, l, n=None):
                return self.sem, l * self.per + (self.per if n is None else n)

        class Chain:

            def __init__(self, name):
                self.sem, self.n = ctx.enter_context(nc.semaphore(name)), 0

            def add(self, ins):
                ins.then_inc(self.sem, 1)
                self.n += 1

            def join(self, eng):
                eng.wait_ge(self.sem, self.n)

        bank = [ctx.enter_context(nc.psum_tensor(f"bank{i}", [P, 512], F32)) for i in range(8)]

        ring = sb("ring", [P, NSLOT, KD, BCOL])
        x_tm = sb("x_rows", [P, TT, D])
        x_cm = sb("x_cm", [P, KD, S])
        ident = sb("ident", [P, P])
        ident2 = sb("ident2", [P, HD])
        head_ones = sb("head_ones", [P, P])
        tri_incl = sb("tri_incl", [P, P])
        tri_after = sb("tri_after", [P, P])
        chunk_mask = sb("chunk_mask", [P, 2, P])
        level_mask = sb("level_mask", [P, 6, P])
        level0_tm = sb("level0_tm", [P, P])
        scan_reset = sb("scan_reset", [P, S])
        vec_rows = sb("vec_rows", [P, P])
        vec = sb("vec", [P, n_rows])
        om_mu = sb("om_mu", [P, L * 8])
        om_ka = sb("om_ka", [P, L * 2])
        neg_w0 = sb("neg_w0", [P, L * 2])
        neg_a0 = sb("neg_a0", [P, L * 2])
        lr_w = sb("lr_w", [P, L, RW])
        g2_w = sb("g2_w", [P, L, RW])
        alpha_w = sb("alpha_w", [RANK, L, GW])
        rout_w = sb("rout_w", [P, KD, NE])
        rout_b = sb("rout_b", [P, NE])
        ln_vec = sb("ln_vec", [P, 2, D])
        ssd_small = sb("ssd_small", [P, 3, L, SH])
        unit_gain = sb("unit_gain", [P, 1])
        ln_shift = sb("ln_shift", [P, 1])
        eps_ln = sb("eps_ln", [P, 1])
        eps_gn = sb("eps_gn", [P, 1])
        rms_s = sb("rms_s", [P, TT, 2])
        bn6 = sb("bn6", [P, TT, 2, 6])
        bn2 = sb("bn2", [P, TT, 2])
        rt = sb("rt", [P, 6, TT, NE])
        rg = sb("rg", [P, 4, TT, NG])
        gate = sb("gate", [P, TT, NE])
        tri_before = sb("tri_before", [P, P])
        all_ones = sb("all_ones", [P, P])
        slot_row = sb("slot_row", [P, P])
        pos = sb("pos", [P, TT, NE])
        crowded = sb("crowded", [P, 1], mybir.dt.int32)

        mixers = ExitStack()

        def mx(name, shape):
            return mixers.enter_context(nc.sbuf_tensor(name, shape, F32))

        heads = mx("heads", [P, TT, D])
        gn_vec = mx("gn_vec", [P, 2, RW])
        gla_q = mx("gla_q", [P, 2, S])
        gla_k = mx("gla_k", [P, 2, S])
        gla_kt = mx("gla_kt", [P, TT, GW])
        gla_vg = mx("gla_vg", [P, TT, 2 * GW])
        z_tm = mx("z_rows", [P, TT, SW])
        xbc = mx("xbc", [P, XB, S])
        alr = mx("alr", [RANK, S])
        dt = mx("dt", [P, TT, SH])
        da = mx("da", [P, TT, SH])
        dte = mx("dte", [P, 4, SH])
        big = mx("big", [P, 16 * S])
        rwc = big[:, 0:8 * S].rearrange("p (b s) -> p b s", b=8)
        fac = [big[:, (8 + 2 * i) * S:(10 + 2 * i) * S].rearrange("p (b s) -> p b s", b=2) for i in range(4)]
        gmat = big[:].rearrange("p (t h x y s) -> p t h x y s", t=TT, h=NH, x=2, y=2)
        sc = [mx(f"sc{i}", [P, 2, S]) for i in range(4)]
        tmq = mx("tmq", [P, TT, 3, RW])
        a_w1 = mx("a_w1", [P, TT, NH, 2, HD])
        b_cm = mx("b_cm", [P, 2, S])
        k_cm = mx("k_cm", [P, 2, S])
        ar_cm = mx("ar_cm", [P, 2, 2, S])
        anchor = mx("anchor", [P, 2, 3, NC])
        anchor_g = mx("anchor_g", [P, 2, 3, NC])
        inv = mx("inv", [P, TT, NH, P])
        inv_t = mx("inv_t", [P, TT, NH, P])
        lvl = mx("lvl", [P, TT, NH, P])
        tm_t = mx("tm_t", [P, 2, 2, HD])
        g_tm = mx("g_rows", [P, TT, RW])
        st_rw = mx("st_rw", [P, 2, NC, HD])
        st_gla = mx("st_gla", [P, 2, NC, HD])
        st_ssd = mx("st_ssd", [P, 4 * HD])
        bonus = mx("bonus", [P, TT, NH])
        g_silu = mx("g_silu", [P, TT, GW])
        b_tm = mx("b_tm", [P, P])
        gn = mx("gn", [P, 2, TT, NH])
        rms = mx("rms", [P, TT, NH])
        mixers.close()

        F32R = mybir.dt.float32r
        w_hi = [sb(f"w_hi{i}", [P, 4, BCOL], F32R) for i in range(3)]
        w_lo = [sb(f"w_lo{i}", [P, 4, BCOL], F32R) for i in range(3)]
        x_hi = sb("x_hi", [P, TT, D], F32R)
        x_lo = sb("x_lo", [P, TT, D], F32R)
        xg_hi = sb("xg_hi", [P, KD, P], F32R)
        xg_lo = sb("xg_lo", [P, KD, P], F32R)
        y_hi = sb("y_hi", [P, D], F32R)
        y_lo = sb("y_lo", [P, D], F32R)
        pick = [sb(f"pick{i}", [P, TT, P], F32R) for i in range(2)]
        pick_t = sb("pick_t", [P, S], F32R)
        act_g = sb("act_g", [P, BCOL])
        he = sb("he", [P, BCOL])
        he_t = sb("he_t", [P, FB, P])
        g_slot = sb("g_slot", [P, 1])

        slot_full = [ctx.enter_context(nc.semaphore(f"slot_full{i}")) for i in range(NSLOT)]
        x_loaded = ctx.enter_context(nc.semaphore("x_loaded"))
        rows_loaded = ctx.enter_context(nc.semaphore("rows_loaded"))
        small_loaded = ctx.enter_context(nc.semaphore("small_loaded"))
        ln_loaded = Signal("ln_loaded", 2 * 32)
        gn_loaded = Signal("gn_loaded", 32)
        stored = ctx.enter_context(nc.semaphore("stored"))
        masks_done = ctx.enter_context(nc.semaphore("masks_done"))
        s_small = ctx.enter_context(nc.semaphore("s_small"))
        rows_zero = ctx.enter_context(nc.semaphore("rows_zero"))
        pool_step = ctx.enter_context(nc.semaphore("pool_step"))
        vec_turned = ctx.enter_context(nc.semaphore("vec_turned"))
        vec_ready = ctx.enter_context(nc.semaphore("vec_ready"))
        SIG = {}
        STEPS = dict(t_gather=1, t_gslot=1, t_use=4, t_he=1, t_down=1, t_scat=1,
                     v_pick=1, v_gslot=1, v_wlo=4, v_he=1, v_xglo=1, v_ylo=1,
                     s_whi=4, s_silu=1, s_xghi=1, s_het=2, s_yhi=1)
        for name, per in dict(
                t_x=4, t_x1=4, t_proj=14, t_lowrank=4, t_turned=5, t_pair=8, t_ltm=2, t_mv=2, t_lp=10, t_inv=10, t_xa=2,
                t_q=1, t_carry=1, t_srw=3, t_yrw=1, t_glaz=1, t_ssd_tm=3, t_edge=1, t_cb=1, t_seg=4, t_yssd=3,
                t_sssd=1, t_gkt=1, t_gsc=2, t_sgla=1, t_ygla=1, t_cat=4, t_mix=4, t_route=1, t_slots=1,
                v_proj=8, v_gates=2, v_ssmax=1, v_decay=1, v_ratio=1, v_bonus=1, v_kcm=1, v_bcm=1, v_rcm=1,
                v_pair=8, v_inv0=2, v_lvl=10, v_inv=10, v_q=1, v_carry=1, v_srw=3, v_gz=1, v_gcum=1, v_gqk=1,
                v_xbc=3, v_dt=1, v_da=1, v_lhs=4, v_w=4, v_xdt=2, v_xw=1, v_sssd=1, v_yssd=2,
                v_gsc=2, v_sgla=3, v_gnvar=1, v_glasum=1, v_heads=3, v_var=4, v_x1=1, v_logit=1,
 v_sel=1, v_flag=1, v_xlo=1, v_x2=1, v_cat=4,
                s_x=4, s_x1=4, s_route=1, s_mu=4, s_conv=3, s_low=2, s_sq=1, s_ez=1, s_ea=1, s_g=1, s_norm=1, s_e=3, s_turned=5,
                s_mv=2, s_lp=10, s_xa=2, s_qk=2, s_vg=2, s_z=2, s_gln=1, s_ge=1, s_silx=3, s_dtl=1, s_seg=4,
                s_edge=1, s_xs=3, s_rssd=2, s_gnr=1, s_rgla=1, s_cat=4, s_rstd=4, s_xhi=1, s_expl=1,
                s_silg=1, s_silz=2).items():
            SIG[name] = Signal(name, per)
        for name, per in STEPS.items():
            SIG[name] = Signal(name, per * 2 * NE)

        def done(name, l, n=None):
            assert n is None or 1 <= n <= SIG[name].per
            return SIG[name](l, n)

        def inc(ins, name, by=1):
            SIG[name].given += by
            return ins.then_inc(SIG[name].sem, by)

        def last_use(l, name):
            kind = name.rstrip("0123456789")
            e = int(name[len(kind):] or 0)
            n = {"rw": 2 * e + 2, "xbc": 2 * e + 6, "qk": 10, "vg": 12, "z": 14, "out": 2 * e + 2,
                 "gate": 8 * e + 6, "up": 8 * e + 8, "down": 2 * e + 2}[kind]
            return {"out": "t_mix", "gate": "v_wlo", "up": "v_wlo", "down": "t_down"}.get(kind, "t_proj"), l, n

        def vcol(name, l, b):
            at, per = rows[name]
            return vec[:, at + l * per + b:at + l * per + b + 1]

        def halves(h):
            return slice(HALF * (h % 2), HALF * (h % 2) + HALF), h // 2

        def tile_(j):
            return slice(P * j, P * j + P)

        def each(ap, n):
            return ap.unsqueeze(1).to_broadcast([P, n, ap.shape[-1]])

        def wide(ap, n):
            return ap.unsqueeze(2).to_broadcast([P, ap.shape[1], n])

        V, A, T, G = nc.vector, nc.scalar, nc.tensor, nc.gpsimd
        block = ctx.enter_context(nc.Block())

        CROWD = P + 0.5
        b_gate, b_up, b_y = bank[4], bank[5], (bank[6], bank[7])

        def two_ways(eng, l, emit):
            eng.wait_ge(*done("v_flag", l))
            flag = eng.value_load(crowded[0:1, 0:1], min_val=0, max_val=1)
            for rounds, value in ((1, 0), (2, 1)):
                with eng.If(flag == value):
                    emit(rounds)

        def experts_t(pe, weights, l, rounds):
            N = NE * rounds

            def at(name, n):
                return done(name, l, n * 2 // rounds)

            def gather(n):
                if n >= 2:
                    pe.wait_ge(*at("s_yhi", n - 1))
                    pe.wait_ge(*at("v_ylo", n - 1))
                pe.wait_ge(*at("v_pick", n + 1))
                for k in range(KD):
                    o = b_y[k // 4][:, (k % 4) * P:(k % 4) * P + P]
                    for j in range(TT):
                        for x in (x_hi, x_lo):
                            m = T.matmul(o, x[:, j, k::KD], pick[n % 2][:, j, :], start=(j == 0 and x is x_hi),
                                         stop=(j == TT - 1 and x is x_lo))
                inc(m, "t_gather", 2 // rounds)

            def scatter(n):
                pe.wait_ge(*at("s_het", 2 * n + 2))
                pe.wait_ge(*at("s_yhi", n + 1))
                pe.wait_ge(*at("v_ylo", n + 1))
                for j in range(TT):
                    for hf in range(2):
                        for y in (y_hi, y_lo):
                            m = T.matmul(bank[2 * j + hf][:], pick_t[:, tile_(j)], y[:, hf * 512:hf * 512 + 512],
                                         start=(n == 0 and y is y_hi), stop=(n == N - 1 and y is y_lo))
                inc(m, "t_scat", 2 // rounds)

            pe.wait_ge(*done("s_xhi", l))
            pe.wait_ge(*done("v_xlo", l))
            gather(0)
            for n in range(N):
                e = n // rounds
                pe.wait_ge(*at("s_het", 2 * n)) if n else None
                for j in range(TT):
                    m = T.matmul(b_up[:, 0:1], pick[n % 2][:, j, :].bitcast(F32), gate[:, j, e:e + 1], start=(j == 0),
                                 stop=(j == TT - 1))
                inc(m, "t_gslot", 2 // rounds)
                pe.wait_ge(*at("s_xghi", n + 1))
                pe.wait_ge(*at("v_xglo", n + 1))
                for q in range(4):
                    if q == 2:
                        pe.wait_ge(*at("v_gslot", n + 1))
                    pe.wait_ge(*at("s_whi", 4 * n + q + 1))
                    pe.wait_ge(*at("v_wlo", 4 * n + q + 1))
                    i = (4 * n + q) % 3
                    for k in range(4):
                        kk = 4 * (q % 2) + k
                        for t3, (x, w) in enumerate(((xg_hi, w_hi[i]), (xg_hi, w_lo[i]), (xg_lo, w_hi[i]))):
                            m = T.matmul((b_gate, b_up)[q // 2][:], x[:, kk, :], w[:, k, :], start=(kk == 0 and t3 == 0),
                                         stop=(kk == KD - 1 and t3 == 2))
                    inc(m, "t_use", 2 // rounds)
                if n + 1 < N:
                    gather(n + 1)
                if n:
                    scatter(n - 1)
                pe.wait_ge(*at("v_he", n + 1))
                for fb in range(FB):
                    T.transpose(b_gate[:, fb * P:fb * P + P], he[:, fb::FB], ident[:])
                for j in range(TT):
                    m = T.transpose(b_up[:, tile_(j)], pick[n % 2][:, j, :].bitcast(F32), ident[:])
                inc(m, "t_he", 2 // rounds)
                w = weights(l, f"down{e}").rearrange("p a b -> p (a b)").rearrange("p (b n) -> p b n", b=FB)
                pe.wait_ge(*at("s_het", 2 * n + 1))
                if n + 1 < N:
                    pe.wait_ge(*at("s_xghi", n + 2))
                    pe.wait_ge(*at("v_xglo", n + 2))
                for hf in range(2):
                    for fb in range(FB):
                        m = T.matmul(b_y[hf][:], he_t[:, fb, :], w[:, fb, hf * 512:hf * 512 + 512], start=(fb == 0),
                                     stop=(fb == FB - 1))
                inc(m, "t_down", 2 // rounds)
            scatter(N - 1)

        def split_order(N):
            first = [0, 1, 2]
            return first, [[4 * n + 3, 4 * n + 4, 4 * n + 5, 4 * n + 6] for n in range(N)]

        def half_block(l, q, rounds):
            n, i = divmod(q, 4)
            b = index[l, f"{'gate' if i < 2 else 'up'}{n // rounds}"]
            return b, ring[:, b % NSLOT, 4 * (i % 2):4 * (i % 2) + 4, :]

        def experts_s(act, l, rounds):
            N = NE * rounds

            def at(name, n):
                return done(name, l, n * 2 // rounds)

            def w_split(q):
                if q >= 4 * N:
                    return
                if q >= 3:
                    act.wait_ge(*at("t_use", q - 2))
                b, w = half_block(l, q, rounds)
                act.wait_ge(slot_full[b % NSLOT], landed[b])
                inc(A.activation(w_hi[q % 3][:], w, ACT.Copy), "s_whi", 2 // rounds)

            def x_split(n):
                act.wait_ge(*at("t_gather", n + 1))
                for i in range(2):
                    m = A.activation(xg_hi[:, 4 * i:4 * i + 4], b_y[i][:].rearrange("p (k s) -> p k s", k=4), ACT.Copy)
                inc(m, "s_xghi", 2 // rounds)

            first, later = split_order(N)
            x_split(0)
            for q in first:
                w_split(q)
            for n in range(N):
                if n:
                    act.wait_ge(*at("t_down", n))
                    for i in range(2):
                        m = A.activation(y_hi[:, i * 512:i * 512 + 512], b_y[i][:], ACT.Copy)
                    inc(m, "s_yhi", 2 // rounds)
                for q in later[n][:3]:
                    w_split(q)
                act.wait_ge(*at("t_use", 4 * n + 4))
                inc(A.activation(act_g[:], b_gate[:], ACT.Silu), "s_silu", 2 // rounds)
                if n + 1 < N:
                    x_split(n + 1)
                act.wait_ge(*at("t_he", n + 1))
                inc(A.activation(he_t[:], b_gate[:].rearrange("p (b s) -> p b s", b=FB), ACT.Copy), "s_het", 2 // rounds)
                inc(A.activation(pick_t[:], b_up[:, 0:S], ACT.Copy), "s_het", 2 // rounds)
                w_split(later[n][3])
            act.wait_ge(*at("t_down", N))
            for i in range(2):
                m = A.activation(y_hi[:, i * 512:i * 512 + 512], b_y[i][:], ACT.Copy)
            inc(m, "s_yhi", 2 // rounds)

        def experts_v(dve, l, rounds):
            N = NE * rounds

            def at(name, n):
                return done(name, l, n * 2 // rounds)

            def w_split(q):
                if q >= 4 * N:
                    return
                b, w = half_block(l, q, rounds)
                dve.wait_ge(*at("s_whi", q + 1))
                inc(V.tensor_tensor(w_lo[q % 3][:], w, w_hi[q % 3][:].bitcast(F32), ALU.subtract), "v_wlo", 2 // rounds)

            def x_split(n):
                dve.wait_ge(*at("s_xghi", n + 1))
                for i in range(2):
                    m = V.tensor_tensor(xg_lo[:, 4 * i:4 * i + 4], b_y[i][:].rearrange("p (k s) -> p k s", k=4),
                                        xg_hi[:, 4 * i:4 * i + 4].bitcast(F32), ALU.subtract)
                inc(m, "v_xglo", 2 // rounds)

            def y_split(n):
                dve.wait_ge(*at("s_yhi", n + 1))
                for i in range(2):
                    cs = slice(i * 512, i * 512 + 512)
                    m = V.tensor_tensor(y_lo[:, cs], b_y[i][:], y_hi[:, cs].bitcast(F32), ALU.subtract)
                inc(m, "v_ylo", 2 // rounds)

            def picks(n):
                if n >= N:
                    return
                if n >= 2:
                    dve.wait_ge(*at("t_he", n - 1))
                e, r = divmod(n, rounds)
                for j in range(TT):
                    m = V.tensor_scalar(pick[n % 2][:, j, :], slot_row[:], float(P * r), pos[:, j, e:e + 1], ALU.add,
                                        ALU.is_equal)
                inc(m, "v_pick", 2 // rounds)

            first, later = split_order(N)
            picks(0)
            picks(1)
            x_split(0)
            for q in first:
                w_split(q)
            for n in range(N):
                if n:
                    y_split(n - 1)
                dve.wait_ge(*at("t_gslot", n + 1))
                inc(V.tensor_copy(g_slot[:], b_up[:, 0:1]), "v_gslot", 2 // rounds)
                for q in later[n][:3]:
                    w_split(q)
                dve.wait_ge(*at("s_silu", n + 1))
                dve.wait_ge(*at("v_gslot", n + 1))
                inc(V.scalar_tensor_tensor(out=he[:], in0=act_g[:], scalar=g_slot[:, 0:1], in1=b_up[:], op0=ALU.mult,
                                           op1=ALU.mult), "v_he", 2 // rounds)
                if n + 1 < N:
                    x_split(n + 1)
                picks(n + 2)
                w_split(later[n][3])
            y_split(N - 1)


        def seg_in(q, i):
            return sc[q][:].rearrange("p b s -> p (b s)")[:, tile_(i)]

        def seg_w4(q):
            return (lvl, inv)[q // 2][:, q % 2]

        def seg_w(q, i):
            return seg_w4(q)[:, i, :]

        def xdt(j):
            return inv_t[:, j].rearrange("p h s -> p (h s)")

        xw = b_cm[:].rearrange("p b s -> p (b s)")

        def gsc4(j):
            return sc[j][:].rearrange("p b s -> p (b s)").rearrange("p (h s) -> p h s", h=NH)

        def gsc(j, h):
            return gsc4(j)[:, h, :]

        def cat_gain(l, b):
            return vcol("gla_norm_g", l, 0) if b < 2 else vcol("ssd_norm_g", l, b - 2) if b < 6 else unit_gain[:]
        @block.sync
        def _(sp):
            for j in range(TT):
                sp.dma_start(x_tm[:, j, :], t["x"][0, tile_(j), :]).then_inc(x_loaded, 16)
            sp.wait_ge(rows_zero, 1)
            for name, (at, per) in rows.items():
                src = t[name]
                if name == "gla_norm_g":
                    for h in range(2):
                        sp.dma_start(vec_rows[at:at + L, h * HD:(h + 1) * HD], src).then_inc(rows_loaded, 16)
                    continue
                if name == "ssd_conv_w":
                    flat = src.rearrange("l k (b p) -> (l k b) p", p=P)
                elif name == "rwkv_r_k":
                    flat = src.rearrange("l (b h) n -> (l b) (h n)", h=2)
                else:
                    flat = src.rearrange("l (b p) -> (l b) p", p=P)
                sp.dma_start(vec_rows[at:at + L * per, :], flat).then_inc(rows_loaded, 16)
            for n, (l, name, parts) in enumerate(order):
                if n >= NSLOT:
                    sp.wait_ge(*done(*last_use(*order[n - NSLOT][:2])))
                for src, c in parts:
                    rows_n, cols = src.shape[1], src.shape[2]
                    dst = ring[:, n % NSLOT].rearrange("p k n -> p (k n)").rearrange("p (k n) -> p k n", k=rows_n)
                    sp.dma_start(dst[:, :, c:c + cols], src).then_inc(slot_full[n % NSLOT], 16)
            sp.wait_ge(*done("v_x2", L - 1))
            for j in range(TT):
                sp.dma_start(out[0, tile_(j), :], x_tm[:, j, :]).then_inc(stored, 16)
            sp.wait_ge(stored, 16 * TT)

        @block.gpsimd
        def _(pool):
            n = 0

            def step(ins):
                nonlocal n
                ins.then_inc(pool_step, 1)
                n += 1
                pool.wait_ge(pool_step, n)

            def keep(ap, base, pattern, mult, op=ALU.is_ge):
                step(G.affine_select(out=ap, in_=ap, compare_op=op, fill=0.0, base=base, pattern=pattern,
                                     channel_multiplier=mult))

            G.memset(vec_rows[:], 0.0).then_inc(rows_zero, 1)
            small = [(lr_w[0:HALF], t["rwkv_w2"].rearrange("l r c -> r l c")),
                     (lr_w[HALF:P], t["rwkv_a2"].rearrange("l r c -> r l c")),
                     (g2_w[:], t["rwkv_g2"].rearrange("l r c -> r l c")),
                     (alpha_w[:], t["gla_w_alpha"].rearrange("l r c -> r l c")),
                     (rout_w[:], t["router_w"].rearrange("(p k) e -> p k e", k=KD)),
                     (rout_b[:], t["router_b"].partition_broadcast(P))]
            for i, name in enumerate(("ssd_dt_bias", "ssd_A_log", "ssd_D")):
                for l in range(L):
                    small.append((ssd_small[:, i, l, :], t[name][l].partition_broadcast(P)))
            for dst, src in small:
                pool.dma_start(dst, src).then_inc(small_loaded, 16)
            n_small = len(small)

            for m in (ident, ident2, head_ones, tri_incl, tri_after, tri_before, all_ones, chunk_mask, level_mask, level0_tm, scan_reset):
                one = 0.0 if m is level_mask else 1.0
                step(G.memset(m[:], one))
            keep(ident[:], 0, [[-1, P]], 1)
            keep(ident[:], 0, [[1, P]], -1)
            for h in range(2):
                keep(ident2[HALF * h:HALF * h + HALF, :], 0, [[-1, HD]], 1)
                keep(ident2[HALF * h:HALF * h + HALF, :], 0, [[1, HD]], -1)
            halves2 = head_ones[:].rearrange("p (b c) -> p b c", b=2)
            keep(halves2, 0, [[-HALF, 2], [0, HALF]], 1)
            keep(halves2, HALF - 1, [[HALF, 2], [0, HALF]], -1)
            keep(tri_incl[:], 0, [[1, P]], -1)
            keep(tri_after[:], -1, [[-1, P]], 1)
            keep(tri_before[:], -1, [[1, P]], -1)
            step(G.iota(slot_row[:], [[1, P]], base=0, channel_multiplier=0, allow_small_or_imprecise_dtypes=True))
            for i in range(2):
                m = chunk_mask[:, i, :].rearrange("p (b c) -> p b c", b=2)
                keep(m, 0, [[-CH, 2], [0, CH]], 1)
                keep(m, i - 1, [[CH, 2], [1, CH]], -1)
            for j in range(6):
                m, nb = 2 ** j, P // 2 ** (j + 1)
                v = level_mask[:, j, :].rearrange("p (b h i) -> p b h i", h=2, i=m)[:, :, 1, :]
                step(G.memset(v, 1.0))
                keep(v, 0, [[-2 * m, nb], [0, m]], 1)
                keep(v, m - 1, [[2 * m, nb], [0, m]], -1)
            v = level0_tm[:].rearrange("p (b h) -> p b h", h=2)
            step(G.memset(v[:, :, 1], 0.0))
            keep(v[:, :, 0], -1, [[-2, P // 2]], 1)
            keep(v[:, :, 0], 1, [[2, P // 2]], -1)
            step(G.memset(scan_reset[:].rearrange("p (c i) -> p c i", i=CH)[:, :, 0], 0.0))
            for ap, value in ((ln_shift, 15 * float(np.log(2.0))), (eps_ln, EPS), (eps_gn, GN_EPS)):
                step(G.memset(ap[:], value))
            G.memset(unit_gain[:], 1.0).then_inc(masks_done, 1)
            for l in range(L):
                if l:
                    pool.wait_ge(*done("v_x2", l - 1))
                for which in range(2):
                    if which:
                        pool.wait_ge(*done("v_x1", l))
                    for i, name in enumerate(("ln1_g", "ln1_b") if which == 0 else ("ln2_g", "ln2_b")):
                        pool.dma_start(ln_vec[:, i, :], t[name][l].partition_broadcast(P)).then_inc(ln_loaded.sem, 16)
                    if which == 0:
                        for i, name in enumerate(("rwkv_ln_g", "rwkv_ln_b")):
                            pool.dma_start(gn_vec[:, i, :], t[name][l].partition_broadcast(P)) \
                                .then_inc(gn_loaded.sem, 16)

        @block.tensor
        def _(pe):
            def weights(l, name):
                n = index[l, name]
                pe.wait_ge(slot_full[n % NSLOT], landed[n])
                return ring[:, n % NSLOT]

            rows_chain = Chain("t_rows")

            def rows_done(m):
                rows_chain.add(m)
                rows_chain.join(pe)

            def turn_x(l):
                for i in range(4):
                    for k in (2 * i, 2 * i + 1):
                        for j in range(TT):
                            m = T.transpose(bank[i][:, (k % 2) * S + P * j:(k % 2) * S + P * j + P],
                                            x_tm[:, j, k::KD], ident[:])
                    inc(m, "t_x")

            def project(l, i):
                if i < 2:
                    pass
                elif i - 2 < 8:
                    pe.wait_ge(*done("v_proj", l, i - 1))
                else:
                    pe.wait_ge(*done(("s_qk", "s_qk", "s_vg", "s_vg")[i - 10], l, (i - 10) % 2 + 1))
                dst = bank[i % 2]
                name = ("rw0", "rw0", "rw1", "rw1", "xbc0", "xbc0", "xbc1", "xbc1", "qk", "qk", "vg", "vg", "z", "z")[i]
                w = weights(l, name)

                def cm(out_, c, n):
                    for k in range(KD):
                        m = T.matmul(out_, w[:, k, c:c + n], x_cm[:, k, :], start=(k == 0), stop=(k == KD - 1))
                    return m

                def tm(out_, j, c, n):
                    for k in range(KD):
                        m = T.matmul(out_, x_cm[:, k, tile_(j)], w[:, k, c:c + n], start=(k == 0), stop=(k == KD - 1))
                    return m

                if i == 7:
                    c = XBC - BCOL
                    cm(dst[0:RANK, 0:S], c + SH, RANK)
                    for j in range(TT):
                        m = tm(dst[:, S + SH * j:S + SH * j + SH], j, c, SH)
                elif i < 10:
                    for b in range(2):
                        m = cm(dst[:, b * S:b * S + S], (2 * (i % 2) + b) * P if i != 6 else b * P, P)
                else:
                    m = tm(dst[:], i % 2, 0, BCOL)
                inc(m, "t_proj")

            for l in range(L):
                def proj(i):
                    project(l, i)

                if l == 0:
                    pe.wait_ge(x_loaded, 16 * TT)
                    pe.wait_ge(masks_done, 1)
                    turn_x(0)
                    pe.wait_ge(rows_loaded, 16 * (len(rows) + 1))
                    T.transpose(bank[4][:, 0:P], vec_rows[:], ident[:]).then_inc(vec_turned, 1)
                    pe.wait_ge(small_loaded, 16 * (6 + 3 * L))
                pe.wait_ge(*done("s_x", l))
                for i in range(4):
                    proj(i)
                proj(4)
                pe.wait_ge(*done("v_gates", l, 1))
                for b in range(2):
                    m = T.matmul(bank[2][:, b * S:b * S + S], lr_w[0:HALF, l, b * P:b * P + P],
                                 fac[3][0:HALF, 0, :], start=True, stop=True)
                inc(m, "t_lowrank")
                for b in range(2):
                    m = T.matmul(bank[3][:, b * S:b * S + S], lr_w[HALF:P, l, b * P:b * P + P],
                                 rwc[HALF:P, 6, :], start=True, stop=True)
                inc(m, "t_lowrank")
                pe.wait_ge(*done("v_gates", l, 2))
                for j in range(TT):
                    m = T.matmul(bank[4][:, j * RW:j * RW + RW], fac[3][:, 1, tile_(j)], g2_w[:, l, :],
                                 start=True, stop=True)
                inc(m, "t_lowrank")
                pe.wait_ge(*done("s_sq", l))
                inc(T.matmul(bank[5][:], head_ones[:], fac[2], start=True, stop=True), "t_lowrank")
                for i in (5, 6, 7):
                    proj(i)
                pe.wait_ge(*done("v_ssmax", l))
                pe.wait_ge(*done("v_proj", l, 8))
                for b in range(2):
                    m = T.matmul(bank[5][:, b * S:b * S + S], alpha_w[:, l, b * P:b * P + P], alr[:],
                                 start=True, stop=True)
                inc(m, "t_glaz")
                proj(8)
                for j in range(TT):
                    for b in range(2):
                        m = T.transpose(bank[6][:, j * RW + b * P:j * RW + b * P + P], rwc[:, 4 + b, tile_(j)], ident[:])
                inc(m, "t_turned")
                pe.wait_ge(*done("v_bonus", l))
                pe.wait_ge(*done("s_g", l))
                for j in range(TT):
                    for b in range(2):
                        m = T.matmul(bank[4][:, j * NH + 2 * b:j * NH + 2 * b + 2], fac[0][:, b, tile_(j)],
                                     head_ones[:, 0:P:HALF], start=True, stop=True)
                inc(m, "t_turned")
                for src, dst, ready in ((ar_cm[:, :, 0, :], bank[7], "v_ratio"), (k_cm, bank[3], "v_kcm"),
                                        (b_cm, bank[2], "v_bcm")):
                    pe.wait_ge(*done(ready, l))
                    for j in range(TT):
                        for b in range(2):
                            m = T.transpose(dst[:, j * RW + b * P:j * RW + b * P + P], src[:, b, tile_(j)], ident[:])
                    inc(m, "t_turned")
                proj(9)
                pe.wait_ge(*done("v_rcm", l))
                for u in range(TT * NH):
                    j, h = divmod(u, NH)
                    ps, b = halves(h)
                    if u < 2:
                        pe.wait_ge(*done("s_turned", l, 3))
                    else:
                        pe.wait_ge(*done("v_pair", l, u - 1))
                    for i, src in enumerate((b_cm, k_cm)):
                        m = T.matmul(bank[6 + u % 2][:, 2 * P * i:2 * P * i + 2 * P], src[ps, b, tile_(j)],
                                     ar_cm[ps, b, :, tile_(j)], start=True, stop=True)
                    inc(m, "t_pair")
                pe.wait_ge(*done("s_turned", l, 5))
                for par in range(2):
                    for j in range(TT):
                        for h in (par, par + 2):
                            ps, b = halves(h)
                            m = T.matmul(bank[2 + j][:, tile_(h)], ar_cm[ps, b, 0, tile_(j)], b_cm[ps, b, tile_(j)],
                                         start=True, stop=True)
                        if par:
                            inc(m, "t_ltm")
                    if not par:
                        rows_done(m)
                for j in range(TT):
                    pe.wait_ge(*done("v_pair", l, NH * (j + 1)))
                    for h in range(NH):
                        m = T.matmul(bank[4][:, j * RW + h * HD:j * RW + h * HD + HD], gmat[:, j, h, 1, 0, :],
                                     tmq[:, j, 2, h * HD:h * HD + HD], start=True, stop=True)
                    inc(m, "t_mv")
                for lev in range(5):
                    for j in range(TT):
                        n = lev * TT + j
                        pe.wait_ge(*done("v_lvl", l, n + 1))
                        if lev == 0:
                            pe.wait_ge(*done("v_inv0", l, j + 1))
                        else:
                            pe.wait_ge(*done("v_inv", l, n - 1))
                        for h in range(NH):
                            m = T.matmul(bank[2 + j][:, tile_(h)], lvl[:, j, h, :], inv[:, j, h, :], start=True, stop=True)
                        inc(m, "t_lp")
                    if lev < 4:
                        proj(10 + lev)
                    for j in range(TT):
                        n = lev * TT + j
                        pe.wait_ge(*done("s_lp", l, n + 1))
                        if lev == 0:
                            pe.wait_ge(*done("s_mv", l, j + 1))
                            pe.wait_ge(*done("v_gz", l))
                        for h in range(NH):
                            m = T.matmul(bank[4 + j][:, tile_(h)], lvl[:, j, h, :], inv_t[:, j, h, :], start=True, stop=True)
                        if lev < 4:
                            for h in range(NH):
                                m = T.matmul(bank[6 + j][:, tile_(h)], inv_t[:, j, h, :], lvl[:, j, h, :],
                                             start=True, stop=True)
                        inc(m, "t_inv")
                for j in range(TT):
                    pe.wait_ge(*done("v_inv", l, 9 + j))
                    for h in range(NH):
                        m = T.matmul(bank[2 + j][:, tile_(h)], inv_t[:, j, h, :],
                                     a_w1[:, j, h].rearrange("p a b -> p (a b)"), start=True, stop=True)
                    inc(m, "t_xa")
                pe.wait_ge(*done("s_xa", l))
                for h in range(NH):
                    ps, b = halves(h)
                    for j in range(TT):
                        m = T.matmul(bank[4][ps, (j * 2 + b) * P:(j * 2 + b) * P + P], a_w1[:, j, h, 0, :],
                                     gmat[:, j, h, 0, 1, :], start=True, stop=True)
                inc(m, "t_q")
                for c in (1, 2):
                    pc, j = halves(c)
                    for h in range(NH):
                        ps, b = halves(h)
                        m = T.matmul(bank[6][ps, (b * 2 + c - 1) * HD:(b * 2 + c) * HD], a_w1[pc, j, h, 0, :],
                                     tmq[pc, j, 0, h * HD:h * HD + HD], start=True, stop=True)
                    if c == 1:
                        rows_done(m)
                inc(m, "t_carry")
                for j in range(TT):
                    for h in range(NH):
                        o = bank[5][:, j * RW + h * HD:j * RW + h * HD + HD]
                        T.matmul(o, gmat[:, j, h, 0, 1, :], a_w1[:, j, h, 1, :], start=(j == 0 and h == 0), stop=False,
                                 skip_group_check=True)
                        T.matmul(o, gmat[:, j, h, 1, 1, :], tmq[:, j, 2, h * HD:h * HD + HD], start=False, stop=False,
                                 skip_group_check=True)
                def carried(c, h):
                    ps, b = halves(h)
                    return bank[7][ps, (c * 2 + b) * HD:(c * 2 + b) * HD + HD]

                for c in (0, 2, 1):
                    pc, j = halves(c)
                    for h in range(NH):
                        hs = slice(h * HD, h * HD + HD)
                        T.matmul(carried(c, h), tmq[pc, j, 0, hs], a_w1[pc, j, h, 1, :], start=(c == 0 and h < 2), stop=False,
                                 skip_group_check=True)
                        m = T.matmul(carried(c, h), tmq[pc, j, 1, hs], tmq[pc, j, 2, hs], start=False, stop=(c == 0),
                                     skip_group_check=True)
                    if c == 1:
                        inc(m, "t_srw")
                    else:
                        rows_done(m)
                pe.wait_ge(*done("v_carry", l))
                for c in (1, 2):
                    pe.wait_ge(*done("v_srw", l, c))
                    for par in range(2):
                        for h in (par, par + 2):
                            ps, b = halves(h)
                            m = T.matmul(carried(c, h), tm_t[ps, b, c - 1, :], st_rw[ps, b, c, :], start=False, stop=True,
                                         skip_group_check=True)
                        if not par:
                            rows_done(m)
                    inc(m, "t_srw")
                pe.wait_ge(*done("v_q", l))
                pe.wait_ge(*done("v_srw", l))

                def from_state(q, st, name):
                    for par in range(2):
                        for c in range(1, NC):
                            pc, j = halves(c)
                            for h in (par, par + 2):
                                ps, b = halves(h)
                                m = T.matmul(bank[5][pc, j * RW + h * HD:j * RW + h * HD + HD],
                                             q[ps, b, c * CH:c * CH + CH], st[ps, b, c, :], start=False,
                                             stop=(c == NC - 1), skip_group_check=True)
                        if not par:
                            rows_done(m)
                    inc(m, name)

                from_state(ar_cm[:, :, 1, :], st_rw, "t_yrw")

                pe.wait_ge(*done("s_z", l))
                pe.wait_ge(*done("v_xbc", l))
                for j in range(TT):
                    for b in range(4):
                        m = T.transpose(bank[j][:, tile_(b)], xbc[:, b, tile_(j)], ident[:])
                    inc(m, "t_ssd_tm")
                inc(T.transpose(bank[2][:, 0:P], xbc[:, 4, tile_(0)], ident[:]), "t_ssd_tm")
                pe.wait_ge(*done("v_da", l))
                T.matmul(bank[2][:, 2 * P:2 * P + SH], tri_after[:], da[:, 0, :], start=True, stop=True)
                inc(T.matmul(bank[2][:, 2 * P + SH:2 * P + 2 * SH], tri_incl[:], da[:, 1, :], start=True, stop=True), "t_edge")
                for g in range(2):
                    ps = slice(HALF * g, HALF * g + HALF)
                    for j in range(TT):
                        m = T.matmul(bank[3][:, (j * 2 + g) * P:(j * 2 + g) * P + P], xbc[ps, 4, tile_(j)],
                                     xbc[ps, 5, tile_(j)], start=True, stop=True)
                    if g == 0:
                        rows_done(m)
                inc(m, "t_cb")
                for q in range(4):
                    pe.wait_ge(*done("v_lhs", l, q + 1))
                    if q == 3:
                        pe.wait_ge(*done("s_seg", l, 1))
                    dst = bank[(4, 6, 7, 4)[q]]
                    for i in range(4):
                        m = T.matmul(dst[:, tile_(i)], seg_in(q, i), tri_incl[:], start=True, stop=True)
                    inc(m, "t_seg")
                for j in range(TT):
                    pe.wait_ge(*done("v_w", l, 2 * j + 2))
                    pe.wait_ge(*done("s_xs", l, j + 1))
                    pe.wait_ge(*done("v_xdt", l, j + 1))
                    for h in range(SH):
                        m = T.matmul(bank[j][:, h * HD:h * HD + HD], seg_w(2 * j + h // 4, h % 4),
                                     xdt(j)[:, h * HD:h * HD + HD], start=True, stop=True)
                    inc(m, "t_yssd")
                pe.wait_ge(*done("v_xw", l))
                pe.wait_ge(*done("s_xs", l, 3))
                pe.wait_ge(*done("s_edge", l))
                for g in range(2):
                    ps = slice(HALF * g, HALF * g + HALF)
                    m = T.matmul(bank[2][ps, 0:4 * HD], b_tm[:, ps], xw[:, 4 * HD * g:4 * HD * g + 4 * HD],
                                 start=True, stop=True)
                inc(m, "t_sssd")
                pe.wait_ge(*done("v_sssd", l))
                pe.wait_ge(*done("s_seg", l, 2))
                for g in range(2):
                    ps = slice(HALF * g, HALF * g + HALF)
                    m = T.matmul(bank[6][:, 4 * HD * g:4 * HD * g + 4 * HD], xbc[ps, 5, tile_(1)], st_ssd[ps, :],
                                 start=True, stop=True)
                    if g == 0:
                        rows_done(m)
                inc(m, "t_yssd")

                pe.wait_ge(*done("v_gqk", l))
                pe.wait_ge(*done("v_w", l))
                for j in range(TT):
                    for b in range(2):
                        m = T.transpose(bank[3][:, j * GW + b * P:j * GW + b * P + P], gla_k[:, b, tile_(j)], ident[:])
                inc(m, "t_gkt")
                pe.wait_ge(*done("s_seg", l))
                for par in range(2):
                    for j in range(TT):
                        for h in (par, par + 2):
                            ps, b = halves(h)
                            m = T.matmul(bank[(4, 7)[j]][:, tile_(h)], gla_k[ps, b, tile_(j)], gla_q[ps, b, tile_(j)],
                                         start=True, stop=True)
                        if par:
                            inc(m, "t_gsc")
                    if not par:
                        rows_done(m)
                pe.wait_ge(*done("s_gln", l))
                for c in range(NC - 1):
                    pc, j = halves(c)
                    for h in range(NH):
                        ps, b = halves(h)
                        hs = slice(h * HD, h * HD + HD)
                        m = T.matmul(bank[2][ps, (c * 2 + b) * HD:(c * 2 + b) * HD + HD], gla_kt[pc, j, hs],
                                     gla_vg[pc, j, hs], start=True, stop=True)
                    if c < NC - 2:
                        rows_done(m)
                inc(m, "t_sgla")
                pe.wait_ge(*done("v_heads", l, 1))
                for j in range(TT):
                    pe.wait_ge(*done("v_gsc", l, j + 1))
                    for h in range(NH):
                        hs = slice(h * HD, h * HD + HD)
                        T.matmul(bank[5][:, j * GW + h * HD:j * GW + h * HD + HD], gsc(j, h), gla_vg[:, j, hs],
                                 start=(j == 0 and h == 0), stop=False, skip_group_check=True)
                pe.wait_ge(*done("v_sgla", l))
                from_state(gla_q, st_gla, "t_ygla")

                pe.wait_ge(*done("v_heads", l))
                for i in range(4):
                    for b in (2 * i, 2 * i + 1):
                        for j in range(TT):
                            m = T.transpose(bank[i][:, (b % 2) * S + P * j:(b % 2) * S + P * j + P],
                                            heads[:, j, b * P:b * P + P], ident[:])
                    inc(m, "t_cat")
                pe.wait_ge(*done("v_cat", l))
                pe.wait_ge(*done("s_cat", l))
                for hf in range(2):
                    w = weights(l, f"out{hf}")
                    for j in range(TT):
                        for b in range(KD):
                            m = T.matmul(bank[4 + 2 * hf + j][:], x_cm[:, b, tile_(j)], w[:, b, :], start=(b == 0),
                                         stop=(b == KD - 1))
                        inc(m, "t_mix")
                pe.wait_ge(*done("v_x1", l))
                for i in range(4):
                    for k in (2 * i, 2 * i + 1):
                        for j in range(TT):
                            m = T.transpose(bank[i][:, (k % 2) * S + P * j:(k % 2) * S + P * j + P],
                                            x_tm[:, j, k::KD], ident[:])
                    inc(m, "t_x1")
                pe.wait_ge(*done("s_x1", l))
                for j in range(TT):
                    for k in range(KD):
                        m = T.matmul(bank[4][:, j * NE:j * NE + NE], x_cm[:, k, tile_(j)], rout_w[:, k, :],
                                     start=(k == 0), stop=(k == KD - 1))
                inc(m, "t_route")
                pe.wait_ge(*done("v_sel", l))
                sel = rt[:, 3]
                T.matmul(bank[5][:, 0:NE], tri_before[:], sel[:, 0], start=True, stop=True)
                T.matmul(bank[5][:, NE:2 * NE], tri_before[:], sel[:, 1], start=True, stop=False)
                T.matmul(bank[5][:, NE:2 * NE], all_ones[:], sel[:, 0], start=False, stop=True)
                T.matmul(bank[5][:, 2 * NE:3 * NE], all_ones[:], sel[:, 0], start=True, stop=False)
                inc(T.matmul(bank[5][:, 2 * NE:3 * NE], all_ones[:], sel[:, 1], start=False, stop=True), "t_slots")
                two_ways(pe, l, lambda rounds: experts_t(pe, weights, l, rounds))
                if l < L - 1:
                    pe.wait_ge(*done("v_x2", l))
                    turn_x(l + 1)

        E_HALF = float(np.exp(-0.5))

        def conv_taps(l, i):
            for b in range(2):
                blk = 2 * (i - 4) + b
                for tap in range(TAPS - 1):
                    s = TAPS - 1 - tap
                    yield (xbc[:, blk, s:], bank[i % 2][:, b * S:b * S + S - s], vcol("ssd_conv_w", l, tap * XB + blk))

        @block.vector
        def _(dve):
            c = Chain("v_chain")

            def do(ins):
                c.add(ins)
                c.join(dve)

            def recip1(ap, plus=True):
                do(V.tensor_scalar(ap, ap, 1.0, None, ALU.add))
                return V.reciprocal(ap, ap)

            dve.wait_ge(vec_turned, 1)
            c.add(V.tensor_copy(vec[:], bank[4][:, 0:n_rows]))
            dve.wait_ge(small_loaded, 16 * (6 + 3 * L))
            c.join(dve)
            for dst, name, sc_, off in ((om_mu, "rwkv_mu", -1.0, 1.0), (om_ka, "rwkv_k_a", -1.0, 1.0),
                                        (neg_w0, "rwkv_w0", -1.0, 0.0), (neg_a0, "rwkv_a0", -1.0, 0.0)):
                at, per = rows[name]
                c.add(V.tensor_scalar(dst[:], vec[:, at:at + L * per], sc_, off, ALU.mult, ALU.add))
            c.join(dve)
            dve.wait_ge(s_small, 1)
            V.tensor_scalar(ssd_small[:, 1], ssd_small[:, 1], -1.0, None, ALU.mult).then_inc(vec_ready, 1)
            dve.wait_ge(vec_ready, 1)

            def cat(p):
                return p.rearrange("p b s -> p (b s)")

            def by_chunk(p):
                return p.rearrange("p b (c i) -> p (b c) i", i=CH)

            def anchors(cum, an):
                v = cum.rearrange("p b (c i) -> p b c i", i=CH)
                do(V.tensor_copy(an[:, :, 0, :], v[:, :, :, CH // 2 - 1]))
                do(V.tensor_tensor(an[:, :, 1, :], v[:, :, :, CH - 1], an[:, :, 0, :], ALU.subtract))
                c.add(V.tensor_tensor(an[:, :, 2, 0:NC - 1], an[:, :, 1, 0:NC - 1], an[:, :, 0, 1:NC], ALU.add))
                do(V.tensor_copy(an[:, :, 2, NC - 1:NC], an[:, :, 1, NC - 1:NC]))

            def minus_anchor(out_, cum, an):
                for b in range(2):
                    i = V.tensor_tensor(out_[:, b].rearrange("p (c i) -> p c i", i=CH),
                                        cum[:, b].rearrange("p (c i) -> p c i", i=CH),
                                        wide(an[:, b, 0, :], CH), ALU.subtract)
                    if b == 0:
                        c.add(i)
                return i

            def layer_norm(l, which):
                for j in range(TT):
                    for hf in range(2):
                        if which == 0:
                            dve.wait_ge(*done("t_mix", l, 2 * hf + j + 1))
                        else:
                            dve.wait_ge(*done("t_scat", l))
                        cs = slice(hf * 512, hf * 512 + 512)
                        c.add(V.scalar_tensor_tensor(out=x_tm[:, j, cs], in0=x_tm[:, j, cs], scalar=ALPHA,
                                                     in1=bank[4 + 2 * hf + j if which == 0 else 2 * j + hf][:],
                                                     op0=ALU.mult, op1=ALU.add))
                    c.join(dve)
                    for hf in range(2):
                        c.add(V.bn_stats(bn6[:, j, hf, :], x_tm[:, j, hf * 512:hf * 512 + 512]))
                    c.join(dve)
                    inc(V.bn_aggr(bn2[:, j, :], bn6[:, j].rearrange("p a b -> p (a b)")), "v_var")
                dve.wait_ge(ln_loaded.sem, 64 * l + 32 * (which + 1))
                for j in range(TT):
                    dve.wait_ge(*done("s_rstd", l, 2 * which + j + 1))
                    do(V.tensor_scalar(x_tm[:, j], x_tm[:, j], bn2[:, j, 0:1], bn2[:, j, 1:2], ALU.subtract, ALU.mult))
                    do(V.tensor_tensor(x_tm[:, j], x_tm[:, j], ln_vec[:, 0], ALU.mult))
                    ins = V.tensor_tensor(x_tm[:, j], x_tm[:, j], ln_vec[:, 1], ALU.add)
                inc(ins, "v_x1" if which == 0 else "v_x2")

            for l in range(L):
                for i in range(4):
                    dve.wait_ge(*done("s_mu", l, i + 1))
                    for b in range(2):
                        k = 2 * i + b
                        ins = V.scalar_tensor_tensor(out=rwc[:, k, 1:], in0=bank[i % 2][:, b * S:b * S + S - 1],
                                                     scalar=vcol("rwkv_mu", l, k), in1=rwc[:, k, 1:],
                                                     op0=ALU.mult, op1=ALU.add)
                        if b == 0:
                            c.add(ins)
                    c.join(dve)
                    inc(ins, "v_proj")
                dve.wait_ge(*done("v_proj", l, 4))
                dve.wait_ge(*done("s_low", l, 1))
                th = fac[3][0:HALF, 0, :]
                do(recip1(th))
                inc(V.tensor_scalar(th, th, 2.0, -1.0, ALU.mult, ALU.add), "v_gates")
                dve.wait_ge(*done("s_low", l, 2))
                inc(recip1(fac[3][:, 1, :]), "v_gates")

                def conv(i):
                    dve.wait_ge(*done("s_conv", l, i - 3))
                    for n, (o, p, w) in enumerate(conv_taps(l, i)):
                        if n % 3:
                            c.join(dve)
                        ins = V.scalar_tensor_tensor(out=o, in0=p, scalar=w, in1=o, op0=ALU.mult, op1=ALU.add)
                        if n < 5:
                            c.add(ins)
                    c.join(dve)
                    inc(ins, "v_proj")

                conv(4)
                dve.wait_ge(*done("t_lowrank", l, 4))
                inc(V.tensor_scalar(cat(fac[2]), bank[5][:], 1e-24, None, ALU.max), "v_ssmax")
                dve.wait_ge(*done("s_ez", l))
                do(recip1(cat(fac[0])))
                do(V.tensor_scalar(cat(fac[0]), cat(fac[0]), -E_HALF, None, ALU.mult))
                dve.wait_ge(*done("t_lowrank", l, 3))
                for b in range(2):
                    c.add(V.tensor_tensor_scan(fac[3][:, b], scan_reset[:], fac[0][:, b], 0.0, ALU.mult, ALU.add))
                c.join(dve)
                anchors(fac[3], anchor)
                do(minus_anchor(fac[3], fac[3], anchor))
                inc(V.tensor_tensor(cat(fac[0]), cat(fac[3]), cat(fac[0]), ALU.subtract), "v_decay")
                conv(5)
                dve.wait_ge(*done("s_ea", l))
                do(recip1(cat(fac[1])))
                dve.wait_ge(*done("s_norm", l))
                for b in range(2):
                    c.add(V.scalar_tensor_tensor(out=fac[2][:, b], in0=rwc[:, 2 + b], scalar=vcol("rwkv_k_k", l, b),
                                                 in1=fac[2][:, b], op0=ALU.mult, op1=ALU.mult))
                c.join(dve)
                dve.wait_ge(*done("s_e", l, 1))
                inc(V.scalar_tensor_tensor(out=ar_cm[:, :, 0, :], in0=fac[2], scalar=-1.0, in1=fac[0],
                                           op0=ALU.mult, op1=ALU.mult), "v_ratio")
                dve.wait_ge(*done("v_ratio", l))
                for b in range(2):
                    c.add(V.tensor_scalar(fac[0][:, b], fac[1][:, b], vcol("rwkv_k_a", l, b),
                                          om_ka[:, l * 2 + b:l * 2 + b + 1], ALU.mult, ALU.add))
                c.join(dve)
                do(V.tensor_tensor(rwc[:, 2:4], rwc[:, 2:4], fac[0], ALU.mult))
                for b in range(2):
                    ins = V.scalar_tensor_tensor(out=fac[0][:, b], in0=rwc[:, b], scalar=vcol("rwkv_r_k", l, b),
                                                 in1=rwc[:, 2 + b], op0=ALU.mult, op1=ALU.mult)
                    if b == 0:
                        c.add(ins)
                c.join(dve)
                inc(ins, "v_bonus")
                do(V.tensor_tensor(fac[1], fac[2], fac[1], ALU.mult))
                dve.wait_ge(*done("s_e", l, 2))
                inc(V.tensor_tensor(k_cm[:], rwc[:, 2:4], b_cm[:], ALU.mult), "v_kcm")
                dve.wait_ge(*done("v_kcm", l))
                inc(V.tensor_tensor(b_cm[:], fac[1], b_cm[:], ALU.mult), "v_bcm")
                dve.wait_ge(*done("s_e", l, 3))
                inc(V.tensor_tensor(ar_cm[:, :, 1, :], rwc[:, 0:2], fac[3], ALU.mult), "v_rcm")
                conv(6)
                dve.wait_ge(*done("t_proj", l, 8))
                c.add(V.tensor_copy(alr[:], bank[1][0:RANK, 0:S]))
                ins = V.tensor_tensor(dt[:], bank[1][:, S:S + TT * SH].rearrange("p (j h) -> p j h", j=TT),
                                      each(ssd_small[:, 0, l, :], TT), ALU.add)
                c.join(dve)
                inc(ins, "v_proj")

                dve.wait_ge(*done("t_glaz", l))
                for b in range(2):
                    ins = V.tensor_scalar(sc[1][:, b], bank[5][:, b * S:b * S + S], vcol("gla_b_alpha", l, b), None, ALU.add)
                inc(ins, "v_gz")

                for u in range(TT * NH):
                    j, h = divmod(u, NH)
                    dve.wait_ge(*done("t_pair", l, u + 1))
                    inc(V.tensor_tensor(gmat[:, j, h].rearrange("p x y s -> p x (y s)"),
                                        bank[6 + u % 2][:].rearrange("p (x z) -> p x z", x=2),
                                        each(chunk_mask[:].rearrange("p y s -> p (y s)"), 2), ALU.mult), "v_pair")
                for j in range(TT):
                    dve.wait_ge(*done("v_pair", l, NH * (j + 1)))
                    c.add(V.tensor_tensor(inv_t[:, j], gmat[:, j, :, 0, 0, :], each(level_mask[:, 0, :], NH), ALU.mult))
                    inc(V.tensor_tensor(lvl[:, j], gmat[:, j, :, 0, 0, :], each(level_mask[:, 1, :], NH), ALU.mult), "v_lvl")
                    dve.wait_ge(*done("t_ltm", l, j + 1))
                    do(V.tensor_tensor(inv[:, j], bank[2 + j][:].rearrange("p (h s) -> p h s", h=NH),
                                       each(level0_tm[:], NH), ALU.mult))
                    do(V.tensor_tensor(inv_t[:, j], inv_t[:, j], each(ident[:], NH), ALU.add))
                    inc(V.tensor_tensor(inv[:, j], inv[:, j], each(ident[:], NH), ALU.add), "v_inv0")

                def xbc_silu(i):
                    dve.wait_ge(*done("s_silx", l, i + 1))
                    do(recip1(cat(sc[0][:])))
                    inc(V.tensor_tensor(xbc[:, 2 * i:2 * i + 2], xbc[:, 2 * i:2 * i + 2], sc[0][:], ALU.mult), "v_xbc")

                def gla_cum():
                    dve.wait_ge(*done("s_ge", l))
                    do(V.scalar_tensor_tensor(out=cat(sc[1][:]), in0=cat(sc[1][:]), scalar=0.0, in1=cat(sc[2][:]),
                                              op0=ALU.min, op1=ALU.subtract))
                    for b in range(2):
                        c.add(V.tensor_tensor_scan(sc[3][:, b], scan_reset[:], sc[1][:, b], 0.0, ALU.mult, ALU.add))
                    c.join(dve)
                    anchors(sc[3][:], anchor_g)
                    inc(minus_anchor(sc[3], sc[3], anchor_g), "v_gcum")

                def gla_qk():
                    dve.wait_ge(*done("s_expl", l))
                    dve.wait_ge(*done("s_qk", l))
                    c.add(V.scalar_tensor_tensor(out=cat(gla_q[:]), in0=cat(gla_q[:]), scalar=HD ** -0.5,
                                                 in1=cat(sc[2][:]), op0=ALU.mult, op1=ALU.mult))
                    ins = V.tensor_tensor(cat(gla_k[:]), cat(gla_k[:]), cat(sc[3][:]), ALU.mult)
                    c.join(dve)
                    inc(ins, "v_gqk")

                def ssd_dt():
                    dve.wait_ge(*done("s_dtl", l))
                    inc(V.scalar_tensor_tensor(out=dt[:], in0=dt[:], scalar=0.0, in1=dte[:, 0:2], op0=ALU.max,
                                               op1=ALU.add), "v_dt")
                    dve.wait_ge(*done("v_dt", l))
                    inc(V.tensor_tensor(da[:], dt[:], each(ssd_small[:, 1, l, :], TT), ALU.mult), "v_da")

                def gate_silu():
                    dve.wait_ge(*done("s_silg", l))
                    for j in range(TT):
                        g = g_silu[:, j]
                        do(recip1(g))
                        c.add(V.tensor_tensor(gla_vg[:, j, GW:], gla_vg[:, j, GW:], g, ALU.mult))
                    c.join(dve)

                fill = [lambda: xbc_silu(0), gla_cum, lambda: xbc_silu(1), ssd_dt, gla_qk, lambda: xbc_silu(2)]
                for lev in range(5):
                    for j in range(TT):
                        n = lev * TT + j
                        dve.wait_ge(*done("t_inv", l, n + 1))
                        if lev < 4:
                            c.add(V.tensor_tensor(inv[:, j], inv[:, j],
                                                  bank[6 + j][:].rearrange("p (h s) -> p h s", h=NH), ALU.add))
                        ins = V.tensor_tensor(inv_t[:, j], inv_t[:, j],
                                              bank[4 + j][:].rearrange("p (h s) -> p h s", h=NH), ALU.add)
                        c.join(dve)
                        inc(ins, "v_inv")
                        if lev < 4:
                            inc(V.tensor_tensor(lvl[:, j], gmat[:, j, :, 0, 0, :],
                                                each(level_mask[:, lev + 2, :], NH), ALU.mult), "v_lvl")
                    if fill:
                        fill.pop(0)()
                for f in fill:
                    f()
                for q in range(4):
                    if q == 0:
                        for name in ("v_gqk", "v_da", "v_xbc"):
                            dve.wait_ge(*done(name, l))
                    for i in range(4):
                        j, h = q // 2, 4 * (q % 2) + i
                        ins = V.tensor_scalar(seg_in(q, i), tri_after[:], da[:, j, h:h + 1], None, ALU.mult)
                        if i < 3:
                            c.add(ins)
                    c.join(dve)
                    inc(ins, "v_lhs")
                dve.wait_ge(*done("t_q", l))
                for j in range(TT):
                    ins = V.tensor_tensor(ar_cm[:, :, 1, tile_(j)], ar_cm[:, :, 1, tile_(j)],
                                          bank[4][:, j * S:j * S + S].rearrange("p (b s) -> p b s", b=2), ALU.add)
                    if j == 0:
                        c.add(ins)
                c.join(dve)
                inc(ins, "v_q")
                dve.wait_ge(*done("t_carry", l))
                inc(V.tensor_tensor(tm_t[:].rearrange("p b c n -> p (b c) n"),
                                    bank[6][:, 0:S].rearrange("p (b n) -> p b n", n=HD), each(ident2[:], 4), ALU.add), "v_carry")
                dve.wait_ge(*done("s_e", l, 3))
                for i in range(NC - 1):
                    dve.wait_ge(*done("t_srw", l, i + 1))
                    inc(V.tensor_tensor(st_rw[:, :, i + 1, :],
                                        bank[7][:, i * P:i * P + P].rearrange("p (b n) -> p b n", b=2),
                                        wide(anchor[:, :, 2, i], HD), ALU.mult), "v_srw")
                dve.wait_ge(*done("t_cb", l))
                do(V.tensor_tensor(k_cm[:].rearrange("p a b -> p (a b)").rearrange("p (q s) -> p q s", q=4),
                                   bank[3][:].rearrange("p (q s) -> p q s", q=4), each(tri_incl[:], 4), ALU.mult))
                for j in range(TT):
                    dve.wait_ge(*done("s_xs", l, j + 1))
                    inc(V.tensor_tensor(xdt(j).rearrange("p (h n) -> p h n", n=HD),
                                        heads[:, j, GW:GW + SW].rearrange("p (h n) -> p h n", n=HD),
                                        wide(dt[:, j, :], HD), ALU.mult), "v_xdt")
                for q in range(4):
                    dve.wait_ge(*done("s_seg", l, q + 1))
                    cb = k_cm[:].rearrange("p a b -> p (a b)")[:, q * P:q * P + P]
                    inc(V.tensor_tensor(seg_w4(q), seg_w4(q), each(cb, 4), ALU.mult), "v_w")
                dve.wait_ge(*done("s_edge", l))
                dve.wait_ge(*done("v_xdt", l, 1))
                inc(V.tensor_tensor(xw.rearrange("p (h n) -> p h n", n=HD), xdt(0).rearrange("p (h n) -> p h n", n=HD),
                                    wide(dte[:, 2, :], HD), ALU.mult), "v_xw")
                dve.wait_ge(*done("t_sssd", l))
                inc(V.tensor_copy(st_ssd[:], bank[2][:, 0:4 * HD]), "v_sssd")
                gate_silu()
                dve.wait_ge(*done("t_seg", l))
                for j in range(TT):
                    dve.wait_ge(*done("t_gsc", l, j + 1))
                    inc(V.tensor_tensor(gsc4(j), bank[(4, 7)[j]][:].rearrange("p (h s) -> p h s", h=NH),
                                        each(chunk_mask[:, 1, :], NH), ALU.mult), "v_gsc")
                dve.wait_ge(*done("t_sgla", l))
                for i in range(NC - 1):
                    src = bank[2][:, i * P:i * P + P].rearrange("p (b n) -> p b n", b=2)
                    dst = st_gla[:, :, i + 1, :]
                    if i:
                        do(V.tensor_tensor(dst, src, st_gla[:, :, i, :], ALU.add))
                        src = dst
                    inc(V.tensor_tensor(dst, src, wide(anchor_g[:, :, 2, i], HD), ALU.mult), "v_sgla")
                    dve.wait_ge(*done("v_sgla", l, i + 1))
                dve.wait_ge(*done("t_yrw", l))
                y = bank[5][:].rearrange("p (h n) -> p h n", n=HD)
                mean = gn[:, 0].rearrange("p j h -> p (j h)")
                rstd = gn[:, 1].rearrange("p j h -> p (j h)")
                yc, sq = cat(sc[2][:]).rearrange("p (h n) -> p h n", n=HD), cat(sc[3][:]).rearrange("p (h n) -> p h n", n=HD)
                do(V.tensor_reduce(mean, y, AX.X, ALU.add))
                do(V.tensor_scalar(mean, mean, 1.0 / HD, None, ALU.mult))
                do(V.tensor_tensor(yc, y, wide(mean, HD), ALU.subtract))
                do(V.tensor_tensor(sq, yc, yc, ALU.mult))
                inc(V.tensor_reduce(rstd, sq, AX.X, ALU.add), "v_gnvar")
                dve.wait_ge(*done("s_gnr", l))
                dve.wait_ge(gn_loaded.sem, 32 * (l + 1))
                do(V.tensor_tensor(yc, yc, wide(rstd, HD), ALU.mult))
                for j in range(TT):
                    o = heads[:, j, GW + SW:]
                    yj = sc[2][:, j]
                    bv = sc[3][:, j]
                    c.add(V.tensor_tensor(yj, yj, gn_vec[:, 0], ALU.mult))
                    do(V.tensor_tensor(bv.rearrange("p (h n) -> p h n", n=HD),
                                       tmq[:, j, 2, :].rearrange("p (h n) -> p h n", n=HD), wide(bonus[:, j, :], HD), ALU.mult))
                    do(V.tensor_tensor(yj, yj, gn_vec[:, 1], ALU.add))
                    do(V.tensor_tensor(yj, yj, bv, ALU.add))
                    ins = V.tensor_tensor(o, yj, g_tm[:, j], ALU.mult)
                    if j == 0:
                        c.add(ins)
                c.join(dve)
                inc(ins, "v_heads")
                for j in range(TT):
                    dve.wait_ge(*done("s_silz", l, j + 1))
                    zj, o = z_tm[:, j], heads[:, j, GW:GW + SW]
                    oh = o.rearrange("p (h n) -> p h n", n=HD)
                    do(recip1(cat(sc[2][:])) if j == 0 else recip1(cat(sc[3][:])))
                    do(V.tensor_tensor(zj, zj, cat(sc[2 + j][:]), ALU.mult))
                    do(V.tensor_tensor(oh, oh, wide(ssd_small[:, 2, l, :], HD), ALU.mult))
                    dve.wait_ge(*done("t_yssd", l, j + 1))
                    do(V.tensor_tensor(o, o, bank[j][:], ALU.add))
                    if j:
                        dve.wait_ge(*done("t_yssd", l, 3))
                        tmp = cat(sc[2][:])
                        do(V.tensor_tensor(tmp.rearrange("p (h n) -> p h n", n=HD),
                                           bank[6][:].rearrange("p (h n) -> p h n", n=HD), wide(dte[:, 3, :], HD), ALU.mult))
                        do(V.tensor_tensor(o, o, tmp, ALU.add))
                    inc(V.tensor_tensor(o, o, zj, ALU.mult), "v_yssd")
                for j in range(TT):
                    dve.wait_ge(*done("s_rssd", l, j + 1))
                    for g in range(2):
                        o = heads[:, j, GW + g * 256:GW + g * 256 + 256]
                        ins = V.tensor_scalar(o, o, rms_s[:, j, g:g + 1], None, ALU.mult)
                        if (j, g) != (1, 1):
                            c.add(ins)
                c.join(dve)
                inc(ins, "v_heads")
                dve.wait_ge(*done("t_ygla", l))
                do(V.tensor_copy(cat(sc[2][:]), bank[5][:]))
                do(V.tensor_tensor(cat(sc[3][:]), cat(sc[2][:]), cat(sc[2][:]), ALU.mult))
                rr = rms[:].rearrange("p j h -> p (j h)")
                inc(V.tensor_reduce(rr, cat(sc[3][:]).rearrange("p (h n) -> p h n", n=HD), AX.X, ALU.add), "v_glasum")
                dve.wait_ge(*done("s_rgla", l))
                do(V.tensor_tensor(yc, yc, wide(rr, HD), ALU.mult))
                for j in range(TT):
                    ins = V.tensor_tensor(heads[:, j, 0:GW], sc[2][:, j], gla_vg[:, j, GW:], ALU.mult)
                    if j == 0:
                        c.add(ins)
                c.join(dve)
                inc(ins, "v_heads")
                for i in (1, 3):
                    dve.wait_ge(*done("t_cat", l, i + 1))
                    for b in range(2):
                        inc(V.tensor_scalar(x_cm[:, 2 * i + b, :], bank[i][:, b * S:b * S + S], cat_gain(l, 2 * i + b),
                                            None, ALU.mult), "v_cat")
                layer_norm(l, 0)

                dve.wait_ge(*done("t_route", l))
                inc(V.tensor_copy(rt[:, 0].rearrange("p j e -> p (j e)"), bank[4][:, 0:TT * NE]), "v_logit")
                dve.wait_ge(*done("s_route", l))
                score, sel = rt[:, 1], rt[:, 2]
                do(recip1(score))
                do(V.tensor_tensor(sel, score, each(rout_b[:], TT), ALU.add))
                s4 = sel.rearrange("p j (g k) -> p (j g) k", k=EPG)
                pr = rt[:, 3:5].rearrange("p a j e -> p (a j e)")[:, 0:6 * TT * NG].rearrange("p (k m) -> p k m", k=6)
                n = 0
                for a in range(EPG):
                    for b in range(a + 1, EPG):
                        c.add(V.tensor_tensor(pr[:, n, :], s4[:, :, a], s4[:, :, b], ALU.add))
                        n += 1
                c.join(dve)
                gs = rg[:, 0].rearrange("p j g -> p (j g)")
                do(V.tensor_reduce(gs, pr.rearrange("p k m -> p m k"), AX.X, ALU.max))
                beat = rg[:, 1]
                do(V.memset(beat, 0.0))
                g3 = rg[:, 0]
                for a in range(NG):
                    if a:
                        do(V.tensor_tensor(rg[:, 2, :, 0:a], g3[:, :, a:a + 1].to_broadcast([P, TT, a]), g3[:, :, 0:a], ALU.is_gt))
                        do(V.tensor_tensor(beat[:, :, 0:a], beat[:, :, 0:a], rg[:, 2, :, 0:a], ALU.add))
                    if a < NG - 1:
                        do(V.tensor_tensor(rg[:, 2, :, a + 1:], g3[:, :, a:a + 1].to_broadcast([P, TT, NG - 1 - a]),
                                           g3[:, :, a + 1:], ALU.is_ge))
                        do(V.tensor_tensor(beat[:, :, a + 1:], beat[:, :, a + 1:], rg[:, 2, :, a + 1:], ALU.add))
                do(V.tensor_scalar(beat, beat, 0.5, None, ALU.is_lt))
                rank = rt[:, 3]
                do(V.memset(rank, 0.0))
                r4 = rank.rearrange("p j (g k) -> p (j g) k", k=EPG)
                t4 = rt[:, 4].rearrange("p j (g k) -> p (j g) k", k=EPG)
                for a in range(EPG):
                    if a:
                        do(V.tensor_tensor(t4[:, :, 0:a], s4[:, :, a:a + 1].to_broadcast([P, TT * NG, a]), s4[:, :, 0:a], ALU.is_gt))
                        do(V.tensor_tensor(r4[:, :, 0:a], r4[:, :, 0:a], t4[:, :, 0:a], ALU.add))
                    if a < EPG - 1:
                        do(V.tensor_tensor(t4[:, :, a + 1:], s4[:, :, a:a + 1].to_broadcast([P, TT * NG, EPG - 1 - a]),
                                           s4[:, :, a + 1:], ALU.is_ge))
                        do(V.tensor_tensor(r4[:, :, a + 1:], r4[:, :, a + 1:], t4[:, :, a + 1:], ALU.add))
                do(V.tensor_scalar(rank, rank, 1.5, None, ALU.is_lt))
                inc(V.tensor_tensor(r4, r4, wide(beat.rearrange("p j g -> p (j g)"), EPG), ALU.mult), "v_sel")
                dve.wait_ge(*done("v_sel", l))
                do(V.tensor_tensor(gate[:], rank, score, ALU.mult))
                do(V.tensor_reduce(rms_s[:, :, 0], gate[:], AX.X, ALU.add))
                do(V.reciprocal(rms_s[:, :, 0], rms_s[:, :, 0]))
                do(V.tensor_tensor(gate[:], gate[:], wide(rms_s[:, :, 0], NE), ALU.mult))

                dve.wait_ge(*done("s_xhi", l))
                inc(V.tensor_tensor(x_lo[:], x_tm[:], x_hi[:].bitcast(F32), ALU.subtract), "v_xlo")
                dve.wait_ge(*done("t_slots", l))
                do(V.tensor_scalar(pos[:], bank[5][:, 0:TT * NE].rearrange("p (j e) -> p j e", j=TT), 1.0, None, ALU.add))
                do(V.tensor_tensor(pos[:], pos[:], rank, ALU.mult))
                do(V.tensor_scalar(pos[:], pos[:], -1.0, None, ALU.add))
                do(V.tensor_reduce(rms_s[:, 0, 0:1], bank[5][:, 2 * NE:3 * NE], AX.X, ALU.max))
                inc(V.tensor_scalar(crowded[:], rms_s[:, 0, 0:1], CROWD, None, ALU.is_gt), "v_flag")
                two_ways(dve, l, lambda rounds: experts_v(dve, l, rounds))
                layer_norm(l, 1)

        LN2 = float(np.log(2.0))

        @block.scalar
        def _(act):
            c = Chain("s_chain")

            def do(ins):
                c.add(ins)
                c.join(act)

            def flat(p):
                return p.rearrange("p b s -> p (b s)")

            def silu_arg(out_, in_, name):
                return inc(A.activation(out_, in_, ACT.Exp, scale=-1.0), name)

            A.preload_act_table_set("natural_log_exp_and_others")
            act.wait_ge(small_loaded, 16 * (6 + 3 * L))
            A.activation(ssd_small[:, 1], ssd_small[:, 1], ACT.Exp).then_inc(s_small, 1)
            for l in range(L):
                for i in range(4):
                    act.wait_ge(*done("t_x", l, i + 1))
                    inc(A.activation(x_cm[:, 2 * i:2 * i + 2, :], bank[i][:].rearrange("p (k s) -> p k s", k=2),
                                     ACT.Copy), "s_x")
                if l == 0:
                    act.wait_ge(vec_ready, 1)
                for i in range(4):
                    act.wait_ge(*done("t_proj", l, i + 1))
                    for b in range(2):
                        k = 2 * i + b
                        ins = A.activation(rwc[:, k, :], bank[i % 2][:, b * S:b * S + S], ACT.Copy,
                                           scale=om_mu[:, l * 8 + k:l * 8 + k + 1])
                    inc(ins, "s_mu")

                def conv(i):
                    act.wait_ge(*done("t_proj", l, i + 1))
                    for b in range(2):
                        blk = 2 * (i - 4) + b
                        ins = A.activation(xbc[:, blk, :], bank[i % 2][:, b * S:b * S + S], ACT.Identity,
                                           scale=vcol("ssd_conv_w", l, (TAPS - 1) * XB + blk), bias=vcol("ssd_conv_b", l, blk))
                    inc(ins, "s_conv")

                act.wait_ge(*done("v_proj", l, 4))
                inc(A.activation(fac[3][0:HALF, 0, :], rwc[0:HALF, 6, :], ACT.Exp, scale=-2.0), "s_low")
                inc(A.activation(fac[3][:, 1, :], rwc[:, 7, :], ACT.Exp, scale=-1.0), "s_low")
                for b in range(2):
                    ins = A.activation(fac[2][:, b], rwc[:, 2 + b], ACT.Square, scale=vcol("rwkv_k_k", l, b))
                inc(ins, "s_sq")
                conv(4)
                act.wait_ge(*done("t_lowrank", l, 1))
                for b in range(2):
                    ins = A.activation(fac[0][:, b], bank[2][:, b * S:b * S + S], ACT.Exp, scale=-1.0,
                                       bias=neg_w0[:, l * 2 + b:l * 2 + b + 1])
                inc(ins, "s_ez")
                act.wait_ge(*done("t_lowrank", l, 2))
                for b in range(2):
                    ins = A.activation(fac[1][:, b], bank[3][:, b * S:b * S + S], ACT.Exp, scale=-1.0,
                                       bias=neg_a0[:, l * 2 + b:l * 2 + b + 1])
                inc(ins, "s_ea")
                act.wait_ge(*done("t_lowrank", l, 3))
                inc(A.activation(g_tm[:], bank[4][:].rearrange("p (j c) -> p j c", j=TT), ACT.Copy), "s_g")
                act.wait_ge(*done("v_ssmax", l))
                do(A.activation(flat(fac[2]), flat(fac[2]), ACT.Ln, scale=2.0 ** 30))
                inc(A.activation(flat(fac[2]), flat(fac[2]), ACT.Exp, scale=-0.5, bias=ln_shift[:]), "s_norm")
                conv(5)
                act.wait_ge(*done("v_decay", l))
                inc(A.activation(flat(fac[0]), flat(fac[0]), ACT.Exp), "s_e")
                inc(A.activation(b_cm[:], fac[3], ACT.Exp, scale=-1.0), "s_e")
                A.activation(anchor[:, :, 2, :], anchor[:, :, 2, :], ACT.Exp)
                inc(A.activation(flat(fac[3]), flat(fac[3]), ACT.Exp), "s_e")
                conv(6)
                act.wait_ge(*done("v_proj", l, 8))
                do(A.activation(dte[:, 0:2], dt[:], ACT.Abs))
                do(A.activation(dte[:, 0:2], dte[:, 0:2], ACT.Exp, scale=-1.0))
                inc(A.activation(dte[:, 0:2], dte[:, 0:2], ACT.Ln, bias=1.0), "s_dtl")
                act.wait_ge(*done("v_gz", l))
                do(A.activation(flat(sc[2][:]), flat(sc[1][:]), ACT.Abs))
                do(A.activation(flat(sc[2][:]), flat(sc[2][:]), ACT.Exp, scale=-1.0))
                inc(A.activation(flat(sc[2][:]), flat(sc[2][:]), ACT.Ln, bias=1.0), "s_ge")
                for n, (src, dst) in enumerate(((6, tmq[:, :, 2, :]), (4, None), (7, None), (3, tmq[:, :, 1, :]),
                                                (2, tmq[:, :, 0, :]))):
                    act.wait_ge(*done("t_turned", l, n + 1))
                    if n == 1:
                        ins = A.activation(bonus[:].rearrange("p j h -> p (j h)"), bank[4][:, 0:TT * NH], ACT.Copy)
                    elif n == 2:
                        for j in range(TT):
                            ins = A.activation(a_w1[:, j, :, 0, :], bank[7][:, j * RW:j * RW + RW]
                                               .rearrange("p (h n) -> p h n", n=HD), ACT.Copy)
                    else:
                        ins = A.activation(dst, bank[src][:].rearrange("p (j c) -> p j c", j=TT), ACT.Copy)
                    inc(ins, "s_turned")
                for i, (name, dst) in enumerate((("s_qk", gla_q), ("s_qk", gla_k))):
                    act.wait_ge(*done("t_proj", l, 9 + i))
                    inc(A.activation(dst[:], bank[i][:].rearrange("p (b s) -> p b s", b=2), ACT.Copy), name)
                act.wait_ge(*done("t_mv", l))
                for j in range(TT):
                    inc(A.activation(a_w1[:, j, :, 1, :], bank[4][:, j * RW:j * RW + RW].rearrange("p (h n) -> p h n", n=HD),
                                     ACT.Copy), "s_mv")

                def silx(i):
                    act.wait_ge(*done("v_proj", l, 5 + i))
                    if i:
                        act.wait_ge(*done("v_xbc", l, i))
                    inc(A.activation(sc[0][:], xbc[:, 2 * i:2 * i + 2], ACT.Exp, scale=-1.0), "s_silx")

                def gla_exp():
                    act.wait_ge(*done("v_gcum", l))
                    A.activation(anchor_g[:, :, 2, :], anchor_g[:, :, 2, :], ACT.Exp, scale=1.0 / 16)
                    do(A.activation(sc[2][:], sc[3][:], ACT.Exp, scale=1.0 / 16))
                    inc(A.activation(sc[3][:], sc[3][:], ACT.Exp, scale=-1.0 / 16), "s_expl")

                def vg(i):
                    act.wait_ge(*done("t_proj", l, 11 + i))
                    inc(A.activation(gla_vg[:, i], bank[i % 2][:], ACT.Copy), "s_vg")

                def zz(i):
                    act.wait_ge(*done("t_proj", l, 13 + i))
                    inc(A.activation(z_tm[:, i], bank[i % 2][:], ACT.Copy), "s_z")

                fill = [lambda: (silx(0), vg(0)), lambda: (vg(1), gla_exp()), lambda: (silx(1), zz(0)), lambda: zz(1),
                        lambda: silx(2)]
                for lev in range(5):
                    for j in range(TT):
                        n = lev * TT + j
                        act.wait_ge(*done("t_lp", l, n + 1))
                        inc(A.activation(lvl[:, j], bank[2 + j][:].rearrange("p (h s) -> p h s", h=NH), ACT.Copy), "s_lp")
                    fill.pop(0)()
                act.wait_ge(*done("v_xbc", l))
                inc(A.activation(g_silu[:], gla_vg[:, :, GW:], ACT.Exp, scale=-1.0), "s_silg")
                for j in range(TT):
                    act.wait_ge(*done("t_xa", l, j + 1))
                    inc(A.activation(a_w1[:, j].rearrange("p h a n -> p (h a n)"), bank[2 + j][:], ACT.Copy), "s_xa")
                for j in range(TT):
                    act.wait_ge(*done("t_ssd_tm", l, j + 1))
                    inc(A.activation(heads[:, j, GW:GW + SW], bank[j][:], ACT.Copy), "s_xs")
                act.wait_ge(*done("t_edge", l))
                inc(A.activation(b_tm[:], bank[2][:, 0:P], ACT.Copy), "s_xs")
                act.wait_ge(*done("t_edge", l))
                inc(A.activation(dte[:, 2:4].rearrange("p a b -> p (a b)"), bank[2][:, 2 * P:2 * P + 2 * SH], ACT.Exp), "s_edge")
                act.wait_ge(*done("t_q", l))
                for q in range(4):
                    act.wait_ge(*done("t_seg", l, q + 1))
                    inc(A.activation(seg_w4(q), bank[(4, 6, 7, 4)[q]][:].rearrange("p (h s) -> p h s", h=4), ACT.Exp), "s_seg")
                act.wait_ge(*done("t_gkt", l))
                inc(A.activation(gla_kt[:], bank[3][:].rearrange("p (j c) -> p j c", j=TT), ACT.Copy), "s_gln")

                def rstd(out_, in_, n, eps, name):
                    do(A.activation(out_, in_, ACT.Ln, scale=1.0 / n, bias=eps[:]))
                    inc(A.activation(out_, out_, ACT.Exp, scale=-0.5), name)

                act.wait_ge(*done("v_gnvar", l))
                rstd(gn[:, 1], gn[:, 1], HD, eps_gn, "s_gnr")
                act.wait_ge(*done("v_heads", l, 1))
                for j in range(TT):
                    inc(A.activation(flat(sc[2 + j][:]), z_tm[:, j], ACT.Exp, scale=-1.0), "s_silz")
                for j in range(TT):
                    act.wait_ge(*done("v_yssd", l, j + 1))
                    for g in range(2):
                        ins = A.activation(k_cm[:, 0, :], heads[:, j, GW + g * 256:GW + g * 256 + 256], ACT.Square,
                                           accum_out=rms_s[:, j, g:g + 1])
                        do(ins)
                    rstd(rms_s[:, j], rms_s[:, j], SW // 2, eps_ln, "s_rssd")
                act.wait_ge(*done("v_glasum", l))
                rstd(rms[:], rms[:], HD, eps_ln, "s_rgla")
                for i in (0, 2):
                    act.wait_ge(*done("t_cat", l, i + 1))
                    for b in range(2):
                        inc(A.activation(x_cm[:, 2 * i + b, :], bank[i][:, b * S:b * S + S], ACT.Copy,
                                         scale=cat_gain(l, 2 * i + b)), "s_cat")

                def ln_rstd(which):
                    for j in range(TT):
                        act.wait_ge(*done("v_var", l, 2 * which + j + 1))
                        rstd(bn2[:, j, 1:2], bn2[:, j, 1:2], 1, eps_ln, "s_rstd")

                ln_rstd(0)
                for i in range(4):
                    act.wait_ge(*done("t_x1", l, i + 1))
                    inc(A.activation(x_cm[:, 2 * i:2 * i + 2, :], bank[i][:].rearrange("p (k s) -> p k s", k=2),
                                     ACT.Copy), "s_x1")
                act.wait_ge(*done("v_logit", l))
                inc(A.activation(rt[:, 1], rt[:, 0], ACT.Exp, scale=-1.0), "s_route")
                inc(A.activation(x_hi[:], x_tm[:], ACT.Copy), "s_xhi")
                two_ways(act, l, lambda rounds: experts_s(act, l, rounds))
                ln_rstd(1)

        for name, signal in SIG.items():
            assert signal.given == L * signal.per * (2 if name in STEPS else 1), (name, signal.given, signal.per)


_INS = ["x", "w_in", "gla_w_alpha", "gla_b_alpha", "gla_norm_g", "ssd_conv_w", "ssd_conv_b", "ssd_dt_bias", "ssd_A_log",
        "ssd_D", "ssd_norm_g", "rwkv_mu", "rwkv_w0", "rwkv_w2", "rwkv_a0", "rwkv_a2", "rwkv_g2", "rwkv_k_k", "rwkv_k_a",
        "rwkv_r_k", "rwkv_ln_g", "rwkv_ln_b", "w_out", "ln1_g", "ln1_b", "router_w", "router_b", "exp_w_gate",
        "exp_w_up", "exp_w_down", "ln2_g", "ln2_b"]


def kernel(**inputs):
    import numpy as _np
    import concourse.bacc as _bacc
    from concourse import mybir as _mybir
    from concourse.bass_utils import run_bass_kernel_spmd as _run

    nc = _bacc.Bacc("TRN2", target_bir_lowering=False, num_devices=1)
    arrays, aps = {}, {}
    for name in _INS:
        a = _np.ascontiguousarray(inputs[name])
        arrays[f"in_{name}"] = a
        aps[name] = nc.dram_tensor(f"in_{name}", a.shape, _mybir.dt.from_np(a.dtype), kind="ExternalInput").ap()
    shape = inputs["x"].shape
    out = nc.dram_tensor("out_x", shape, _mybir.dt.float32, kind="ExternalOutput").ap()
    hybrid_trunk(nc, aps, out)
    r = _run(nc, [arrays], core_ids=[0])
    return r.results[0]["out_x"]
```

```python
from contextlib import ExitStack

import concourse.bass as bass
import numpy as np
from concourse import mybir

ALU = mybir.AluOpType
ACT = mybir.ActivationFunctionType
AX = mybir.AxisListType
F32 = mybir.dt.float32

P = 128
HALF = 64


def hybrid_trunk(nc: bass.Bass, t: dict, out: bass.AP):
    L, D, N_IN = t["w_in"].shape
    S = t["x"].shape[1]
    TT = S // P
    KD = D // P
    NE = t["exp_w_gate"].shape[1]
    FF = t["exp_w_gate"].shape[3]
    FB = FF // P
    GW = t["gla_w_alpha"].shape[2]
    RANK = t["gla_w_alpha"].shape[1]
    SW = t["ssd_norm_g"].shape[1]
    SH = t["ssd_D"].shape[1]
    RW = t["rwkv_w0"].shape[1]
    HD = t["gla_norm_g"].shape[1]
    NH = GW // HD
    XBC = t["ssd_conv_w"].shape[2]
    TAPS = t["ssd_conv_w"].shape[1]
    XB = XBC // P
    NG = 4
    EPG = NE // NG
    CH = 64
    NC = S // CH
    ALPHA = float((2 * L) ** 0.25)
    EPS = 1e-5
    GN_EPS = 64e-5
    BCOL = 512
    o_z = 4 * GW + RANK
    o_xbc = o_z + SW
    o_dt = o_xbc + XBC
    o_rw = o_dt + SH
    assert o_rw + 4 * RW == N_IN and EPG == NG and D == 1024 and S == 256 and HD == CH == HALF

    NSLOT = 8
    MORE = 2
    SL = 64
    ROUNDS = S // SL
    NW = 4

    def w_in_cols(l, c, n):
        return t["w_in"][l, :, c:c + n].rearrange("(p k) n -> p k n", k=KD)

    def blocks(l):
        b = [("rw0", [(w_in_cols(l, o_rw, BCOL), 0)]),
             ("rw1", [(w_in_cols(l, o_rw + BCOL, BCOL), 0)]),
             ("xbc0", [(w_in_cols(l, o_xbc, BCOL), 0)]),
             ("xbc1", [(w_in_cols(l, o_xbc + BCOL, XBC - BCOL + SH), 0),
                       (w_in_cols(l, 4 * GW, RANK), XBC - BCOL + SH)]),
             ("qk", [(w_in_cols(l, 0, BCOL), 0)]),
             ("vg", [(w_in_cols(l, BCOL, BCOL), 0)]),
             ("z", [(w_in_cols(l, o_z, BCOL), 0)])]
        for h in range(2):
            b.append((f"out{h}", [(t["w_out"][l, :, h * BCOL:(h + 1) * BCOL].rearrange("(b p) n -> p b n", p=P), 0)]))
        for e in range(NE):
            b.append((f"gate{e}", [(t["exp_w_gate"][l, e].rearrange("(p k) f -> p k f", k=KD), 0)]))
            b.append((f"up{e}", [(t["exp_w_up"][l, e].rearrange("(p k) f -> p k f", k=KD), 0)]))
            b.append((f"down{e}", [(t["exp_w_down"][l, e].rearrange("(p b) n -> p b n", b=FB), 0)]))
        return b

    order = [(l, name, parts) for l in range(L) for name, parts in blocks(l)]
    index = {(l, name): n for n, (l, name, _) in enumerate(order)}
    slot_of, before, landed = [], [], []
    seen, holds, at = [0] * (NSLOT + MORE), [None] * (NSLOT + MORE), 0
    for n, (l, name, parts) in enumerate(order):
        if name == "gate0":
            cycle = [(at + i) % NSLOT for i in range(NSLOT)] + [NSLOT + i for i in range(MORE)]
            at = 0
        elif name == "rw0":
            cycle, at = list(range(NSLOT)), min(range(0, NSLOT, 2), key=lambda b: holds[b]) if l else 0
        for _ in range(2):
            slot = cycle[at]
            at = (at + 1) % len(cycle)
            seen[slot] += 16 * len(parts)
            slot_of.append(slot)
            before.append(holds[slot])
            landed.append(seen[slot])
            holds[slot] = len(slot_of) - 1

    rows, n_rows = {}, 0
    for name, per in (("ssd_conv_w", TAPS * XB), ("ssd_conv_b", XB), ("rwkv_mu", 8), ("rwkv_w0", 2), ("rwkv_a0", 2),
                      ("rwkv_k_k", 2), ("rwkv_k_a", 2), ("rwkv_r_k", 2), ("gla_b_alpha", 2), ("ssd_norm_g", 4),
                      ("gla_norm_g", 1)):
        rows[name] = (n_rows, per)
        n_rows += L * per

    with ExitStack() as ctx:
        def sb(name, shape, dt=F32):
            return ctx.enter_context(nc.sbuf_tensor(name, shape, dt))

        class Signal:

            def __init__(self, name, per=1):
                self.sem, self.per, self.given = ctx.enter_context(nc.semaphore(name)), per, 0

            def __call__(self, l, n=None):
                return self.sem, l * self.per + (self.per if n is None else n)

        class Chain:

            def __init__(self, name):
                self.sem, self.n = ctx.enter_context(nc.semaphore(name)), 0

            def add(self, ins):
                ins.then_inc(self.sem, 1)
                self.n += 1

            def join(self, eng):
                eng.wait_ge(self.sem, self.n)

        bank = [ctx.enter_context(nc.psum_tensor(f"bank{i}", [P, 512], F32)) for i in range(8)]

        ring = sb("ring", [P, NSLOT, 4, BCOL])
        x_tm = sb("x_rows", [P, TT, D])
        x_cm = sb("x_cm", [P, KD, S])
        ident = sb("ident", [P, P])
        ident2 = sb("ident2", [P, HD])
        head_ones = sb("head_ones", [P, P])
        tri_incl = sb("tri_incl", [P, P])
        tri_after = sb("tri_after", [P, P])
        chunk_mask = sb("chunk_mask", [P, 2, P])
        level_mask = sb("level_mask", [P, 6, P])
        level0_tm = sb("level0_tm", [P, P])
        scan_reset = sb("scan_reset", [P, S])
        vec_rows = sb("vec_rows", [P, P])
        vec = sb("vec", [P, n_rows])
        om_mu = sb("om_mu", [P, L * 8])
        om_ka = sb("om_ka", [P, L * 2])
        neg_w0 = sb("neg_w0", [P, L * 2])
        neg_a0 = sb("neg_a0", [P, L * 2])
        lr_w = sb("lr_w", [P, L, RW])
        g2_w = sb("g2_w", [P, L, RW])
        alpha_w = sb("alpha_w", [RANK, L, GW])
        rout_w = sb("rout_w", [P, KD, NE])
        rout_b = sb("rout_b", [P, NE])
        ln_vec = sb("ln_vec", [P, 2, D])
        ssd_small = sb("ssd_small", [P, 3, L, SH])
        unit_gain = sb("unit_gain", [P, 1])
        ln_shift = sb("ln_shift", [P, 1])
        eps_ln = sb("eps_ln", [P, 1])
        eps_gn = sb("eps_gn", [P, 1])
        rms_s = sb("rms_s", [P, TT, 2])
        bn6 = sb("bn6", [P, TT, 2, 6])
        bn2 = sb("bn2", [P, TT, 2])
        rt = sb("rt", [P, 6, TT, NE])
        rg = sb("rg", [P, 4, TT, NG])
        gate = sb("gate", [P, TT, NE])
        place = sb("place", [P, 2, EPG * EPG])
        tri_before = sb("tri_before", [P, P])
        all_ones = sb("all_ones", [P, P])
        slot_row = sb("slot_row", [P, P])
        gate_r = sb("gate_r", [P, TT, NE, 2], mybir.dt.float32r)
        ident_r = sb("ident_r", [P, P], mybir.dt.float32r)
        ident2_r = sb("ident2_r", [P, HD], mybir.dt.float32r)
        pos = sb("pos", [P, TT, NE])
        crowded = sb("crowded", [P, 1], mybir.dt.int32)

        mixers = ExitStack()

        def mx(name, shape):
            return mixers.enter_context(nc.sbuf_tensor(name, shape, F32))

        heads = mx("heads", [P, TT, D])
        gn_vec = mx("gn_vec", [P, 2, RW])
        gla_q = mx("gla_q", [P, 2, S])
        gla_k = mx("gla_k", [P, 2, S])
        gla_kt = mx("gla_kt", [P, TT, GW])
        gla_vg = mx("gla_vg", [P, TT, 2 * GW])
        z_tm = mx("z_rows", [P, TT, SW])
        xbc = mx("xbc", [P, XB, S])
        alr = mx("alr", [RANK, S])
        dt = mx("dt", [P, TT, SH])
        da = mx("da", [P, TT, SH])
        dte = mx("dte", [P, 4, SH])
        big = mx("big", [P, 16 * S])
        rwc = big[:, 0:8 * S].rearrange("p (b s) -> p b s", b=8)
        fac = [big[:, (8 + 2 * i) * S:(10 + 2 * i) * S].rearrange("p (b s) -> p b s", b=2) for i in range(4)]
        gmat = big[:].rearrange("p (t h x y s) -> p t h x y s", t=TT, h=NH, x=2, y=2)
        sc = [mx(f"sc{i}", [P, 2, S]) for i in range(4)]
        tmq = mx("tmq", [P, TT, 3, RW])
        a_w1 = mx("a_w1", [P, TT, NH, 2, HD])
        b_cm = mx("b_cm", [P, 2, S])
        k_cm = mx("k_cm", [P, 2, S])
        ar_cm = mx("ar_cm", [P, 2, 2, S])
        anchor = mx("anchor", [P, 2, 3, NC])
        anchor_g = mx("anchor_g", [P, 2, 3, NC])
        inv = mx("inv", [P, TT, NH, P])
        inv_t = mx("inv_t", [P, TT, NH, P])
        lvl = mx("lvl", [P, TT, NH, P])
        tm_t = mx("tm_t", [P, 2, 2, HD])
        g_tm = mx("g_rows", [P, TT, RW])
        st_rw = mx("st_rw", [P, 2, NC, HD])
        st_gla = mx("st_gla", [P, 2, NC, HD])
        st_ssd = mx("st_ssd", [P, 4 * HD])
        bonus = mx("bonus", [P, TT, NH])
        b_tm = mx("b_tm", [P, P])
        gn = mx("gn", [P, 2, TT, NH])
        rms = mx("rms", [P, TT, NH])
        mixers.close()

        F32R = mybir.dt.float32r
        w_hi = [sb(f"w_hi{i}", [P, 2, BCOL], F32R) for i in range(NW)]
        w_lo = [sb(f"w_lo{i}", [P, 2, BCOL], F32R) for i in range(NW)]
        ring_more = sb("ring_more", [P, MORE, 4, BCOL])
        x_hi = sb("x_hi", [P, TT, D], F32R)
        x_lo = sb("x_lo", [P, TT, D], F32R)
        xg = [sb(f"xg{i}", [P, KD, 2, 2, SL], F32R) for i in range(2)]
        pick = [sb(f"pick{i}", [P, TT, 2, 2, SL], F32R) for i in range(2)]
        pick_t = sb("pick_t", [P, S], F32R)
        gu_hi = sb("gu_hi", [P, 2, BCOL], F32R)
        gu_lo = sb("gu_lo", [P, 2, BCOL], F32R)
        he_t = x_cm[:, 0:2].rearrange("p k s -> p (k s)").rearrange("p (b a s) -> p b a s", b=FB, a=2)
        act_g = x_cm[:, 2].rearrange("p (b s) -> p b s", b=FB)
        he_r = gu_lo[:, 1].rearrange("p (b a s) -> p b a s", b=FB, a=2)
        y_lo = sb("y_lo", [P, BCOL], F32R)
        y_st = sb("y_st", [P, D], F32R)
        g_slot = sb("g_slot", [P, 1])

        slot_full = [ctx.enter_context(nc.semaphore(f"slot_full{i}")) for i in range(NSLOT + MORE)]
        x_loaded = ctx.enter_context(nc.semaphore("x_loaded"))
        rows_loaded = ctx.enter_context(nc.semaphore("rows_loaded"))
        small_loaded = ctx.enter_context(nc.semaphore("small_loaded"))
        ln_loaded = Signal("ln_loaded", 2 * 32)
        gn_loaded = Signal("gn_loaded", 32)
        stored = ctx.enter_context(nc.semaphore("stored"))
        masks_done = ctx.enter_context(nc.semaphore("masks_done"))
        s_small = ctx.enter_context(nc.semaphore("s_small"))
        rows_zero = ctx.enter_context(nc.semaphore("rows_zero"))
        pool_step = ctx.enter_context(nc.semaphore("pool_step"))
        vec_turned = ctx.enter_context(nc.semaphore("vec_turned"))
        vec_ready = ctx.enter_context(nc.semaphore("vec_ready"))
        SIG = {}
        STEPS = dict(t_gather=0.5, t_pick=1, t_use=10, t_sum=1, t_scat=1,
                     v_pick=1, v_gslot=1, v_gate=1, v_up=1, v_he=1, v_hi=1, v_hl=1, v_xlo_g=1, v_y=2,
                     s_whi=10, s_gate=1, s_up=1, s_silu=1, s_xhi_g=1, s_pick_t=1, s_y=2)
        for name, per in dict(
                t_x=4, t_x1=8, t_proj=14, t_lowrank=4, t_turned=5, t_pair=8, t_ltm=2, t_mv=2, t_lp=10, t_inv=10, t_xa=2,
                t_q=1, t_carry=1, t_srw=3, t_yrw=1, t_glaz=1, t_ssd_tm=3, t_edge=1, t_cb=1, t_seg=4, t_yssd=3,
                t_sssd=1, t_gkt=1, t_gsc=2, t_sgla=1, t_ygla=1, t_cat=4, t_mix=4, t_route=1, t_slots=1, t_down=NE,
                t_down_more=NE * (ROUNDS - 1),
                v_proj=8, v_gates=2, v_ssmax=1, v_decay=1, v_ratio=1, v_bonus=1, v_kcm=1, v_bcm=1, v_rcm=1,
                v_pair=8, v_inv0=2, v_lvl=10, v_inv=10, v_q=1, v_carry=1, v_srw=3, v_gz=1, v_gcum=1, v_gqk=1,
                v_dt=1, v_da=1, v_lhs=4, v_w=4, v_xdt=2, v_xw=1, v_sssd=1, v_yssd=2,
                v_gsc=2, v_sgla=3, v_gnvar=1, v_glasum=1, v_heads=3, v_var=4, v_x1=2, v_logit=1,
                v_sel=1, v_flag=1, v_xlo=2, v_wlo=8 * NE, v_wlo_more=8 * NE * (ROUNDS - 1),
                v_dlo=2 * NE, v_dlo_more=2 * NE * (ROUNDS - 1), v_x2=2,
                s_x=4, s_x1=8, s_route=1, s_mu=4, s_conv=3, s_low=2, s_sq=1, s_ez=1, s_ea=1, s_g=1, s_norm=1,
                s_e=3, s_turned=5,
                s_mv=2, s_lp=10, s_xa=2, s_qk=2, s_vg=2, s_z=2, s_gln=1, s_ge=1, s_silx=3, s_dtl=1, s_seg=4,
                s_edge=1, s_xs=3, s_rssd=2, s_gnr=1, s_rgla=1, s_cat=8, s_rstd=4, s_xhi=2, s_expl=1).items():
            SIG[name] = Signal(name, per)
        for name, per in STEPS.items():
            SIG[name] = Signal(name, int(per * ROUNDS * NE))

        def done(name, l, n=None):
            assert n is None or 1 <= n <= SIG[name].per
            return SIG[name](l, n)

        def slot_ap(slot):
            return ring[:, slot] if slot < NSLOT else ring_more[:, slot - NSLOT]

        def inc(ins, name, by=1):
            SIG[name].given += by
            return ins.then_inc(SIG[name].sem, by)

        def last_use(l, name, h):
            kind = name.rstrip("0123456789")
            e = int(name[len(kind):] or 0)
            n = {"rw": 2 * e + 2, "xbc": 2 * e + 6, "qk": 10, "vg": 12, "z": 14, "out": e + 3,
                 "gate": 8 * e + 2 * h + 2, "up": 8 * e + 2 * h + 6, "down": e + 1 if h else 2 * e + 2}[kind]
            return {"out": "t_mix", "gate": "v_wlo", "up": "v_wlo", "down": "t_down" if h else "v_dlo"}.get(kind, "t_proj"), l, n

        def vcol(name, l, b):
            at, per = rows[name]
            return vec[:, at + l * per + b:at + l * per + b + 1]

        def halves(h):
            return slice(HALF * (h % 2), HALF * (h % 2) + HALF), h // 2

        def tile_(j):
            return slice(P * j, P * j + P)

        def each(ap, n):
            return ap.unsqueeze(1).to_broadcast([P, n, ap.shape[-1]])

        def wide(ap, n):
            return ap.unsqueeze(2).to_broadcast([P, ap.shape[1], n])

        V, A, T, G = nc.vector, nc.scalar, nc.tensor, nc.gpsimd
        block = ctx.enter_context(nc.Block())

        CROWD = SL + 0.5
        b_gate, b_up, b_xg, b_y = bank[4], bank[5], (bank[6], bank[7]), (bank[7], bank[6])

        def two_ways(eng, l, emit):
            eng.wait_ge(*done("v_flag", l))
            flag = eng.value_load(crowded[0:1, 0:1], min_val=0, max_val=1)
            for rounds, value in ((1, 0), (ROUNDS, 1)):
                with eng.If(flag == value):
                    emit(rounds)

        class Steps:

            def __init__(self, l, rounds):
                self.l, self.rounds = l, rounds

            def at(self, name, n):
                return done(name, self.l, n * (ROUNDS // self.rounds))

            def mark(self, ins, name):
                return inc(ins, name, ROUNDS // self.rounds)

            def last_round(self, name, n, per, i):
                e, r = divmod(n, self.rounds)
                if r == self.rounds - 1:
                    return name, e * per + i
                return name + "_more", (e * (ROUNDS - 1) + r) * per + i

            def at_last(self, name, n, per, i):
                which, value = self.last_round(name, n, per, i)
                return done(which, self.l, value)

            def mark_last(self, ins, name, n, per, i):
                return inc(ins, self.last_round(name, n, per, i)[0])

            def skip(self, eng, name):
                if self.rounds == 1:
                    eng.sem_inc(SIG[name].sem, SIG[name].per)

        def experts_t(pe, l, rounds):
            N, st = NE * rounds, Steps(l, rounds)
            at, mark = st.at, st.mark
            _, split_at = split_order(N)

            def hidden(n, half):
                b = (b_gate, b_up)[half]
                if half == 0:
                    pe.wait_ge(*at("s_xhi_g", n // 2 * 2 + 2))
                    pe.wait_ge(*at("v_xlo_g", n // 2 * 2 + 2))
                    if n:
                        pe.wait_ge(*at("s_pick_t", n))
                        pe.wait_ge(*at("v_gslot", n))
                elif n:
                    pe.wait_ge(*at("v_he", n))
                for q in range(4):
                    at_q = split_at["up" if half else "gate", n, q]
                    pe.wait_ge(*at("s_whi", at_q + 1))
                    pe.wait_ge(*st.at_last("v_wlo", n, 8, 4 * half + q + 1))
                    i = at_q % NW
                    for k in range(2):
                        kk = 2 * q + k
                        x = xg[n // 2 % 2][:, kk, n % 2].rearrange("p a s -> p (a s)")
                        T.matmul(b[:], x, w_hi[i][:, k, :], start=(kk == 0), stop=False)
                        m = T.matmul(b[:], x, w_lo[i][:, k, :], start=False, stop=(kk == KD - 1))
                    mark(m, "t_use")

            def gather(n):
                if n >= 4:
                    pe.wait_ge(*at("v_y", 2 * n - 4))
                pe.wait_ge(*at("v_pick", n + 2))
                for k in range(KD):
                    for j in range(TT):
                        for x in (x_hi, x_lo):
                            m = T.matmul(b_xg[k // 4][:, (k % 4) * P:(k % 4) * P + P], x[:, j, k::KD],
                                         pick[n // 2 % 2][:, j, :, 0, :],
                                         start=(j == 0 and x is x_hi), stop=(j == TT - 1 and x is x_lo))
                mark(m, "t_gather")

            def down(n):
                pe.wait_ge(*at("v_he", n + 1))
                for hf in range(2):
                    g = (n + 4) // 2 * 2
                    if hf == 0 and g <= N:
                        pe.wait_ge(*at("s_xhi_g", g))
                        pe.wait_ge(*at("v_xlo_g", g))
                    if n:
                        pe.wait_ge(*at("v_y", 2 * n - 1 + hf))
                    if hf == 0:
                        pe.wait_ge(*at("v_hl", n + 1))
                        for q in range(2):
                            at_q = split_at["down", n, q]
                            pe.wait_ge(*at("s_whi", at_q + 1))
                            pe.wait_ge(*st.at_last("v_dlo", n, 2, q + 1))
                            for fb in (2 * q, 2 * q + 1):
                                h_ = he_r[:, fb].rearrange("p a s -> p (a s)")
                                T.matmul(b_y[0][:], h_, w_hi[at_q % NW][:, fb % 2, :], start=(fb == 0), stop=False)
                                m = T.matmul(b_y[0][:], h_, w_lo[at_q % NW][:, fb % 2, :], start=False, stop=(fb == FB - 1))
                            mark(m, "t_use")
                        continue
                    q = 2 * index[l, f"down{n // rounds}"] + 1
                    pe.wait_ge(slot_full[slot_of[q]], landed[q])
                    for fb in range(FB):
                        m = T.matmul(b_y[1][:], he_t[:, fb].rearrange("p a s -> p (a s)"), slot_ap(slot_of[q])[:, fb, :],
                                     start=(fb == 0), stop=(fb == FB - 1))
                    st.mark_last(m, "t_down", n, 1, 1)

            def scatter(n):
                for hf in range(2):
                    pe.wait_ge(*at("v_y", 2 * n + hf + 1))
                    parts = (y_st[:, 0:BCOL], y_lo[:]) if hf == 0 else (y_st[:, BCOL:],)
                    for j in range(TT):
                        for i, y in enumerate(parts):
                            m = T.matmul(bank[2 * j + hf][:], pick_t[:, tile_(j)], y, start=(n == 0 and i == 0),
                                         stop=(n == N - 1 and i == len(parts) - 1))
                mark(m, "t_scat")

            def turn_pick(n):
                pe.wait_ge(*at("s_gate", n + 1))
                pe.wait_ge(*at("v_gate", n + 1))
                p_ = [pick[n // 2 % 2][:, j, n % 2].rearrange("p a s -> p (a s)") for j in range(TT)]
                for j in range(TT):
                    T.matmul(b_gate[:, tile_(j)], p_[j], ident_r[:], start=True, stop=True)
                for j in range(TT):
                    m = T.matmul(b_gate[:, S:S + 2], p_[j], gate_r[:, j, n // rounds], start=(j == 0), stop=(j == TT - 1))
                mark(m, "t_pick")

            def sum_halves(n):
                pe.wait_ge(*at("s_up", n + 1))
                pe.wait_ge(*at("v_up", n + 1))
                for i in range(2):
                    for fb in range(FB):
                        for gu in (gu_hi, gu_lo):
                            m = T.matmul(b_up[:, (i * FB + fb) * SL:(i * FB + fb) * SL + SL], gu[:, i, fb::FB],
                                         ident2_r[:], start=(gu is gu_hi), stop=(gu is gu_lo))
                mark(m, "t_sum")

            pe.wait_ge(*done("s_xhi", l))
            pe.wait_ge(*done("v_xlo", l))
            gather(0)
            for n in range(N):
                hidden(n, 0)
                if n:
                    down(n - 1)
                hidden(n, 1)
                if n:
                    scatter(n - 1)
                turn_pick(n)
                if n % 2 == 0 and n + 2 < N:
                    gather(n + 2)
                sum_halves(n)
            down(N - 1)
            scatter(N - 1)
            st.skip(pe, "t_down_more")

        def gathered(i):
            return b_xg[i][:].rearrange("p (k e s) -> p k e s", k=4, e=2)

        def split_order(N):
            split_list = []
            for n in range(N + 1):
                if n < N:
                    split_list += [("gate", n, i) for i in range(4)]
                if n:
                    split_list += [("down", n - 1, i) for i in range(2)]
                if n < N:
                    split_list += [("up", n, i) for i in range(4)]
            return split_list, {q: i for i, q in enumerate(split_list)}

        def quarter(l, kind, n, i, rounds):
            b = 2 * index[l, f"{kind}{n // rounds}"] + i // 2
            return b, slot_ap(slot_of[b])[:, 2 * (i % 2):2 * (i % 2) + 2]

        def experts_s(act, l, rounds):
            N, st = NE * rounds, Steps(l, rounds)
            at, mark = st.at, st.mark
            split_list, split_at = split_order(N)

            def w_split(q):
                if q >= len(split_list):
                    return
                if q >= NW:
                    act.wait_ge(*at("t_use", q - NW + 1))
                b, w = quarter(l, *split_list[q], rounds)
                act.wait_ge(slot_full[slot_of[b]], landed[b])
                mark(A.activation(w_hi[q % NW][:], w, ACT.Copy), "s_whi")

            def x_split(n):
                act.wait_ge(*at("t_gather", n // 2 + 1))
                for i in range(2):
                    mark(A.activation(xg[n // 2 % 2][:, 4 * i:4 * i + 4, :, 0], gathered(i), ACT.Copy), "s_xhi_g")

            def y_split(n):
                act.wait_ge(*at("v_gslot", n + 1))
                for hf in range(2):
                    if hf == 0:
                        act.wait_ge(*at("t_use", split_at["down", n, 1] + 1))
                    else:
                        act.wait_ge(*st.at_last("t_down", n, 1, 1))
                    if n:
                        act.wait_ge(*at("t_scat", n))
                    mark(A.activation(y_st[:, hf * BCOL:hf * BCOL + BCOL], b_y[hf][:], ACT.Copy, scale=g_slot[:]), "s_y")

            def take_pick(n):
                act.wait_ge(*at("t_pick", n + 1))
                if n:
                    act.wait_ge(*at("t_scat", n))
                mark(A.activation(pick_t[:], b_gate[:, 0:S], ACT.Copy), "s_pick_t")

            def splits(n, *which):
                for i in which:
                    w_split(split_at["gate", n, 0] + NW + i)

            for q in range(NW):
                w_split(q)
            x_split(0)
            for n in range(N):
                splits(n, 0, 1, 2)
                act.wait_ge(*at("t_use", split_at["gate", n, 3] + 1))
                mark(A.activation(gu_hi[:, 0], b_gate[:], ACT.Copy), "s_gate")
                splits(n, 3)
                if n:
                    splits(n, 4, 5)
                    y_split(n - 1)
                k = 6 if n else 4
                splits(n, k, k + 1)
                act.wait_ge(*at("t_use", split_at["up", n, 3] + 1))
                mark(A.activation(gu_hi[:, 1], b_up[:], ACT.Copy), "s_up")
                splits(n, k + 2)
                take_pick(n)
                splits(n, k + 3)
                if n % 2 == 0 and n + 2 < N:
                    x_split(n + 2)
                act.wait_ge(*at("t_sum", n + 1))
                mark(A.activation(act_g[:], b_up[:, 0:FB * SL].rearrange("p (b s) -> p b s", b=FB), ACT.Silu), "s_silu")
            y_split(N - 1)

        def experts_v(dve, l, rounds):
            N, st = NE * rounds, Steps(l, rounds)
            at, mark = st.at, st.mark
            split_list, split_at = split_order(N)

            def w_split(q):
                if q >= len(split_list):
                    return
                kind, n, i = split_list[q]
                b, w = quarter(l, kind, n, i, rounds)
                dve.wait_ge(*at("s_whi", q + 1))
                ins = V.tensor_tensor(w_lo[q % NW][:], w, w_hi[q % NW][:].bitcast(F32), ALU.subtract)
                if kind == "down":
                    st.mark_last(ins, "v_dlo", n, 2, i + 1)
                else:
                    st.mark_last(ins, "v_wlo", n, 8, i + (5 if kind == "up" else 1))

            def x_split(n):
                for i in range(2):
                    x = xg[n // 2 % 2][:, 4 * i:4 * i + 4]
                    dve.wait_ge(*at("s_xhi_g", n + i + 1))
                    mark(V.tensor_tensor(x[:, :, :, 1], gathered(i), x[:, :, :, 0].bitcast(F32), ALU.subtract), "v_xlo_g")

            def y_split(n):
                dve.wait_ge(*at("s_y", 2 * n + 1))
                if n:
                    dve.wait_ge(*at("t_scat", n))
                mark(V.scalar_tensor_tensor(out=y_lo[:], in0=b_y[0][:], scalar=g_slot[:], in1=y_st[:, 0:BCOL].bitcast(F32),
                                            op0=ALU.mult, op1=ALU.subtract), "v_y")
                dve.wait_ge(*at("s_y", 2 * n + 2))
                mark(V.scalar_tensor_tensor(out=y_st[SL:P, BCOL:], in0=b_y[1][SL:P], scalar=g_slot[SL:P],
                                            in1=y_st[SL:P, BCOL:].bitcast(F32), op0=ALU.mult, op1=ALU.subtract), "v_y")

            def picks(n):
                if n >= 4:
                    dve.wait_ge(*at("t_pick", n - 2))
                for i in range(2):
                    e, r = divmod(n + i, rounds)
                    for j in range(TT):
                        m = V.tensor_scalar(pick[n // 2 % 2][:, j, i], slot_row[:].rearrange("p (a s) -> p a s", a=2),
                                            float(SL * r), pos[:, j, e:e + 1], ALU.add, ALU.is_equal)
                    mark(m, "v_pick")

            def slots_gate(n):
                dve.wait_ge(*at("s_pick_t", n + 1))
                if n:
                    dve.wait_ge(*at("s_y", 2 * n))
                    dve.wait_ge(*at("v_y", 2 * n))
                mark(V.tensor_reduce(g_slot[:], b_gate[:, S:S + 2], AX.X, ALU.add), "v_gslot")

            def low(i, b, n, name):
                dve.wait_ge(*at("s_" + name, n + 1))
                mark(V.tensor_tensor(gu_lo[:, i], b[:], gu_hi[:, i].bitcast(F32), ALU.subtract), "v_" + name)

            def splits(n, *which):
                for i in which:
                    w_split(split_at["gate", n, 0] + NW + i)

            picks(0)
            for q in range(NW):
                w_split(q)
            x_split(0)
            for n in range(N):
                splits(n, 0, 1, 2)
                low(0, b_gate, n, "gate")
                splits(n, 3)
                if n:
                    splits(n, 4, 5)
                if n % 2 == 0 and n + 2 < N:
                    picks(n + 2)
                if n:
                    dve.wait_ge(*at("v_gslot", n))
                    y_split(n - 1)
                k = 6 if n else 4
                splits(n, k, k + 1)
                low(1, b_up, n, "up")
                splits(n, k + 2)
                slots_gate(n)
                splits(n, k + 3)
                if n % 2 == 0 and n + 2 < N:
                    x_split(n + 2)
                dve.wait_ge(*at("s_silu", n + 1))
                mark(V.tensor_tensor(he_t[:], act_g[:].unsqueeze(2).to_broadcast([P, FB, 2, SL]),
                                     b_up[:, FB * SL:].rearrange("p (b s) -> p b s", b=FB).unsqueeze(2)
                                     .to_broadcast([P, FB, 2, SL]), ALU.mult), "v_he")
                dve.wait_ge(*at("v_he", n + 1))
                mark(V.tensor_copy(he_r[:, :, 0], he_t[:, :, 0]), "v_hi")
                dve.wait_ge(*at("v_hi", n + 1))
                mark(V.tensor_tensor(he_r[:, :, 1], he_t[:, :, 0], he_r[:, :, 0].bitcast(F32), ALU.subtract), "v_hl")
            dve.wait_ge(*at("v_gslot", N))
            y_split(N - 1)
            st.skip(dve, "v_wlo_more")
            st.skip(dve, "v_dlo_more")



        def seg_in(q, i):
            return sc[q][:].rearrange("p b s -> p (b s)")[:, tile_(i)]

        def seg_w4(q):
            return (lvl, inv)[q // 2][:, q % 2]

        def seg_w(q, i):
            return seg_w4(q)[:, i, :]

        def xdt(j):
            return inv_t[:, j].rearrange("p h s -> p (h s)")

        xw = b_cm[:].rearrange("p b s -> p (b s)")

        def gsc4(j):
            return sc[j][:].rearrange("p b s -> p (b s)").rearrange("p (h s) -> p h s", h=NH)

        def gsc(j, h):
            return gsc4(j)[:, h, :]

        def cat_gain(l, b):
            return vcol("gla_norm_g", l, 0) if b < 2 else vcol("ssd_norm_g", l, b - 2) if b < 6 else unit_gain[:]
        @block.sync
        def _(sp):
            for j in range(TT):
                sp.dma_start(x_tm[:, j, :], t["x"][0, tile_(j), :]).then_inc(x_loaded, 16)
            def load_rows():
                sp.wait_ge(rows_zero, 1)
                for name, (at, per) in rows.items():
                    src = t[name]
                    if name == "gla_norm_g":
                        for h in range(2):
                            sp.dma_start(vec_rows[at:at + L, h * HD:(h + 1) * HD], src).then_inc(rows_loaded, 16)
                        continue
                    if name == "ssd_conv_w":
                        flat = src.rearrange("l k (b p) -> (l k b) p", p=P)
                    elif name == "rwkv_r_k":
                        flat = src.rearrange("l (b h) n -> (l b) (h n)", h=2)
                    else:
                        flat = src.rearrange("l (b p) -> (l b) p", p=P)
                    sp.dma_start(vec_rows[at:at + L * per, :], flat).then_inc(rows_loaded, 16)

            for n, (l, name, parts) in enumerate(order):
                if n == 1:
                    load_rows()
                for h in range(2):
                    q = 2 * n + h
                    slot = slot_of[q]
                    if before[q] is not None:
                        sp.wait_ge(*done(*last_use(*order[before[q] // 2][:2], before[q] % 2)))
                    if slot >= NSLOT and (before[q] is None or order[before[q] // 2][0] < l):
                        sp.wait_ge(*done("s_xhi", l))
                    for src, c in parts:
                        if name.startswith("down"):
                            src = src[:, :, h * BCOL:h * BCOL + BCOL]
                        else:
                            src = src[:, 4 * h:4 * h + 4]
                        sp.dma_start(slot_ap(slot)[:, :, c:c + src.shape[2]], src).then_inc(slot_full[slot], 16)
            sp.wait_ge(*done("v_x2", L - 1))
            for j in range(TT):
                sp.dma_start(out[0, tile_(j), :], x_tm[:, j, :]).then_inc(stored, 16)
            sp.wait_ge(stored, 16 * TT)

        @block.gpsimd
        def _(pool):
            n = 0

            def step(ins):
                nonlocal n
                ins.then_inc(pool_step, 1)
                n += 1
                pool.wait_ge(pool_step, n)

            def keep(ap, base, pattern, mult, op=ALU.is_ge):
                step(G.affine_select(out=ap, in_=ap, compare_op=op, fill=0.0, base=base, pattern=pattern,
                                     channel_multiplier=mult))

            G.memset(vec_rows[:], 0.0).then_inc(rows_zero, 1)
            step(G.memset(ident[:], 1.0))
            keep(ident[:], 0, [[-1, P]], 1)
            keep(ident[:], 0, [[1, P]], -1)
            step(G.memset(place[:], 1.0))
            for i, sign in enumerate((1, -1)):
                keep(place[:, i].rearrange("p (a b) -> p a b", a=EPG), -1, [[sign, EPG], [-sign, EPG]], 0)
            for m in (ident2, head_ones, tri_incl, tri_after, tri_before, all_ones, chunk_mask, level_mask, level0_tm,
                      scan_reset):
                one = 0.0 if m is level_mask else 1.0
                step(G.memset(m[:], one))
            for h in range(2):
                keep(ident2[HALF * h:HALF * h + HALF, :], 0, [[-1, HD]], 1)
                keep(ident2[HALF * h:HALF * h + HALF, :], 0, [[1, HD]], -1)
            halves2 = head_ones[:].rearrange("p (b c) -> p b c", b=2)
            keep(halves2, 0, [[-HALF, 2], [0, HALF]], 1)
            keep(halves2, HALF - 1, [[HALF, 2], [0, HALF]], -1)
            step(G.tensor_copy(ident_r[:], ident[:]))
            step(G.tensor_copy(ident2_r[:], ident2[:]))
            keep(tri_incl[:], 0, [[1, P]], -1)
            keep(tri_after[:], -1, [[-1, P]], 1)
            keep(tri_before[:], -1, [[1, P]], -1)
            step(G.iota(slot_row[:].rearrange("p (a s) -> p a s", a=2), [[0, 2], [1, SL]], base=0,
                        channel_multiplier=0, allow_small_or_imprecise_dtypes=True))
            for i in range(2):
                m = chunk_mask[:, i, :].rearrange("p (b c) -> p b c", b=2)
                keep(m, 0, [[-CH, 2], [0, CH]], 1)
                keep(m, i - 1, [[CH, 2], [1, CH]], -1)
            for j in range(6):
                m, nb = 2 ** j, P // 2 ** (j + 1)
                v = level_mask[:, j, :].rearrange("p (b h i) -> p b h i", h=2, i=m)[:, :, 1, :]
                step(G.memset(v, 1.0))
                keep(v, 0, [[-2 * m, nb], [0, m]], 1)
                keep(v, m - 1, [[2 * m, nb], [0, m]], -1)
            v = level0_tm[:].rearrange("p (b h) -> p b h", h=2)
            step(G.memset(v[:, :, 1], 0.0))
            keep(v[:, :, 0], -1, [[-2, P // 2]], 1)
            keep(v[:, :, 0], 1, [[2, P // 2]], -1)
            step(G.memset(scan_reset[:].rearrange("p (c i) -> p c i", i=CH)[:, :, 0], 0.0))
            for ap, value in ((ln_shift, 15 * float(np.log(2.0))), (eps_ln, EPS), (eps_gn, GN_EPS)):
                step(G.memset(ap[:], value))
            G.memset(unit_gain[:], 1.0).then_inc(masks_done, 1)
            for l in range(L):
                if l:
                    pool.wait_ge(*done("v_x2", l - 1))
                for which in range(2):
                    if which:
                        pool.wait_ge(*done("v_x1", l))
                    for i, name in enumerate(("ln1_g", "ln1_b") if which == 0 else ("ln2_g", "ln2_b")):
                        pool.dma_start(ln_vec[:, i, :], t[name][l].partition_broadcast(P)).then_inc(ln_loaded.sem, 16)
                    if which == 0:
                        for i, name in enumerate(("rwkv_ln_g", "rwkv_ln_b")):
                            pool.dma_start(gn_vec[:, i, :], t[name][l].partition_broadcast(P)) \
                                .then_inc(gn_loaded.sem, 16)

        @block.tensor
        def _(pe):
            def weights(l, name):
                a = 2 * index[l, name]
                for q in (a, a + 1):
                    pe.wait_ge(slot_full[slot_of[q]], landed[q])
                return ring[:, slot_of[a]:slot_of[a] + 2].rearrange("p h k n -> p (h k) n")

            rows_chain = Chain("t_rows")

            def rows_done(m):
                rows_chain.add(m)
                rows_chain.join(pe)

            def turn_tile(j, name):
                for i in range(4):
                    for k in (2 * i, 2 * i + 1):
                        m = T.transpose(bank[i][:, (k % 2) * S + P * j:(k % 2) * S + P * j + P], x_tm[:, j, k::KD], ident[:])
                    if name == "t_x1" or j == TT - 1:
                        inc(m, name)

            def turn_x(l):
                for j in range(TT):
                    if l:
                        pe.wait_ge(*done("v_x2", l - 1, j + 1))
                    turn_tile(j, "t_x")

            def project(l, i):
                if i < 2:
                    pass
                elif i - 2 < 8:
                    pe.wait_ge(*done("v_proj", l, i - 1))
                else:
                    pe.wait_ge(*done(("s_qk", "s_qk", "s_vg", "v_gnvar")[i - 10], l, (1, 2, 1, 1)[i - 10]))
                dst = bank[i % 2 if i < 13 else 5]
                name = ("rw0", "rw0", "rw1", "rw1", "xbc0", "xbc0", "xbc1", "xbc1", "qk", "qk", "vg", "vg", "z", "z")[i]
                w = weights(l, name)

                def cm(out_, c, n):
                    for k in range(KD):
                        m = T.matmul(out_, w[:, k, c:c + n], x_cm[:, k, :], start=(k == 0), stop=(k == KD - 1))
                    return m

                def tm(out_, j, c, n):
                    for k in range(KD):
                        m = T.matmul(out_, x_cm[:, k, tile_(j)], w[:, k, c:c + n], start=(k == 0), stop=(k == KD - 1))
                    return m

                if i == 7:
                    c = XBC - BCOL
                    cm(dst[0:RANK, 0:S], c + SH, RANK)
                    for j in range(TT):
                        m = tm(dst[:, S + SH * j:S + SH * j + SH], j, c, SH)
                elif i < 10:
                    for b in range(2):
                        m = cm(dst[:, b * S:b * S + S], (2 * (i % 2) + b) * P if i != 6 else b * P, P)
                else:
                    m = tm(dst[:], i % 2, 0, BCOL)
                inc(m, "t_proj")

            for l in range(L):
                def proj(i):
                    project(l, i)

                if l == 0:
                    pe.wait_ge(x_loaded, 16 * TT)
                    pe.wait_ge(pool_step, 3)
                    turn_x(0)
                pe.wait_ge(*done("s_x", l))
                for i in range(4):
                    proj(i)
                    if l == 0 and i == 0:
                        pe.wait_ge(rows_loaded, 16 * (len(rows) + 1))
                        T.transpose(bank[4][:, 0:P], vec_rows[:], ident[:]).then_inc(vec_turned, 1)
                if l == 0:
                    pe.wait_ge(masks_done, 1)
                    pe.wait_ge(small_loaded, 16 * (6 + 3 * L))
                proj(4)
                pe.wait_ge(*done("v_gates", l, 1))
                for b in range(2):
                    m = T.matmul(bank[2][:, b * S:b * S + S], lr_w[0:HALF, l, b * P:b * P + P],
                                 fac[3][0:HALF, 0, :], start=True, stop=True)
                inc(m, "t_lowrank")
                for b in range(2):
                    m = T.matmul(bank[3][:, b * S:b * S + S], lr_w[HALF:P, l, b * P:b * P + P],
                                 rwc[HALF:P, 6, :], start=True, stop=True)
                inc(m, "t_lowrank")
                pe.wait_ge(*done("v_gates", l, 2))
                for j in range(TT):
                    m = T.matmul(bank[4][:, j * RW:j * RW + RW], fac[3][:, 1, tile_(j)], g2_w[:, l, :],
                                 start=True, stop=True)
                inc(m, "t_lowrank")
                pe.wait_ge(*done("s_sq", l))
                inc(T.matmul(bank[5][:], head_ones[:], fac[2], start=True, stop=True), "t_lowrank")
                for i in (5, 6, 7):
                    proj(i)
                proj(8)
                pe.wait_ge(*done("v_ssmax", l))
                pe.wait_ge(*done("v_proj", l, 8))
                for b in range(2):
                    m = T.matmul(bank[5][:, b * S:b * S + S], alpha_w[:, l, b * P:b * P + P], alr[:],
                                 start=True, stop=True)
                inc(m, "t_glaz")
                for j in range(TT):
                    for b in range(2):
                        m = T.transpose(bank[6][:, j * RW + b * P:j * RW + b * P + P], rwc[:, 4 + b, tile_(j)], ident[:])
                inc(m, "t_turned")
                pe.wait_ge(*done("v_bonus", l))
                pe.wait_ge(*done("s_g", l))
                for j in range(TT):
                    for b in range(2):
                        m = T.matmul(bank[4][:, j * NH + 2 * b:j * NH + 2 * b + 2], fac[0][:, b, tile_(j)],
                                     head_ones[:, 0:P:HALF], start=True, stop=True)
                inc(m, "t_turned")
                for src, dst, ready in ((ar_cm[:, :, 0, :], bank[7], "v_ratio"), (k_cm, bank[3], "v_kcm"),
                                        (b_cm, bank[2], "v_bcm")):
                    pe.wait_ge(*done(ready, l))
                    for j in range(TT):
                        for b in range(2):
                            m = T.transpose(dst[:, j * RW + b * P:j * RW + b * P + P], src[:, b, tile_(j)], ident[:])
                    inc(m, "t_turned")
                proj(9)
                pe.wait_ge(*done("v_rcm", l))
                for u in range(TT * NH):
                    j, h = divmod(u, NH)
                    ps, b = halves(h)
                    if u < 2:
                        pe.wait_ge(*done("s_turned", l, 3))
                    else:
                        pe.wait_ge(*done("v_pair", l, u - 1))
                    for i, src in enumerate((b_cm, k_cm)):
                        m = T.matmul(bank[6 + u % 2][:, 2 * P * i:2 * P * i + 2 * P], src[ps, b, tile_(j)],
                                     ar_cm[ps, b, :, tile_(j)], start=True, stop=True)
                    inc(m, "t_pair")
                pe.wait_ge(*done("s_turned", l, 5))
                for par in range(2):
                    for j in range(TT):
                        for h in (par, par + 2):
                            ps, b = halves(h)
                            m = T.matmul(bank[2 + j][:, tile_(h)], ar_cm[ps, b, 0, tile_(j)], b_cm[ps, b, tile_(j)],
                                         start=True, stop=True)
                        if par:
                            inc(m, "t_ltm")
                    if not par:
                        rows_done(m)
                for j in range(TT):
                    pe.wait_ge(*done("v_pair", l, NH * (j + 1)))
                    for h in range(NH):
                        m = T.matmul(bank[4][:, j * RW + h * HD:j * RW + h * HD + HD], gmat[:, j, h, 1, 0, :],
                                     tmq[:, j, 2, h * HD:h * HD + HD], start=True, stop=True)
                    inc(m, "t_mv")
                proj(10)
                for lev in range(5):
                    for j in range(TT):
                        n = lev * TT + j
                        pe.wait_ge(*done("v_lvl", l, n + 1))
                        if lev == 0:
                            pe.wait_ge(*done("v_inv0", l, j + 1))
                        else:
                            pe.wait_ge(*done("v_inv", l, n - 1))
                        for h in range(NH):
                            m = T.matmul(bank[2 + j][:, tile_(h)], lvl[:, j, h, :], inv[:, j, h, :], start=True, stop=True)
                        inc(m, "t_lp")
                    if lev == 0:
                        proj(11)
                    for j in range(TT):
                        n = lev * TT + j
                        pe.wait_ge(*done("s_lp", l, n + 1))
                        if lev == 0:
                            pe.wait_ge(*done("s_mv", l, j + 1))
                            pe.wait_ge(*done("v_gz", l))
                        for h in range(NH):
                            m = T.matmul(bank[4 + j][:, tile_(h)], lvl[:, j, h, :], inv_t[:, j, h, :], start=True, stop=True)
                        if lev < 4:
                            for h in range(NH):
                                m = T.matmul(bank[6 + j][:, tile_(h)], inv_t[:, j, h, :], lvl[:, j, h, :],
                                             start=True, stop=True)
                        inc(m, "t_inv")
                for j in range(TT):
                    pe.wait_ge(*done("v_inv", l, 9 + j))
                    for h in range(NH):
                        m = T.matmul(bank[2 + j][:, tile_(h)], inv_t[:, j, h, :],
                                     a_w1[:, j, h].rearrange("p a b -> p (a b)"), start=True, stop=True)
                    inc(m, "t_xa")
                proj(12)
                pe.wait_ge(*done("s_xa", l))
                for h in range(NH):
                    ps, b = halves(h)
                    for j in range(TT):
                        m = T.matmul(bank[4][ps, (j * 2 + b) * P:(j * 2 + b) * P + P], a_w1[:, j, h, 0, :],
                                     gmat[:, j, h, 0, 1, :], start=True, stop=True)
                inc(m, "t_q")
                for c in (1, 2):
                    pc, j = halves(c)
                    for h in range(NH):
                        ps, b = halves(h)
                        m = T.matmul(bank[6][ps, (b * 2 + c - 1) * HD:(b * 2 + c) * HD], a_w1[pc, j, h, 0, :],
                                     tmq[pc, j, 0, h * HD:h * HD + HD], start=True, stop=True)
                    if c == 1:
                        rows_done(m)
                inc(m, "t_carry")
                for j in range(TT):
                    for h in range(NH):
                        o = bank[5][:, j * RW + h * HD:j * RW + h * HD + HD]
                        T.matmul(o, gmat[:, j, h, 0, 1, :], a_w1[:, j, h, 1, :], start=(j == 0 and h == 0), stop=False,
                                 skip_group_check=True)
                        T.matmul(o, gmat[:, j, h, 1, 1, :], tmq[:, j, 2, h * HD:h * HD + HD], start=False, stop=False,
                                 skip_group_check=True)
                def carried(c, h):
                    ps, b = halves(h)
                    return bank[7][ps, (c * 2 + b) * HD:(c * 2 + b) * HD + HD]

                for c in (0, 2, 1):
                    pc, j = halves(c)
                    for h in range(NH):
                        hs = slice(h * HD, h * HD + HD)
                        T.matmul(carried(c, h), tmq[pc, j, 0, hs], a_w1[pc, j, h, 1, :], start=(c == 0 and h < 2), stop=False,
                                 skip_group_check=True)
                        m = T.matmul(carried(c, h), tmq[pc, j, 1, hs], tmq[pc, j, 2, hs], start=False, stop=(c == 0),
                                     skip_group_check=True)
                    if c == 1:
                        inc(m, "t_srw")
                    else:
                        rows_done(m)
                pe.wait_ge(*done("v_carry", l))
                for c in (1, 2):
                    pe.wait_ge(*done("v_srw", l, c))
                    for par in range(2):
                        for h in (par, par + 2):
                            ps, b = halves(h)
                            m = T.matmul(carried(c, h), tm_t[ps, b, c - 1, :], st_rw[ps, b, c, :], start=False, stop=True,
                                         skip_group_check=True)
                        if not par:
                            rows_done(m)
                    inc(m, "t_srw")
                pe.wait_ge(*done("v_q", l))
                pe.wait_ge(*done("v_srw", l))

                def from_state(q, st, name):
                    for par in range(2):
                        for c in range(1, NC):
                            pc, j = halves(c)
                            for h in (par, par + 2):
                                ps, b = halves(h)
                                m = T.matmul(bank[5][pc, j * RW + h * HD:j * RW + h * HD + HD],
                                             q[ps, b, c * CH:c * CH + CH], st[ps, b, c, :], start=False,
                                             stop=(c == NC - 1), skip_group_check=True)
                        if not par:
                            rows_done(m)
                    inc(m, name)

                from_state(ar_cm[:, :, 1, :], st_rw, "t_yrw")

                pe.wait_ge(*done("s_z", l, 1))
                pe.wait_ge(*done("s_silx", l))
                for j in range(TT):
                    for b in range(4):
                        m = T.transpose(bank[j][:, tile_(b)], xbc[:, b, tile_(j)], ident[:])
                    inc(m, "t_ssd_tm")
                inc(T.transpose(bank[2][:, 0:P], xbc[:, 4, tile_(0)], ident[:]), "t_ssd_tm")
                pe.wait_ge(*done("v_da", l))
                T.matmul(bank[2][:, 2 * P:2 * P + SH], tri_after[:], da[:, 0, :], start=True, stop=True)
                inc(T.matmul(bank[2][:, 2 * P + SH:2 * P + 2 * SH], tri_incl[:], da[:, 1, :], start=True, stop=True), "t_edge")
                for g in range(2):
                    ps = slice(HALF * g, HALF * g + HALF)
                    for j in range(TT):
                        m = T.matmul(bank[3][:, (j * 2 + g) * P:(j * 2 + g) * P + P], xbc[ps, 4, tile_(j)],
                                     xbc[ps, 5, tile_(j)], start=True, stop=True)
                    if g == 0:
                        rows_done(m)
                inc(m, "t_cb")
                for q in range(4):
                    pe.wait_ge(*done("v_lhs", l, q + 1))
                    if q == 3:
                        pe.wait_ge(*done("s_seg", l, 1))
                    dst = bank[(4, 6, 7, 4)[q]]
                    for i in range(4):
                        m = T.matmul(dst[:, tile_(i)], seg_in(q, i), tri_incl[:], start=True, stop=True)
                    inc(m, "t_seg")
                proj(13)
                for j in range(TT):
                    pe.wait_ge(*done("v_w", l, 2 * j + 2))
                    pe.wait_ge(*done("s_xs", l, j + 1))
                    pe.wait_ge(*done("v_xdt", l, j + 1))
                    for h in range(SH):
                        m = T.matmul(bank[j][:, h * HD:h * HD + HD], seg_w(2 * j + h // 4, h % 4),
                                     xdt(j)[:, h * HD:h * HD + HD], start=True, stop=True)
                    inc(m, "t_yssd")
                pe.wait_ge(*done("v_xw", l))
                pe.wait_ge(*done("s_xs", l, 3))
                pe.wait_ge(*done("s_edge", l))
                for g in range(2):
                    ps = slice(HALF * g, HALF * g + HALF)
                    m = T.matmul(bank[2][ps, 0:4 * HD], b_tm[:, ps], xw[:, 4 * HD * g:4 * HD * g + 4 * HD],
                                 start=True, stop=True)
                inc(m, "t_sssd")
                pe.wait_ge(*done("v_sssd", l))
                pe.wait_ge(*done("s_seg", l, 2))
                for g in range(2):
                    ps = slice(HALF * g, HALF * g + HALF)
                    m = T.matmul(bank[6][:, 4 * HD * g:4 * HD * g + 4 * HD], xbc[ps, 5, tile_(1)], st_ssd[ps, :],
                                 start=True, stop=True)
                    if g == 0:
                        rows_done(m)
                inc(m, "t_yssd")

                pe.wait_ge(*done("v_gqk", l))
                pe.wait_ge(*done("v_w", l))
                for j in range(TT):
                    for b in range(2):
                        m = T.transpose(bank[3][:, j * GW + b * P:j * GW + b * P + P], gla_k[:, b, tile_(j)], ident[:])
                inc(m, "t_gkt")
                pe.wait_ge(*done("s_seg", l))
                for par in range(2):
                    for j in range(TT):
                        for h in (par, par + 2):
                            ps, b = halves(h)
                            m = T.matmul(bank[(4, 7)[j]][:, tile_(h)], gla_k[ps, b, tile_(j)], gla_q[ps, b, tile_(j)],
                                         start=True, stop=True)
                        if par:
                            inc(m, "t_gsc")
                    if not par:
                        rows_done(m)
                pe.wait_ge(*done("s_gln", l))
                for c in range(NC - 1):
                    pc, j = halves(c)
                    for h in range(NH):
                        ps, b = halves(h)
                        hs = slice(h * HD, h * HD + HD)
                        m = T.matmul(bank[2][ps, (c * 2 + b) * HD:(c * 2 + b) * HD + HD], gla_kt[pc, j, hs],
                                     gla_vg[pc, j, hs], start=True, stop=True)
                    if c < NC - 2:
                        rows_done(m)
                inc(m, "t_sgla")
                pe.wait_ge(*done("s_z", l))
                for j in range(TT):
                    pe.wait_ge(*done("v_gsc", l, j + 1))
                    for h in range(NH):
                        hs = slice(h * HD, h * HD + HD)
                        T.matmul(bank[5][:, j * GW + h * HD:j * GW + h * HD + HD], gsc(j, h), gla_vg[:, j, hs],
                                 start=(j == 0 and h == 0), stop=False, skip_group_check=True)
                pe.wait_ge(*done("v_sgla", l))
                from_state(gla_q, st_gla, "t_ygla")

                def heads_cm(i):
                    for b in (2 * i, 2 * i + 1):
                        for j in range(TT):
                            m = T.transpose(bank[i][:, (b % 2) * S + P * j:(b % 2) * S + P * j + P],
                                            heads[:, j, b * P:b * P + P], ident[:])
                    inc(m, "t_cat")

                def mix(j, hf, part):
                    w = weights(l, f"out{hf}")
                    for b in part:
                        m = T.matmul(bank[4 + 2 * hf + j][:], x_cm[:, b, tile_(j)], w[:, b, :], start=(b == 2),
                                     stop=(b == 1))
                    if b == 1:
                        inc(m, "t_mix")

                pe.wait_ge(*done("v_heads", l, 1))
                heads_cm(3)
                pe.wait_ge(*done("v_heads", l, 2))
                heads_cm(1)
                heads_cm(2)
                pe.wait_ge(*done("s_cat", l, 6))
                mix(0, 0, range(2, KD))
                pe.wait_ge(*done("v_heads", l, 3))
                heads_cm(0)
                mix(0, 1, range(2, KD))
                pe.wait_ge(*done("s_cat", l, 8))
                mix(0, 0, range(2))
                mix(0, 1, range(2))
                for hf in range(2):
                    mix(1, hf, [*range(2, KD), 0, 1])
                for j in range(TT):
                    pe.wait_ge(*done("v_x1", l, j + 1))
                    turn_tile(j, "t_x1")
                    pe.wait_ge(*done("s_x1", l, 4 * j + 4))
                    for k in range(KD):
                        m = T.matmul(bank[4][:, j * NE:j * NE + NE], x_cm[:, k, tile_(j)], rout_w[:, k, :],
                                     start=(k == 0), stop=(k == KD - 1))
                inc(m, "t_route")
                pe.wait_ge(*done("v_sel", l))
                sel = rt[:, 3]
                T.matmul(bank[5][:, 0:NE], tri_before[:], sel[:, 0], start=True, stop=True)
                T.matmul(bank[5][:, NE:2 * NE], tri_before[:], sel[:, 1], start=True, stop=False)
                T.matmul(bank[5][:, NE:2 * NE], all_ones[:], sel[:, 0], start=False, stop=True)
                T.matmul(bank[5][:, 2 * NE:3 * NE], all_ones[:], sel[:, 0], start=True, stop=False)
                inc(T.matmul(bank[5][:, 2 * NE:3 * NE], all_ones[:], sel[:, 1], start=False, stop=True), "t_slots")
                two_ways(pe, l, lambda rounds: experts_t(pe, l, rounds))
                if l < L - 1:
                    turn_x(l + 1)

        E_HALF = float(np.exp(-0.5))

        def conv_taps(l, i):
            for b in range(2):
                blk = 2 * (i - 4) + b
                for tap in range(TAPS - 1):
                    s = TAPS - 1 - tap
                    yield (xbc[:, blk, s:], bank[i % 2][:, b * S:b * S + S - s], vcol("ssd_conv_w", l, tap * XB + blk))

        @block.vector
        def _(dve):
            c = Chain("v_chain")

            def do(ins):
                c.add(ins)
                c.join(dve)

            def recip1(ap, plus=True):
                do(V.tensor_scalar(ap, ap, 1.0, None, ALU.add))
                return V.reciprocal(ap, ap)

            dve.wait_ge(vec_turned, 1)
            c.add(V.tensor_copy(vec[:], bank[4][:, 0:n_rows]))
            dve.wait_ge(small_loaded, 16 * (6 + 3 * L))
            c.join(dve)
            for dst, name, sc_, off in ((om_mu, "rwkv_mu", -1.0, 1.0), (om_ka, "rwkv_k_a", -1.0, 1.0),
                                        (neg_w0, "rwkv_w0", -1.0, 0.0), (neg_a0, "rwkv_a0", -1.0, 0.0)):
                at, per = rows[name]
                c.add(V.tensor_scalar(dst[:], vec[:, at:at + L * per], sc_, off, ALU.mult, ALU.add))
            c.join(dve)
            dve.wait_ge(s_small, 1)
            V.tensor_scalar(ssd_small[:, 1], ssd_small[:, 1], -1.0, None, ALU.mult).then_inc(vec_ready, 1)
            dve.wait_ge(vec_ready, 1)

            def cat(p):
                return p.rearrange("p b s -> p (b s)")

            def anchors(cum, an):
                v = cum.rearrange("p b (c i) -> p b c i", i=CH)
                do(V.tensor_copy(an[:, :, 0, :], v[:, :, :, CH // 2 - 1]))
                do(V.tensor_tensor(an[:, :, 1, :], v[:, :, :, CH - 1], an[:, :, 0, :], ALU.subtract))
                c.add(V.tensor_tensor(an[:, :, 2, 0:NC - 1], an[:, :, 1, 0:NC - 1], an[:, :, 0, 1:NC], ALU.add))
                do(V.tensor_copy(an[:, :, 2, NC - 1:NC], an[:, :, 1, NC - 1:NC]))

            def minus_anchor(out_, cum, an):
                for b in range(2):
                    i = V.tensor_tensor(out_[:, b].rearrange("p (c i) -> p c i", i=CH),
                                        cum[:, b].rearrange("p (c i) -> p c i", i=CH),
                                        wide(an[:, b, 0, :], CH), ALU.subtract)
                    if b == 0:
                        c.add(i)
                return i

            def low_part_of(l, j):
                dve.wait_ge(*done("s_xhi", l, j + 1))
                inc(V.tensor_tensor(x_lo[:, j], x_tm[:, j], x_hi[:, j].bitcast(F32), ALU.subtract), "v_xlo")

            def layer_norm(l, which):
                def moments(j):
                    for hf in range(2):
                        if which == 0:
                            dve.wait_ge(*done("t_mix", l, 2 * j + hf + 1))
                        else:
                            dve.wait_ge(*done("t_scat", l))
                        cs = slice(hf * 512, hf * 512 + 512)
                        do(V.scalar_tensor_tensor(out=x_tm[:, j, cs], in0=x_tm[:, j, cs], scalar=ALPHA,
                                                  in1=bank[4 + 2 * hf + j if which == 0 else 2 * j + hf][:],
                                                  op0=ALU.mult, op1=ALU.add))
                        c.add(V.bn_stats(bn6[:, j, hf, :], x_tm[:, j, cs]))
                    c.join(dve)
                    inc(V.bn_aggr(bn2[:, j, :], bn6[:, j].rearrange("p a b -> p (a b)")), "v_var")

                def normalize(j):
                    dve.wait_ge(ln_loaded.sem, 64 * l + 32 * (which + 1))
                    dve.wait_ge(*done("v_var", l, 2 * which + j + 1))
                    do(V.scalar_tensor_tensor(out=x_tm[:, j], in0=x_tm[:, j], scalar=bn2[:, j, 0:1], in1=ln_vec[:, 0],
                                              op0=ALU.subtract, op1=ALU.mult))
                    dve.wait_ge(*done("s_rstd", l, 2 * which + j + 1))
                    inc(V.scalar_tensor_tensor(out=x_tm[:, j], in0=x_tm[:, j], scalar=bn2[:, j, 1:2], in1=ln_vec[:, 1],
                                               op0=ALU.mult, op1=ALU.add), "v_x1" if which == 0 else "v_x2")

                if which == 0:
                    for j in range(TT):
                        moments(j)
                        normalize(j)
                        low_part_of(l, j)
                else:
                    for part in (moments, normalize):
                        for j in range(TT):
                            part(j)

            for l in range(L):
                for i in range(4):
                    dve.wait_ge(*done("s_mu", l, i + 1))
                    for b in range(2):
                        k = 2 * i + b
                        ins = V.scalar_tensor_tensor(out=rwc[:, k, 1:], in0=bank[i % 2][:, b * S:b * S + S - 1],
                                                     scalar=vcol("rwkv_mu", l, k), in1=rwc[:, k, 1:],
                                                     op0=ALU.mult, op1=ALU.add)
                        if b == 0:
                            c.add(ins)
                    c.join(dve)
                    inc(ins, "v_proj")
                dve.wait_ge(*done("v_proj", l, 4))
                if l == 0:
                    dve.wait_ge(masks_done, 1)
                dve.wait_ge(*done("s_low", l, 1))
                th = fac[3][0:HALF, 0, :]
                do(recip1(th))
                inc(V.tensor_scalar(th, th, 2.0, -1.0, ALU.mult, ALU.add), "v_gates")
                dve.wait_ge(*done("s_low", l, 2))
                inc(recip1(fac[3][:, 1, :]), "v_gates")

                def conv(i):
                    dve.wait_ge(*done("s_conv", l, i - 3))
                    for n, (o, p, w) in enumerate(conv_taps(l, i)):
                        if n % 3:
                            c.join(dve)
                        ins = V.scalar_tensor_tensor(out=o, in0=p, scalar=w, in1=o, op0=ALU.mult, op1=ALU.add)
                        if n < 5:
                            c.add(ins)
                    c.join(dve)
                    inc(ins, "v_proj")

                conv(4)
                dve.wait_ge(*done("t_lowrank", l, 4))
                inc(V.tensor_scalar(cat(fac[2]), bank[5][:], 1e-24, None, ALU.max), "v_ssmax")
                dve.wait_ge(*done("s_ez", l))
                do(recip1(cat(fac[0])))
                do(V.tensor_scalar(cat(fac[0]), cat(fac[0]), -E_HALF, None, ALU.mult))
                dve.wait_ge(*done("t_lowrank", l, 3))
                for b in range(2):
                    c.add(V.tensor_tensor_scan(fac[3][:, b], scan_reset[:], fac[0][:, b], 0.0, ALU.mult, ALU.add))
                c.join(dve)
                anchors(fac[3], anchor)
                do(minus_anchor(fac[3], fac[3], anchor))
                inc(V.tensor_tensor(cat(fac[0]), cat(fac[3]), cat(fac[0]), ALU.subtract), "v_decay")
                conv(5)
                dve.wait_ge(*done("s_ea", l))
                do(recip1(cat(fac[1])))
                dve.wait_ge(*done("s_norm", l))
                for b in range(2):
                    c.add(V.scalar_tensor_tensor(out=fac[2][:, b], in0=rwc[:, 2 + b], scalar=vcol("rwkv_k_k", l, b),
                                                 in1=fac[2][:, b], op0=ALU.mult, op1=ALU.mult))
                c.join(dve)
                dve.wait_ge(*done("s_e", l, 1))
                inc(V.scalar_tensor_tensor(out=ar_cm[:, :, 0, :], in0=fac[2], scalar=-1.0, in1=fac[0],
                                           op0=ALU.mult, op1=ALU.mult), "v_ratio")
                conv(6)
                dve.wait_ge(*done("v_ratio", l))
                for b in range(2):
                    c.add(V.tensor_scalar(fac[0][:, b], fac[1][:, b], vcol("rwkv_k_a", l, b),
                                          om_ka[:, l * 2 + b:l * 2 + b + 1], ALU.mult, ALU.add))
                c.join(dve)
                do(V.tensor_tensor(rwc[:, 2:4], rwc[:, 2:4], fac[0], ALU.mult))
                for b in range(2):
                    ins = V.scalar_tensor_tensor(out=fac[0][:, b], in0=rwc[:, b], scalar=vcol("rwkv_r_k", l, b),
                                                 in1=rwc[:, 2 + b], op0=ALU.mult, op1=ALU.mult)
                    if b == 0:
                        c.add(ins)
                c.join(dve)
                inc(ins, "v_bonus")
                dve.wait_ge(*done("t_proj", l, 8))
                c.add(V.tensor_copy(alr[:], bank[1][0:RANK, 0:S]))
                ins = V.tensor_tensor(dt[:], bank[1][:, S:S + TT * SH].rearrange("p (j h) -> p j h", j=TT),
                                      each(ssd_small[:, 0, l, :], TT), ALU.add)
                c.join(dve)
                inc(ins, "v_proj")
                do(V.tensor_tensor(fac[1], fac[2], fac[1], ALU.mult))
                dve.wait_ge(*done("s_e", l, 2))
                inc(V.tensor_tensor(k_cm[:], rwc[:, 2:4], b_cm[:], ALU.mult), "v_kcm")
                dve.wait_ge(*done("v_kcm", l))
                inc(V.tensor_tensor(b_cm[:], fac[1], b_cm[:], ALU.mult), "v_bcm")
                dve.wait_ge(*done("s_e", l, 3))
                inc(V.tensor_tensor(ar_cm[:, :, 1, :], rwc[:, 0:2], fac[3], ALU.mult), "v_rcm")
                dve.wait_ge(*done("t_glaz", l))
                for b in range(2):
                    ins = V.tensor_scalar(sc[1][:, b], bank[5][:, b * S:b * S + S], vcol("gla_b_alpha", l, b), None, ALU.add)
                inc(ins, "v_gz")

                for u in range(TT * NH):
                    j, h = divmod(u, NH)
                    dve.wait_ge(*done("t_pair", l, u + 1))
                    inc(V.tensor_tensor(gmat[:, j, h].rearrange("p x y s -> p x (y s)"),
                                        bank[6 + u % 2][:].rearrange("p (x z) -> p x z", x=2),
                                        each(chunk_mask[:].rearrange("p y s -> p (y s)"), 2), ALU.mult), "v_pair")
                for j in range(TT):
                    dve.wait_ge(*done("v_pair", l, NH * (j + 1)))
                    c.add(V.tensor_tensor(inv_t[:, j], gmat[:, j, :, 0, 0, :], each(level_mask[:, 0, :], NH), ALU.mult))
                    inc(V.tensor_tensor(lvl[:, j], gmat[:, j, :, 0, 0, :], each(level_mask[:, 1, :], NH), ALU.mult), "v_lvl")
                    dve.wait_ge(*done("t_ltm", l, j + 1))
                    do(V.tensor_tensor(inv[:, j], bank[2 + j][:].rearrange("p (h s) -> p h s", h=NH),
                                       each(level0_tm[:], NH), ALU.mult))
                    do(V.tensor_tensor(inv_t[:, j], inv_t[:, j], each(ident[:], NH), ALU.add))
                    inc(V.tensor_tensor(inv[:, j], inv[:, j], each(ident[:], NH), ALU.add), "v_inv0")

                def gla_cum():
                    dve.wait_ge(*done("s_ge", l))
                    do(V.scalar_tensor_tensor(out=cat(sc[1][:]), in0=cat(sc[1][:]), scalar=0.0, in1=cat(sc[2][:]),
                                              op0=ALU.min, op1=ALU.subtract))
                    for b in range(2):
                        c.add(V.tensor_tensor_scan(sc[3][:, b], scan_reset[:], sc[1][:, b], 0.0, ALU.mult, ALU.add))
                    c.join(dve)
                    anchors(sc[3][:], anchor_g)
                    inc(minus_anchor(sc[3], sc[3], anchor_g), "v_gcum")

                def gla_qk():
                    dve.wait_ge(*done("s_expl", l))
                    dve.wait_ge(*done("s_qk", l))
                    c.add(V.scalar_tensor_tensor(out=cat(gla_q[:]), in0=cat(gla_q[:]), scalar=HD ** -0.5,
                                                 in1=cat(sc[2][:]), op0=ALU.mult, op1=ALU.mult))
                    ins = V.tensor_tensor(cat(gla_k[:]), cat(gla_k[:]), cat(sc[3][:]), ALU.mult)
                    c.join(dve)
                    inc(ins, "v_gqk")

                def ssd_dt():
                    dve.wait_ge(*done("s_dtl", l))
                    inc(V.scalar_tensor_tensor(out=dt[:], in0=dt[:], scalar=0.0, in1=dte[:, 0:2], op0=ALU.max,
                                               op1=ALU.add), "v_dt")
                    dve.wait_ge(*done("v_dt", l))
                    inc(V.tensor_tensor(da[:], dt[:], each(ssd_small[:, 1, l, :], TT), ALU.mult), "v_da")

                def seg_operands():
                    for q in range(4):
                        if q == 0:
                            dve.wait_ge(*done("v_gqk", l))
                            dve.wait_ge(*done("v_da", l))
                        for i in range(4):
                            j, h = q // 2, 4 * (q % 2) + i
                            ins = V.tensor_scalar(seg_in(q, i), tri_after[:], da[:, j, h:h + 1], None, ALU.mult)
                            if i < 3:
                                c.add(ins)
                        c.join(dve)
                        inc(ins, "v_lhs")

                gla_cum()
                fill = [ssd_dt, gla_qk, seg_operands]
                for lev in range(5):
                    for j in range(TT):
                        n = lev * TT + j
                        dve.wait_ge(*done("t_inv", l, n + 1))
                        if lev < 4:
                            c.add(V.tensor_tensor(inv[:, j], inv[:, j],
                                                  bank[6 + j][:].rearrange("p (h s) -> p h s", h=NH), ALU.add))
                        ins = V.tensor_tensor(inv_t[:, j], inv_t[:, j],
                                              bank[4 + j][:].rearrange("p (h s) -> p h s", h=NH), ALU.add)
                        c.join(dve)
                        inc(ins, "v_inv")
                        if lev < 4:
                            inc(V.tensor_tensor(lvl[:, j], gmat[:, j, :, 0, 0, :],
                                                each(level_mask[:, lev + 2, :], NH), ALU.mult), "v_lvl")
                    if fill:
                        fill.pop(0)()
                for f in fill:
                    f()
                dve.wait_ge(*done("t_q", l))
                for j in range(TT):
                    ins = V.tensor_tensor(ar_cm[:, :, 1, tile_(j)], ar_cm[:, :, 1, tile_(j)],
                                          bank[4][:, j * S:j * S + S].rearrange("p (b s) -> p b s", b=2), ALU.add)
                    if j == 0:
                        c.add(ins)
                c.join(dve)
                inc(ins, "v_q")
                dve.wait_ge(*done("t_carry", l))
                inc(V.tensor_tensor(tm_t[:].rearrange("p b c n -> p (b c) n"),
                                    bank[6][:, 0:S].rearrange("p (b n) -> p b n", n=HD), each(ident2[:], 4), ALU.add), "v_carry")
                dve.wait_ge(*done("s_e", l, 3))
                for i in range(NC - 1):
                    dve.wait_ge(*done("t_srw", l, i + 1))
                    inc(V.tensor_tensor(st_rw[:, :, i + 1, :],
                                        bank[7][:, i * P:i * P + P].rearrange("p (b n) -> p b n", b=2),
                                        wide(anchor[:, :, 2, i], HD), ALU.mult), "v_srw")
                dve.wait_ge(*done("t_yrw", l))
                y = bank[5][:].rearrange("p (h n) -> p h n", n=HD)
                mean = gn[:, 0].rearrange("p j h -> p (j h)")
                dev = gn[:, 1].rearrange("p j h -> p (j h)")
                yc = big[:, 0:TT * RW].rearrange("p (h n) -> p h n", n=HD)
                sq = big[:, TT * RW:2 * TT * RW].rearrange("p (h n) -> p h n", n=HD)
                do(V.tensor_reduce(mean, y, AX.X, ALU.add))
                do(V.tensor_scalar(mean, mean, 1.0 / HD, None, ALU.mult))
                do(V.tensor_tensor(yc, y, wide(mean, HD), ALU.subtract))
                do(V.tensor_tensor(sq, yc, yc, ALU.mult))
                inc(V.tensor_reduce(dev, sq, AX.X, ALU.add), "v_gnvar")

                def group_norm_end():
                    dve.wait_ge(*done("s_gnr", l))
                    dve.wait_ge(gn_loaded.sem, 32 * (l + 1))
                    do(V.tensor_tensor(yc, yc, wide(dev, HD), ALU.mult))
                    for j in range(TT):
                        o = heads[:, j, GW + SW:]
                        yj = big[:, j * RW:j * RW + RW]
                        bv = big[:, (2 + j) * RW:(3 + j) * RW]
                        c.add(V.tensor_tensor(yj, yj, gn_vec[:, 0], ALU.mult))
                        do(V.tensor_tensor(bv.rearrange("p (h n) -> p h n", n=HD),
                                           tmq[:, j, 2, :].rearrange("p (h n) -> p h n", n=HD), wide(bonus[:, j, :], HD), ALU.mult))
                        do(V.tensor_tensor(yj, yj, gn_vec[:, 1], ALU.add))
                        do(V.tensor_tensor(yj, yj, bv, ALU.add))
                        ins = V.tensor_tensor(o, yj, g_tm[:, j], ALU.mult)
                        if j == 0:
                            c.add(ins)
                    c.join(dve)
                    inc(ins, "v_heads")

                dve.wait_ge(*done("t_cb", l))
                do(V.tensor_tensor(k_cm[:].rearrange("p a b -> p (a b)").rearrange("p (q s) -> p q s", q=4),
                                   bank[3][:].rearrange("p (q s) -> p q s", q=4), each(tri_incl[:], 4), ALU.mult))
                for j in range(TT):
                    dve.wait_ge(*done("s_xs", l, j + 1))
                    inc(V.tensor_tensor(xdt(j).rearrange("p (h n) -> p h n", n=HD),
                                        heads[:, j, GW:GW + SW].rearrange("p (h n) -> p h n", n=HD),
                                        wide(dt[:, j, :], HD), ALU.mult), "v_xdt")
                for q in range(4):
                    dve.wait_ge(*done("s_seg", l, q + 1))
                    cb = k_cm[:].rearrange("p a b -> p (a b)")[:, q * P:q * P + P]
                    inc(V.tensor_tensor(seg_w4(q), seg_w4(q), each(cb, 4), ALU.mult), "v_w")
                dve.wait_ge(*done("s_edge", l))
                dve.wait_ge(*done("v_xdt", l, 1))
                inc(V.tensor_tensor(xw.rearrange("p (h n) -> p h n", n=HD), xdt(0).rearrange("p (h n) -> p h n", n=HD),
                                    wide(dte[:, 2, :], HD), ALU.mult), "v_xw")
                group_norm_end()
                for j in range(TT):
                    oh = heads[:, j, GW:GW + SW].rearrange("p (h n) -> p h n", n=HD)
                    c.add(V.tensor_tensor(oh, oh, wide(ssd_small[:, 2, l, :], HD), ALU.mult))
                dve.wait_ge(*done("t_sssd", l))
                inc(V.tensor_copy(st_ssd[:], bank[2][:, 0:4 * HD]), "v_sssd")
                for j in range(TT):
                    dve.wait_ge(*done("s_z", l, j + 1))
                    zj, o = z_tm[:, j], heads[:, j, GW:GW + SW]
                    c.join(dve)
                    dve.wait_ge(*done("t_yssd", l, j + 1))
                    do(V.tensor_tensor(o, o, bank[j][:], ALU.add))
                    if j:
                        dve.wait_ge(*done("t_yssd", l, 3))
                        tmp = cat(sc[2][:])
                        do(V.tensor_tensor(tmp.rearrange("p (h n) -> p h n", n=HD),
                                           bank[6][:].rearrange("p (h n) -> p h n", n=HD), wide(dte[:, 3, :], HD), ALU.mult))
                        do(V.tensor_tensor(o, o, tmp, ALU.add))
                    inc(V.tensor_tensor(o, o, zj, ALU.mult), "v_yssd")
                dve.wait_ge(*done("t_seg", l))
                for j in range(TT):
                    dve.wait_ge(*done("t_gsc", l, j + 1))
                    inc(V.tensor_tensor(gsc4(j), bank[(4, 7)[j]][:].rearrange("p (h s) -> p h s", h=NH),
                                        each(chunk_mask[:, 1, :], NH), ALU.mult), "v_gsc")
                dve.wait_ge(*done("t_sgla", l))
                for i in range(NC - 1):
                    src = bank[2][:, i * P:i * P + P].rearrange("p (b n) -> p b n", b=2)
                    dst = st_gla[:, :, i + 1, :]
                    if i:
                        do(V.tensor_tensor(dst, src, st_gla[:, :, i, :], ALU.add))
                        src = dst
                    inc(V.tensor_tensor(dst, src, wide(anchor_g[:, :, 2, i], HD), ALU.mult), "v_sgla")
                    dve.wait_ge(*done("v_sgla", l, i + 1))
                for j in range(TT):
                    dve.wait_ge(*done("s_rssd", l, j + 1))
                    for g in range(2):
                        o = heads[:, j, GW + g * 256:GW + g * 256 + 256]
                        ins = V.tensor_scalar(o, o, rms_s[:, j, g:g + 1], None, ALU.mult)
                        if (j, g) != (1, 1):
                            c.add(ins)
                c.join(dve)
                inc(ins, "v_heads")
                dve.wait_ge(*done("t_ygla", l))
                do(V.tensor_copy(cat(sc[2][:]), bank[5][:]))
                do(V.tensor_tensor(cat(sc[3][:]), cat(sc[2][:]), cat(sc[2][:]), ALU.mult))
                rr = rms[:].rearrange("p j h -> p (j h)")
                inc(V.tensor_reduce(rr, cat(sc[3][:]).rearrange("p (h n) -> p h n", n=HD), AX.X, ALU.add), "v_glasum")
                dve.wait_ge(*done("s_rgla", l))
                yg = cat(sc[2][:]).rearrange("p (h n) -> p h n", n=HD)
                do(V.tensor_tensor(yg, yg, wide(rr, HD), ALU.mult))
                for j in range(TT):
                    ins = V.tensor_tensor(heads[:, j, 0:GW], sc[2][:, j], gla_vg[:, j, GW:], ALU.mult)
                    if j == 0:
                        c.add(ins)
                c.join(dve)
                inc(ins, "v_heads")
                layer_norm(l, 0)

                dve.wait_ge(*done("t_route", l))
                inc(V.tensor_copy(rt[:, 0].rearrange("p j e -> p (j e)"), bank[4][:, 0:TT * NE]), "v_logit")
                dve.wait_ge(*done("s_route", l))
                score, sel = rt[:, 1], rt[:, 2]
                do(recip1(score))
                do(V.tensor_tensor(sel, score, each(rout_b[:], TT), ALU.add))
                s4 = sel.rearrange("p j (g k) -> p (j g) k", k=EPG)
                pr = rt[:, 3:5].rearrange("p a j e -> p (a j e)")[:, 0:6 * TT * NG].rearrange("p (k m) -> p k m", k=6)
                n = 0
                for a in range(EPG):
                    for b in range(a + 1, EPG):
                        c.add(V.tensor_tensor(pr[:, n, :], s4[:, :, a], s4[:, :, b], ALU.add))
                        n += 1
                c.join(dve)
                gs = rg[:, 0].rearrange("p j g -> p (j g)")
                do(V.tensor_reduce(gs, pr.rearrange("p k m -> p m k"), AX.X, ALU.max))
                pairs = x_cm[:, 0:2]

                def ranks(out_, v, n, K):
                    shape = [P, n, K, K]
                    ge, gt = (pairs[:, i, 0:n * K * K].rearrange("p (m a b) -> p m a b", a=K, b=K) for i in range(2))
                    a_, b_ = v.unsqueeze(3).to_broadcast(shape), v.unsqueeze(2).to_broadcast(shape)
                    c.add(V.tensor_tensor(ge, b_, a_, ALU.is_ge))
                    do(V.tensor_tensor(gt, b_, a_, ALU.is_gt))
                    for x, m in ((ge, 0), (gt, 1)):
                        ins = V.tensor_tensor(x, x, place[:, m].rearrange("p (a b) -> p a b", a=K).unsqueeze(1)
                                              .to_broadcast(shape), ALU.mult)
                        c.add(ins)
                    c.join(dve)
                    do(V.tensor_tensor(ge, ge, gt, ALU.add))
                    do(V.tensor_reduce(out_, ge, AX.X, ALU.add))

                beat = rg[:, 1]
                rank = rt[:, 3]
                r4 = rank.rearrange("p j (g k) -> p (j g) k", k=EPG)
                ranks(beat, rg[:, 0], TT, NG)
                ranks(r4, s4, TT * NG, EPG)
                c.add(V.tensor_scalar(beat, beat, 0.5, None, ALU.is_lt))
                do(V.tensor_scalar(rank, rank, 1.5, None, ALU.is_lt))
                inc(V.tensor_tensor(r4, r4, wide(beat.rearrange("p j g -> p (j g)"), EPG), ALU.mult), "v_sel")
                dve.wait_ge(*done("v_sel", l))
                do(V.tensor_tensor(gate[:], rank, score, ALU.mult))
                do(V.tensor_reduce(rms_s[:, :, 0], gate[:], AX.X, ALU.add))
                do(V.reciprocal(rms_s[:, :, 0], rms_s[:, :, 0]))
                do(V.tensor_tensor(gate[:], gate[:], wide(rms_s[:, :, 0], NE), ALU.mult))

                c.add(V.tensor_copy(gate_r[:, :, :, 0], gate[:]))
                c.join(dve)
                do(V.tensor_tensor(gate_r[:, :, :, 1], gate[:], gate_r[:, :, :, 0].bitcast(F32), ALU.subtract))
                dve.wait_ge(*done("t_slots", l))
                do(V.tensor_scalar(pos[:], bank[5][:, 0:TT * NE].rearrange("p (j e) -> p j e", j=TT), 1.0, None, ALU.add))
                do(V.tensor_tensor(pos[:], pos[:], rank, ALU.mult))
                do(V.tensor_scalar(pos[:], pos[:], -1.0, None, ALU.add))
                do(V.tensor_reduce(rms_s[:, 0, 0:1], bank[5][:, 2 * NE:3 * NE], AX.X, ALU.max))
                inc(V.tensor_scalar(crowded[:], rms_s[:, 0, 0:1], CROWD, None, ALU.is_gt), "v_flag")
                two_ways(dve, l, lambda rounds: experts_v(dve, l, rounds))
                layer_norm(l, 1)


        @block.scalar
        def _(act):
            c = Chain("s_chain")

            def do(ins):
                c.add(ins)
                c.join(act)

            def flat(p):
                return p.rearrange("p b s -> p (b s)")

            small = [(lr_w[0:HALF], t["rwkv_w2"].rearrange("l r c -> r l c")),
                     (lr_w[HALF:P], t["rwkv_a2"].rearrange("l r c -> r l c")),
                     (g2_w[:], t["rwkv_g2"].rearrange("l r c -> r l c")),
                     (alpha_w[:], t["gla_w_alpha"].rearrange("l r c -> r l c")),
                     (rout_w[:], t["router_w"].rearrange("(p k) e -> p k e", k=KD)),
                     (rout_b[:], t["router_b"].partition_broadcast(P))]
            for i, name in enumerate(("ssd_dt_bias", "ssd_A_log", "ssd_D")):
                for l in range(L):
                    small.append((ssd_small[:, i, l, :], t[name][l].partition_broadcast(P)))
            for dst, src in small:
                act.dma_start(dst, src).then_inc(small_loaded, 16)
            A.preload_act_table_set("natural_log_exp_and_others")
            act.wait_ge(small_loaded, 16 * (6 + 3 * L))
            A.activation(ssd_small[:, 1], ssd_small[:, 1], ACT.Exp).then_inc(s_small, 1)
            for l in range(L):
                for i in range(4):
                    act.wait_ge(*done("t_x", l, i + 1))
                    inc(A.activation(x_cm[:, 2 * i:2 * i + 2, :], bank[i][:].rearrange("p (k s) -> p k s", k=2),
                                     ACT.Copy), "s_x")
                if l == 0:
                    act.wait_ge(vec_ready, 1)
                for i in range(4):
                    act.wait_ge(*done("t_proj", l, i + 1))
                    for b in range(2):
                        k = 2 * i + b
                        ins = A.activation(rwc[:, k, :], bank[i % 2][:, b * S:b * S + S], ACT.Copy,
                                           scale=om_mu[:, l * 8 + k:l * 8 + k + 1])
                    inc(ins, "s_mu")

                def conv(i):
                    act.wait_ge(*done("t_proj", l, i + 1))
                    for b in range(2):
                        blk = 2 * (i - 4) + b
                        ins = A.activation(xbc[:, blk, :], bank[i % 2][:, b * S:b * S + S], ACT.Identity,
                                           scale=vcol("ssd_conv_w", l, (TAPS - 1) * XB + blk), bias=vcol("ssd_conv_b", l, blk))
                    inc(ins, "s_conv")

                act.wait_ge(*done("v_proj", l, 4))
                inc(A.activation(fac[3][0:HALF, 0, :], rwc[0:HALF, 6, :], ACT.Exp, scale=-2.0), "s_low")
                inc(A.activation(fac[3][:, 1, :], rwc[:, 7, :], ACT.Exp, scale=-1.0), "s_low")
                for b in range(2):
                    ins = A.activation(fac[2][:, b], rwc[:, 2 + b], ACT.Square, scale=vcol("rwkv_k_k", l, b))
                inc(ins, "s_sq")
                conv(4)
                act.wait_ge(*done("t_lowrank", l, 1))
                for b in range(2):
                    ins = A.activation(fac[0][:, b], bank[2][:, b * S:b * S + S], ACT.Exp, scale=-1.0,
                                       bias=neg_w0[:, l * 2 + b:l * 2 + b + 1])
                inc(ins, "s_ez")
                act.wait_ge(*done("t_lowrank", l, 2))
                for b in range(2):
                    ins = A.activation(fac[1][:, b], bank[3][:, b * S:b * S + S], ACT.Exp, scale=-1.0,
                                       bias=neg_a0[:, l * 2 + b:l * 2 + b + 1])
                inc(ins, "s_ea")
                act.wait_ge(*done("t_lowrank", l, 3))
                inc(A.activation(g_tm[:], bank[4][:].rearrange("p (j c) -> p j c", j=TT), ACT.Copy), "s_g")
                if l == 0:
                    act.wait_ge(masks_done, 1)
                act.wait_ge(*done("v_ssmax", l))
                do(A.activation(flat(fac[2]), flat(fac[2]), ACT.Ln, scale=2.0 ** 30))
                inc(A.activation(flat(fac[2]), flat(fac[2]), ACT.Exp, scale=-0.5, bias=ln_shift[:]), "s_norm")
                conv(5)
                act.wait_ge(*done("v_decay", l))
                inc(A.activation(flat(fac[0]), flat(fac[0]), ACT.Exp), "s_e")
                inc(A.activation(b_cm[:], fac[3], ACT.Exp, scale=-1.0), "s_e")
                A.activation(anchor[:, :, 2, :], anchor[:, :, 2, :], ACT.Exp)
                inc(A.activation(flat(fac[3]), flat(fac[3]), ACT.Exp), "s_e")
                conv(6)
                act.wait_ge(*done("v_proj", l, 8))
                do(A.activation(dte[:, 0:2], dt[:], ACT.Abs))
                do(A.activation(dte[:, 0:2], dte[:, 0:2], ACT.Exp, scale=-1.0))
                inc(A.activation(dte[:, 0:2], dte[:, 0:2], ACT.Ln, bias=1.0), "s_dtl")
                act.wait_ge(*done("v_gz", l))
                do(A.activation(flat(sc[2][:]), flat(sc[1][:]), ACT.Abs))
                do(A.activation(flat(sc[2][:]), flat(sc[2][:]), ACT.Exp, scale=-1.0))
                inc(A.activation(flat(sc[2][:]), flat(sc[2][:]), ACT.Ln, bias=1.0), "s_ge")
                for n, (src, dst) in enumerate(((6, tmq[:, :, 2, :]), (4, None), (7, None), (3, tmq[:, :, 1, :]),
                                                (2, tmq[:, :, 0, :]))):
                    act.wait_ge(*done("t_turned", l, n + 1))
                    if n == 1:
                        ins = A.activation(bonus[:].rearrange("p j h -> p (j h)"), bank[4][:, 0:TT * NH], ACT.Copy)
                    elif n == 2:
                        for j in range(TT):
                            ins = A.activation(a_w1[:, j, :, 0, :], bank[7][:, j * RW:j * RW + RW]
                                               .rearrange("p (h n) -> p h n", n=HD), ACT.Copy)
                    else:
                        ins = A.activation(dst, bank[src][:].rearrange("p (j c) -> p j c", j=TT), ACT.Copy)
                    inc(ins, "s_turned")
                for i, (name, dst) in enumerate((("s_qk", gla_q), ("s_qk", gla_k))):
                    act.wait_ge(*done("t_proj", l, 9 + i))
                    inc(A.activation(dst[:], bank[i][:].rearrange("p (b s) -> p b s", b=2), ACT.Copy), name)
                act.wait_ge(*done("t_mv", l))
                for j in range(TT):
                    inc(A.activation(a_w1[:, j, :, 1, :], bank[4][:, j * RW:j * RW + RW].rearrange("p (h n) -> p h n", n=HD),
                                     ACT.Copy), "s_mv")

                def lp(lev):
                    for j in range(TT):
                        act.wait_ge(*done("t_lp", l, lev * TT + j + 1))
                        inc(A.activation(lvl[:, j], bank[2 + j][:].rearrange("p (h s) -> p h s", h=NH), ACT.Copy), "s_lp")

                def vg(i):
                    act.wait_ge(*done("t_proj", l, 11 + i))
                    A.activation(gla_vg[:, i, 0:GW], bank[i % 2][:, 0:GW], ACT.Copy)
                    inc(A.activation(gla_vg[:, i, GW:], bank[i % 2][:, GW:], ACT.Silu), "s_vg")

                def zz(i):
                    act.wait_ge(*done("t_proj", l, 13 + i))
                    inc(A.activation(z_tm[:, i], bank[5 * i][:], ACT.Silu), "s_z")

                lp(0)
                act.wait_ge(*done("v_gcum", l))
                A.activation(anchor_g[:, :, 2, :], anchor_g[:, :, 2, :], ACT.Exp, scale=1.0 / 16)
                do(A.activation(sc[2][:], sc[3][:], ACT.Exp, scale=1.0 / 16))
                inc(A.activation(sc[3][:], sc[3][:], ACT.Exp, scale=-1.0 / 16), "s_expl")
                for i in range(3):
                    act.wait_ge(*done("v_proj", l, 5 + i))
                    inc(A.activation(xbc[:, 2 * i:2 * i + 2], xbc[:, 2 * i:2 * i + 2], ACT.Silu), "s_silx")
                vg(0)
                lp(1)
                vg(1)
                for lev in range(2, 5):
                    lp(lev)
                for j in range(TT):
                    act.wait_ge(*done("t_xa", l, j + 1))
                    inc(A.activation(a_w1[:, j].rearrange("p h a n -> p (h a n)"), bank[2 + j][:], ACT.Copy), "s_xa")
                zz(0)
                A.preload_act_table_set("natural_log_exp_and_others")

                def rstd(out_, in_, n, eps, name):
                    do(A.activation(out_, in_, ACT.Ln, scale=1.0 / n, bias=eps[:]))
                    inc(A.activation(out_, out_, ACT.Exp, scale=-0.5), name)

                for j in range(TT):
                    act.wait_ge(*done("t_ssd_tm", l, j + 1))
                    inc(A.activation(heads[:, j, GW:GW + SW], bank[j][:], ACT.Copy), "s_xs")
                act.wait_ge(*done("t_edge", l))
                inc(A.activation(b_tm[:], bank[2][:, 0:P], ACT.Copy), "s_xs")
                act.wait_ge(*done("t_edge", l))
                inc(A.activation(dte[:, 2:4].rearrange("p a b -> p (a b)"), bank[2][:, 2 * P:2 * P + 2 * SH], ACT.Exp), "s_edge")
                act.wait_ge(*done("v_gnvar", l))
                rstd(gn[:, 1], gn[:, 1], HD, eps_gn, "s_gnr")
                act.wait_ge(*done("t_q", l))
                for q in range(4):
                    act.wait_ge(*done("t_seg", l, q + 1))
                    inc(A.activation(seg_w4(q), bank[(4, 6, 7, 4)[q]][:].rearrange("p (h s) -> p h s", h=4), ACT.Exp), "s_seg")
                zz(1)
                A.preload_act_table_set("natural_log_exp_and_others")
                act.wait_ge(*done("t_gkt", l))
                inc(A.activation(gla_kt[:], bank[3][:].rearrange("p (j c) -> p j c", j=TT), ACT.Copy), "s_gln")
                def cat_cm(n, i):
                    act.wait_ge(*done("t_cat", l, n))
                    for b in range(2):
                        inc(A.activation(x_cm[:, 2 * i + b, :], bank[i][:, b * S:b * S + S], ACT.Copy,
                                         scale=cat_gain(l, 2 * i + b)), "s_cat")

                for j in range(TT):
                    act.wait_ge(*done("v_yssd", l, j + 1))
                    for g in range(2):
                        ins = A.activation(k_cm[:, 0, :], heads[:, j, GW + g * 256:GW + g * 256 + 256], ACT.Square,
                                           accum_out=rms_s[:, j, g:g + 1])
                        do(ins)
                    rstd(rms_s[:, j], rms_s[:, j], SW // 2, eps_ln, "s_rssd")
                cat_cm(1, 3)
                cat_cm(2, 1)
                cat_cm(3, 2)
                act.wait_ge(*done("v_glasum", l))
                rstd(rms[:], rms[:], HD, eps_ln, "s_rgla")
                cat_cm(4, 0)

                def ln_rstd(which, j):
                    act.wait_ge(*done("v_var", l, 2 * which + j + 1))
                    rstd(bn2[:, j, 1:2], bn2[:, j, 1:2], 1, eps_ln, "s_rstd")

                def high_part(j):
                    act.wait_ge(*done("v_x1", l, j + 1))
                    inc(A.activation(x_hi[:, j], x_tm[:, j], ACT.Copy), "s_xhi")

                def x1_cm(j, i):
                    act.wait_ge(*done("t_x1", l, 4 * j + i + 1))
                    inc(A.activation(x_cm[:, 2 * i:2 * i + 2, tile_(j)], bank[i][:].rearrange("p (k s) -> p k s", k=2)
                                     [:, :, tile_(j)], ACT.Copy), "s_x1")

                ln_rstd(0, 0)
                high_part(0)
                for i in range(4):
                    x1_cm(0, i)
                ln_rstd(0, 1)
                high_part(1)
                for i in range(4):
                    x1_cm(1, i)
                act.wait_ge(*done("v_logit", l))
                inc(A.activation(rt[:, 1], rt[:, 0], ACT.Exp, scale=-1.0), "s_route")
                two_ways(act, l, lambda rounds: experts_s(act, l, rounds))
                A.preload_act_table_set("natural_log_exp_and_others")
                for j in range(TT):
                    ln_rstd(1, j)

        for name, signal in SIG.items():
            assert signal.given == L * signal.per * (2 if name in STEPS or name in ("t_down", "v_wlo", "v_dlo") else 1), name


_INS = ["x", "w_in", "gla_w_alpha", "gla_b_alpha", "gla_norm_g", "ssd_conv_w", "ssd_conv_b", "ssd_dt_bias", "ssd_A_log",
        "ssd_D", "ssd_norm_g", "rwkv_mu", "rwkv_w0", "rwkv_w2", "rwkv_a0", "rwkv_a2", "rwkv_g2", "rwkv_k_k", "rwkv_k_a",
        "rwkv_r_k", "rwkv_ln_g", "rwkv_ln_b", "w_out", "ln1_g", "ln1_b", "router_w", "router_b", "exp_w_gate",
        "exp_w_up", "exp_w_down", "ln2_g", "ln2_b"]


def kernel(**inputs):
    import numpy as _np
    import concourse.bacc as _bacc
    from concourse import mybir as _mybir
    from concourse.bass_utils import run_bass_kernel_spmd as _run

    nc = _bacc.Bacc("TRN2", target_bir_lowering=False, num_devices=1)
    arrays, aps = {}, {}
    for name in _INS:
        a = _np.ascontiguousarray(inputs[name])
        arrays[f"in_{name}"] = a
        aps[name] = nc.dram_tensor(f"in_{name}", a.shape, _mybir.dt.from_np(a.dtype), kind="ExternalInput").ap()
    shape = inputs["x"].shape
    out = nc.dram_tensor("out_x", shape, _mybir.dt.float32, kind="ExternalOutput").ap()
    hybrid_trunk(nc, aps, out)
    r = _run(nc, [arrays], core_ids=[0])
    return r.results[0]["out_x"]
```
